# Optimizing a Trainium2 kernel written in Bass

```python
import jax
import jax.numpy as jnp
from jax import lax
import numpy as np

D_MODEL = 1024
BATCH = 1
SEQ = 256
DEPTH = 2

GRID_W = 64
CTX_LEN = 256
D_MIX = D_MODEL
CONF_W = D_MIX // 4
SCONV_W = D_MIX // 4
LRU_W = D_MIX // 2
MIX_HEAD_DIM = 64
MIX_HEADS = D_MIX // MIX_HEAD_DIM
CONF_K = 31
SCONV_K = 3
LRU_CONV_K = 4
CONF_PAD = ((CONF_K - 1) // 2, (CONF_K - 1) // 2)
SCONV_PAD = ((SCONV_K - 1) // 2, (SCONV_K - 1) // 2)
LRU_PAD = (LRU_CONV_K // 2, LRU_CONV_K - 1 - LRU_CONV_K // 2)
LRU_HEAD_DIM = 64
LRU_HEADS = LRU_W // LRU_HEAD_DIM
LRU_C = 8.0
D_FF = ((8 * D_MODEL // 3 + 127) // 128) * 128
N_EXPERTS = 8
TOP_K = 2
N_DENSE = (DEPTH + 1) // 2
N_MOE = DEPTH // 2
EPS = 1e-6
SPLITS = (CONF_W, 2 * CONF_W, 2 * CONF_W + SCONV_W, 2 * CONF_W + 2 * SCONV_W,
          2 * CONF_W + 3 * SCONV_W, 2 * CONF_W + 3 * SCONV_W + LRU_W)
W_IN_COLS = 2 * CONF_W + 3 * SCONV_W + 2 * LRU_W
C_X_START = SPLITS[4]
C_X_END = SPLITS[5]

kernel_name = 'hybrid_conformer_shortconv_rglru_moe_dit'

def rms_norm(x, g):
    xf = x.astype(jnp.float32)
    y = xf * lax.rsqrt(jnp.mean(xf * xf, axis=-1, keepdims=True) + EPS)
    return (y * g.astype(jnp.float32)).astype(x.dtype)

def layer_norm(x, g, b):
    xf = x.astype(jnp.float32)
    mu = jnp.mean(xf, axis=-1, keepdims=True)
    var = jnp.mean(jnp.square(xf - mu), axis=-1, keepdims=True)
    y = (xf - mu) * lax.rsqrt(var + EPS)
    return (y * g.astype(jnp.float32) + b.astype(jnp.float32)).astype(x.dtype)

def head_rms_norm(y, g):
    bsz, t, _ = y.shape
    yh = y.reshape(bsz, t, MIX_HEADS, MIX_HEAD_DIM).astype(jnp.float32)
    yh = yh * lax.rsqrt(jnp.mean(yh * yh, axis=-1, keepdims=True) + EPS)
    return (yh.reshape(bsz, t, D_MIX) * g.astype(jnp.float32)).astype(y.dtype)

def modulate(x, shift, scale):
    return x * (1.0 + scale) + shift

def dwconv(x, w, pad, b=None):
    y = lax.conv_general_dilated(x, w[:, None, :].astype(x.dtype), window_strides=(1,), padding=[pad],
                                 dimension_numbers=('NWC', 'WIO', 'NWC'), feature_group_count=x.shape[-1])
    return y if b is None else y + b.astype(y.dtype)

def conv_rows(x, w, pad, b=None):
    bsz, t, ch = x.shape
    rows = t // GRID_W
    y = dwconv(x.reshape(bsz * rows, GRID_W, ch), w, pad, b)
    return y.reshape(bsz, t, ch)

def conv_cols(x, w, pad, b=None):
    bsz, t, ch = x.shape
    rows = t // GRID_W
    xc = x.reshape(bsz, rows, GRID_W, ch).transpose(0, 2, 1, 3).reshape(bsz * GRID_W, rows, ch)
    y = dwconv(xc, w, pad, b)
    return y.reshape(bsz, GRID_W, rows, ch).transpose(0, 2, 1, 3).reshape(bsz, t, ch)

def linear_scan(a, b, h0, reverse):
    if reverse:
        b = b.at[:, -1].add(a[:, -1] * h0)
    else:
        b = b.at[:, 0].add(a[:, 0] * h0)

    def combine(e1, e2):
        a1, b1 = e1
        a2, b2 = e2
        return a1 * a2, a2 * b1 + b2

    _, h = lax.associative_scan(combine, (a, b), axis=1, reverse=reverse)
    return h

def rglru_direction(xc, w_a, b_a, w_x, b_x, lam, h0, reverse):
    bsz, t, _ = xc.shape
    xh = xc.reshape(bsz, t, LRU_HEADS, LRU_HEAD_DIM)
    r = jax.nn.sigmoid(jnp.einsum('blhi,hij->blhj', xh, w_a.astype(jnp.float32)).reshape(bsz, t, LRU_W)
                       + b_a.astype(jnp.float32))
    i = jax.nn.sigmoid(jnp.einsum('blhi,hij->blhj', xh, w_x.astype(jnp.float32)).reshape(bsz, t, LRU_W)
                       + b_x.astype(jnp.float32))
    log_a = LRU_C * r * jax.nn.log_sigmoid(lam.astype(jnp.float32))
    a = jnp.exp(log_a)
    mult = jnp.sqrt(jnp.maximum(-jnp.expm1(2.0 * log_a), 0.0))
    return linear_scan(a, mult * (i * xc), h0, reverse)

def rglru_bidir(c_x, p, h0f, h0b):
    xc = dwconv(c_x, p['lru_conv_w'], LRU_PAD, p['lru_conv_b']).astype(jnp.float32)
    hf = rglru_direction(xc, p['lru_wa'][0], p['lru_ba'][0], p['lru_wx'][0], p['lru_bx'][0],
                         p['lru_lam'][0], h0f, False)
    hb = rglru_direction(xc, p['lru_wa'][1], p['lru_ba'][1], p['lru_wx'][1], p['lru_bx'][1],
                         p['lru_lam'][1], h0b, True)
    return hf, hb

def token_mixer(h, p, grid, h0f, h0b):
    proj = h @ p['w_in']
    a_val, a_gate, s_bg, s_cg, s_x, c_x, c_g = jnp.split(proj, list(SPLITS), axis=-1)
    conv_a = conv_rows if grid else dwconv
    conv_b = conv_cols if grid else dwconv
    u = conv_a(a_val * jax.nn.sigmoid(a_gate), p['conf_w'], CONF_PAD, p['conf_b'])
    ya = jax.nn.silu(layer_norm(u, p['conf_ln_g'], p['conf_ln_b']))
    yb = s_bg * conv_b(s_cg * s_x, p['sconv_w'], SCONV_PAD)
    hf, hb = rglru_bidir(c_x, p, h0f, h0b)
    yc = (hf + hb).astype(h.dtype) * jax.nn.gelu(c_g)
    y = head_rms_norm(jnp.concatenate([ya, yb, yc], axis=-1), p['g_mix'])
    return y @ p['w_out'], hf[:, -1], hb[:, 0]

def swiglu(h, w1, w3, w2):
    return (jax.nn.silu(h @ w1) * (h @ w3)) @ w2

def moe_swiglu(h, w_r, b_r, w1, w3, w2):
    logits = (h @ w_r).astype(jnp.float32) + b_r.astype(jnp.float32)
    top_v, top_i = lax.top_k(logits, TOP_K)
    probs = jax.nn.softmax(top_v, axis=-1)
    combine = jnp.einsum('blk,blke->ble', probs, jax.nn.one_hot(top_i, N_EXPERTS, dtype=jnp.float32))
    out = jnp.zeros_like(h)
    for e in range(N_EXPERTS):
        out = out + combine[..., e, None].astype(h.dtype) * swiglu(h, w1[e], w3[e], w2[e])
    return out

def setup_inputs(seed: int = 0) -> dict:
    key = jax.random.key(seed)
    ks = iter(jax.random.split(key, 40))

    def nrm(shape, scale):
        return scale * jax.random.normal(next(ks), shape, jnp.float32)

    def gain(shape):
        return 1.0 + 0.1 * jax.random.normal(next(ks), shape, jnp.float32)

    d = D_MODEL
    x = nrm((BATCH, SEQ, d), 1.0)
    c = nrm((BATCH, d), 1.0)
    ctx = nrm((BATCH, CTX_LEN, d), 1.0)
    c_ctx = nrm((d,), 1.0)
    w_mod = nrm((DEPTH, d, 6 * d), 0.5 * d ** -0.5)
    b_mod = nrm((DEPTH, 6 * d), 0.1)
    g_norm1 = gain((DEPTH, d))
    g_norm2 = gain((DEPTH, d))
    w_in = nrm((DEPTH, d, W_IN_COLS), d ** -0.5)
    conf_w = nrm((DEPTH, CONF_K, CONF_W), CONF_K ** -0.5)
    conf_b = nrm((DEPTH, CONF_W), 0.02)
    conf_ln_g = gain((DEPTH, CONF_W))
    conf_ln_b = nrm((DEPTH, CONF_W), 0.02)
    sconv_w = nrm((DEPTH, SCONV_K, SCONV_W), SCONV_K ** -0.5)
    lru_conv_w = nrm((DEPTH, LRU_CONV_K, LRU_W), LRU_CONV_K ** -0.5)
    lru_conv_b = nrm((DEPTH, LRU_W), 0.02)
    lru_wa = nrm((DEPTH, 2, LRU_HEADS, LRU_HEAD_DIM, LRU_HEAD_DIM), LRU_HEAD_DIM ** -0.5)
    lru_ba = nrm((DEPTH, 2, LRU_W), 0.1)
    lru_wx = nrm((DEPTH, 2, LRU_HEADS, LRU_HEAD_DIM, LRU_HEAD_DIM), LRU_HEAD_DIM ** -0.5)
    lru_bx = nrm((DEPTH, 2, LRU_W), 0.1)
    u = jax.random.uniform(next(ks), (DEPTH, 2, LRU_W), jnp.float32, 0.9, 0.999)
    a_base = u ** (1.0 / LRU_C)
    lru_lam = jnp.log(a_base) - jnp.log1p(-a_base)
    g_mix = gain((DEPTH, D_MIX))
    w_out = nrm((DEPTH, D_MIX, d), D_MIX ** -0.5)
    ffn_w1 = nrm((N_DENSE, d, D_FF), d ** -0.5)
    ffn_w3 = nrm((N_DENSE, d, D_FF), d ** -0.5)
    ffn_w2 = nrm((N_DENSE, D_FF, d), D_FF ** -0.5)
    router_w = nrm((N_MOE, d, N_EXPERTS), d ** -0.5)
    router_b = nrm((N_MOE, N_EXPERTS), 0.01)
    moe_w1 = nrm((N_MOE, N_EXPERTS, d, D_FF), d ** -0.5)
    moe_w3 = nrm((N_MOE, N_EXPERTS, d, D_FF), d ** -0.5)
    moe_w2 = nrm((N_MOE, N_EXPERTS, D_FF, d), D_FF ** -0.5)
    g_final = gain((d,))
    return {'x': x, 'c': c, 'ctx': ctx, 'c_ctx': c_ctx, 'w_mod': w_mod, 'b_mod': b_mod,
            'g_norm1': g_norm1, 'g_norm2': g_norm2, 'w_in': w_in, 'conf_w': conf_w, 'conf_b': conf_b,
            'conf_ln_g': conf_ln_g, 'conf_ln_b': conf_ln_b, 'sconv_w': sconv_w,
            'lru_conv_w': lru_conv_w, 'lru_conv_b': lru_conv_b, 'lru_wa': lru_wa, 'lru_ba': lru_ba,
            'lru_wx': lru_wx, 'lru_bx': lru_bx, 'lru_lam': lru_lam, 'g_mix': g_mix, 'w_out': w_out,
            'ffn_w1': ffn_w1, 'ffn_w3': ffn_w3, 'ffn_w2': ffn_w2, 'router_w': router_w,
            'router_b': router_b, 'moe_w1': moe_w1, 'moe_w3': moe_w3, 'moe_w2': moe_w2,
            'g_final': g_final}

def reference(x, c, ctx, c_ctx, w_mod, b_mod, g_norm1, g_norm2, w_in, conf_w, conf_b, conf_ln_g,
              conf_ln_b, sconv_w, lru_conv_w, lru_conv_b, lru_wa, lru_ba, lru_wx, lru_bx, lru_lam,
              g_mix, w_out, ffn_w1, ffn_w3, ffn_w2, router_w, router_b, moe_w1, moe_w3, moe_w2,
              g_final):
    bsz = x.shape[0]
    zero_state = jnp.zeros((bsz, LRU_W), jnp.float32)
    silu_c = jax.nn.silu(c)
    silu_cc = jax.nn.silu(c_ctx)
    for l in range(DEPTH):
        last = l == DEPTH - 1
        p = {'w_in': w_in[l], 'conf_w': conf_w[l], 'conf_b': conf_b[l], 'conf_ln_g': conf_ln_g[l],
             'conf_ln_b': conf_ln_b[l], 'sconv_w': sconv_w[l], 'lru_conv_w': lru_conv_w[l],
             'lru_conv_b': lru_conv_b[l], 'lru_wa': lru_wa[l], 'lru_ba': lru_ba[l], 'lru_wx': lru_wx[l],
             'lru_bx': lru_bx[l], 'lru_lam': lru_lam[l], 'g_mix': g_mix[l], 'w_out': w_out[l]}

        def channel_mixer(h):
            j = l // 2
            if l % 2 == 0:
                return swiglu(h, ffn_w1[j], ffn_w3[j], ffn_w2[j])
            return moe_swiglu(h, router_w[j], router_b[j], moe_w1[j], moe_w3[j], moe_w2[j])

        mod_x = (silu_c @ w_mod[l] + b_mod[l])[:, None, :]
        sh1, sc1, gt1, sh2, sc2, gt2 = jnp.split(mod_x, 6, axis=-1)
        mod_c = (silu_cc @ w_mod[l] + b_mod[l])[None, None, :]
        csh1, csc1, cgt1, csh2, csc2, cgt2 = jnp.split(mod_c, 6, axis=-1)

        hc = modulate(rms_norm(ctx, g_norm1[l]), csh1, csc1)
        if last:
            hf_c, hb_c = rglru_bidir(hc @ w_in[l][:, C_X_START:C_X_END], p, zero_state, zero_state)
            state_f, state_b = hf_c[:, -1], hb_c[:, 0]
        else:
            out_c, state_f, state_b = token_mixer(hc, p, False, zero_state, zero_state)
            ctx = ctx + cgt1 * out_c
            ctx = ctx + cgt2 * channel_mixer(modulate(rms_norm(ctx, g_norm2[l]), csh2, csc2))

        hx = modulate(rms_norm(x, g_norm1[l]), sh1, sc1)
        out_x, _, _ = token_mixer(hx, p, True, state_f, state_b)
        x = x + gt1 * out_x
        x = x + gt2 * channel_mixer(modulate(rms_norm(x, g_norm2[l]), sh2, sc2))
    return rms_norm(x, g_final)


_drawn_inputs = setup_inputs


def setup_inputs(seed=0):
    import zlib

    import numpy as np

    out = dict(_drawn_inputs(seed))
    spreads = {}
    factors = {'conf_b': 4.668, 'conf_ln_b': 6.595, 'lru_ba': 7.518, 'lru_bx': 4.502, 'router_b': 4.827}
    for name, (base, spread) in spreads.items():
        noise = np.random.default_rng([zlib.crc32(name.encode()), seed]).standard_normal(out[name].shape)
        drawn = base * np.exp(spread * noise) if base else spread * noise
        out[name] = jnp.asarray(drawn.astype(out[name].dtype))
    for name, factor in factors.items():
        out[name] = (out[name] * factor).astype(out[name].dtype)
    return out
```

```python
import concourse.bass as bass
from concourse import mybir
from contextlib import ExitStack

F32 = mybir.dt.float32
F32R = mybir.dt.float32r
I32 = mybir.dt.int32
U32 = mybir.dt.uint32
ALU = mybir.AluOpType
ACT = mybir.ActivationFunctionType
AXX = mybir.AxisListType.X

P = 128
D = 1024
KD = D // P
NC = 256
NX = 256
T = NC + NX
GRID = 64
ROWS = NX // GRID
DFF = 2816
KF = DFF // P
KG = KF // 2
NE = 8
CAP = 128
EPS = 1e-6
CONF_K, SCONV_K, LRU_K = 31, 3, 4
CONF_PAD = CONF_K // 2
CW = 2048
RAW = 5
SPL = 3
WIN_ORDER = [0, 1, 4, 3, 2, 5, 6, 7, 8]
NWIN, NWOUT = 9, 4
UP, DOWN = 2 * KF // 2, KF // 2
PER_EXPERT = UP + DOWN

COL = {}


def table(parts):
    row, out = 0, []
    for name, rows in parts:
        COL[name] = row
        out.append((name, row, rows))
        row += rows
    return out, row


TABLES = []
for _n, _parts in enumerate([
    [("c", 8), ("c_ctx", 8), ("g_norm1", 16), ("g_norm2", 16), ("g_final", 8), ("g_mix", 16),
     ("sconv_w", 12), ("lru_conv_w", 32)],
    [("conf_b", 4), ("conf_ln_g", 4), ("conf_ln_b", 4), ("lru_conv_b", 8), ("lru_ba", 16), ("lru_bx", 16),
     ("lru_lam", 16)],
    [("conf_w", 124)],
    [("b_mod", 96)],
]):
    _t, _rows = table(_parts)
    for _name, _row, _k in _t:
        COL[_name] = 128 * _n + _row
    TABLES.append((_t, _rows))


class Count:

    def __init__(self, marks):
        self.n, self.marks = 0, marks

    def __call__(self, *name):
        self.n += 1
        if name:
            assert name not in self.marks
            self.marks[name] = self.n
        return 1


def schedule():
    chunks = [("x", 0), ("x", 1)] + [("mod", 0, j) for j in range(8)]
    for l in range(2):
        chunks += [("w_in", l, c) for c in WIN_ORDER]
        chunks += [("w_out", l, c) for c in range(SPL)]
        if l == 0:
            chunks += [("mod", 0, j) for j in range(8, 24)]
        chunks += [("w_out", l, c) for c in range(SPL, NWOUT)]
        if l == 0:
            mod = iter(range(24))
            for g in range(2):
                for i in range(KG):
                    chunks.append(("up", g, i))
                    chunks += [("mod", 1, j) for j in [next(mod, None)] if j is not None]
                for d in range(KD):
                    chunks.append(("down", g, d))
                    chunks += [("mod", 1, j) for j in [next(mod, None)] if j is not None]
    return chunks


CHUNKS = schedule()
SPLIT = [c for c in CHUNKS if c[0] in ("w_in", "w_out", "up", "down")]
POS = {c: n for n, c in enumerate(CHUNKS)}
ORD = {c: n for n, c in enumerate(SPLIT)}


def width(c):
    return KG * P if c[0] == "down" else CW


def program(nc, a, out, known, marks):
    def at(*name):
        return known[name] if known else 1

    ctx = ExitStack()
    with ctx:
        def sem(name):
            return ctx.enter_context(nc.semaphore(name))

        cursor = [-(-nc.sbuf_base // 64) * 64]

        def sb(name, shape, dt=F32):
            size = 4
            for s in shape[1:]:
                size *= s
            t = nc.alloc_sbuf_tensor_at(name, shape, dt, offset=cursor[0])
            cursor[0] += -(-size // 32) * 32
            return t

        ident = sb("ident", [P, P])
        ones_d = sb("ones_d", [P, P])
        ones_c = sb("ones_c", [P, P])
        ones_h = sb("ones_h", [P, P])
        eps = sb("eps", [P, 1])
        PT = sb("PT", [P, 4 * P])
        cc = sb("cc", [P, KD, 2])
        modT = sb("modT", [P, 2, 48, 2])
        amp = sb("amp", [P, 2, 2, KD, 2])
        clp = sb("clp", [P, 16])
        cln = sb("cln", [P, 16])
        lt = sb("lt", [P, 4, 16])
        xT = sb("xT", [P, KD, T])
        raw = sb("raw", [P, RAW, CW])
        w_hi = sb("w_hi", [P, SPL, CW], F32R)
        w_lo = sb("w_lo", [P, SPL, CW], F32R)
        G = sb("G", [P, 16, P])
        tb = sb("tb", [P, 2, T])
        sq = sb("sq", [P, 2, T])
        rs = sb("rs", [P, T])
        area = cursor[0]

        h_hi = sb("h_hi", [P, KD, T], F32R)
        h_lo = sb("h_lo", [P, KD, T], F32R)
        rest = cursor[0]
        cxp = sb("cxp", [P, 4, 2, 260])
        xc = sb("xc", [P, 4, T])
        vp = sb("vp", [P, 2, NC + 2 * CONF_PAD + ROWS * (GRID + 2 * CONF_PAD)])
        sx = sb("sx", [P, 2, T])
        sp_ = sb("sp_", [P, 2, NC + 2 + NX + 2 * GRID])
        y = sb("y", [P, KD, T])
        assert cursor[0] <= nc.sbuf_usable_end, cursor[0]
        cursor[0] = area
        lr = sb("lr", [P, 4, T])
        li = sb("li", [P, 4, T])
        la = sb("la", [P, 4, T])
        lm = sb("lm", [P, 4, T])
        cursor[0] = rest
        rows_sb = sb("rows_sb", [P, 4, P])
        cursor[0] = rest
        f_hi = sb("f_hi", [P, KG, T], F32R)
        f_lo = sb("f_lo", [P, KG, T], F32R)
        cursor[0] = area
        hT = sb("hT", [P, KD, NX])
        ht_hi = sb("ht_hi", [P, 2, D], F32R)
        ht_lo = sb("ht_lo", [P, 2, D], F32R)
        sel = sb("sel", [P, 2, CAP], F32R)
        selT = sb("selT", [P, NX], F32R)
        hc_hi = sb("hc_hi", [P, KD, CAP], F32R)
        hc_lo = sb("hc_lo", [P, KD, CAP], F32R)
        gs = sb("gs", [P, 2, 256])
        hid = sb("hid", [P, DFF])
        hd_hi = sb("hd_hi", [P, KF, CAP], F32R)
        hd_lo = sb("hd_lo", [P, KF, CAP], F32R)
        y_hi = sb("y_hi", [P, D], F32R)
        y_lo = sb("y_lo", [P, D], F32R)
        rw = sb("rw", [P, KD, NE])
        rb = sb("rb", [1, NE])
        one = sb("one", [1, P])
        before = sb("before", [P, P])
        all1 = sb("all1", [P, P])
        iota_s = sb("iota_s", [P, CAP])
        iota_e = sb("iota_e", [P, NE])
        lg = sb("lg", [P, 2, NE])
        top = sb("top", [P, 2, 8])
        topi = sb("topi", [P, 2, 8], U32)
        topf = sb("topf", [P, 2, 8])
        pr = sb("pr", [P, 2, 4])
        oh = sb("oh", [P, 2, 2, NE])
        mask = sb("mask", [P, 2, NE])
        comb = sb("comb", [P, 2, NE])
        pos = sb("pos", [P, 2, NE])
        pos1 = sb("pos1", [P, 2, 1])
        cw1 = sb("cw1", [P, 2, 1])
        slot_w = sb("slot_w", [P, 1])
        most = sb("most", [P, 1])
        most_i = sb("most_i", [P, 1], I32)
        assert cursor[0] <= nc.sbuf_usable_end, cursor[0]
        cursor[0] = area
        fq = sb("fq", [P, KD, NX])
        fy = sb("fy", [P, KD, NX])
        fo = sb("fo", [P, 2, D])

        bank = [ctx.enter_context(nc.psum_tensor(f"bank{i}", [P, 512], F32)) for i in range(8)]
        MOD, STAT = bank[6], bank[7]

        pe_done, act_done, dve_done, pool_done = sem("pe_done"), sem("act_done"), sem("dve_done"), sem("pool_done")
        table_in, gate_in, rout_in, stored = sem("table_in"), sem("gate_in"), sem("rout_in"), sem("stored")
        raw_in = [sem(f"raw_in{s}") for s in range(RAW)]
        exp_in = [sem(f"exp_in{s}") for s in range(RAW)]
        ovf_in = [sem(f"ovf_in{s}") for s in range(RAW)]
        fin_dve, fin_act, fin_pe = sem("fin_dve"), sem("fin_act"), sem("fin_pe")

        arrived, level = {}, [0] * RAW
        for n, c in enumerate(CHUNKS):
            level[n % RAW] += 32 if c[0] == "up" else 16
            arrived[c] = level[n % RAW]
        e_arrived, e_level = [], [0] * RAW
        for j in range(PER_EXPERT):
            e_level[j % RAW] += 32 if j < UP else 16
            e_arrived.append(e_level[j % RAW])

        def free_name(c):
            if c[0] == "x":
                return ("xt", KD - 1)
            return ("lo", ORD[c]) if c in ORD else ("used",) + c

        def free_sem(c):
            return dve_done if c in ORD else pe_done

        lo = [0, NC]
        streams = [(0, 1), (1,)]

        def tok(s):
            return slice(s * NC, (s + 1) * NC)

        def colv(name, i, n=1):
            return PT[:, COL[name] + i:COL[name] + i + n]

        def vp_x(t, k):
            v = vp[:, t, NC + 2 * CONF_PAD:].rearrange("p (r w) -> p r w", r=ROWS)
            return v[:, :, k:k + GRID]

        def padded_v(t, s, k):
            return vp[:, t, k:k + NC] if s == 0 else vp_x(t, k)

        def padded_s(t, s, k):
            o = k if s == 0 else NC + 2 + GRID * k
            return sp_[:, t, o:o + 256]

        def grid(ap, s):
            return ap if s == 0 else ap.rearrange("p (r w) -> p r w", r=ROWS)

        def weights(c):
            l = c[1]
            if c[0] == "mod":
                return a["w_mod"][l].rearrange("(k p) c -> p k c", p=P)[:, :, 256 * c[2]:256 * c[2] + 256]
            if c[0] == "w_in":
                return a["w_in"][l].rearrange("(k p) c -> p k c", p=P)[:, :, 256 * c[2]:256 * c[2] + 256]
            if c[0] == "w_out":
                return a["w_out"][l].rearrange("(k p) c -> p k c", p=P)[:, :, 256 * c[2]:256 * c[2] + 256]
            if c[0] == "down":
                w = a["ffn_w2"][0].rearrange("(k p) c -> p k c", p=P)
                return w[:, KG * l:KG * l + KG, P * c[2]:P * c[2] + P]
            return (a["ctx"] if l == 0 else a["x"])[0].rearrange("(t p) c -> p t c", p=P)

        pe_n, act_n, dve_n, pool_n = (Count(marks) for _ in range(4))
        fpe_n, fact_n, fdve_n = (Count(marks) for _ in range(3))
        HEAD = (7, 4)
        LOGIT, RANK = 256, 288

        def evacuated(c):
            if c[0] == "w_in" and c[2] != 3:
                return act_done, at("evac", ORD[c])
            if c[0] == "w_in":
                return dve_done, at("evac", ORD[c])
            if c[0] == "w_out":
                return dve_done, at("xT", "w_out", c[1], 2 * c[2] + 1)
            if c[0] == "up":
                return dve_done, at("hid", c[1], c[2])
            return dve_done, at("xT", "down", c[1], c[2])

        def y_low(i8, l, ts, dve, V):
            dve.wait_ge(act_done, at("y_hi", l, i8))
            V.scalar_tensor_tensor(h_lo[:, i8, ts], y[:, i8, ts], colv("g_mix", 8 * l + i8),
                                   h_hi[:, i8, ts].bitcast(F32), ALU.mult, ALU.subtract)\
                .then_inc(dve_done, dve_n("y_lo", l, i8))

        block = ctx.enter_context(nc.Block())

        @block.sync
        def _(sp):
            def load(c):
                n = POS[c]
                slot = raw[:, n % RAW, :]
                if n >= RAW:
                    sp.wait_ge(free_sem(CHUNKS[n - RAW]), at(*free_name(CHUNKS[n - RAW])))
                if c[0] == "up":
                    dst = slot.rearrange("p (k w c) -> p k w c", k=KD, w=2)
                    f = P * (KG * c[1] + c[2])
                    for w, name in enumerate(("ffn_w1", "ffn_w3")):
                        src = a[name][0].rearrange("(k p) c -> p k c", p=P)[:, :, f:f + P]
                        sp.dma_start(dst[:, :, w, :], src).then_inc(raw_in[n % RAW], 16)
                else:
                    k = {"x": 2, "down": KG}.get(c[0], KD)
                    dst = slot[:, 0:width(c)].rearrange("p (k c) -> p k c", k=k)
                    sp.dma_start(dst, weights(c)).then_inc(raw_in[n % RAW], 16)

            def gate_weights(l):
                for w, name in enumerate(("lru_wa", "lru_wx")):
                    for d in range(2):
                        src = a[name][l, d].rearrange("(t u) i j -> u i t j", u=2)
                        for u in range(2):
                            half = slice(64 * u, 64 * u + 64)
                            sp.dma_start(G[half, 8 * d + 4 * w:8 * d + 4 * w + 4, half], src[u])\
                              .then_inc(gate_in, 16)

            for n, (parts, _) in enumerate(TABLES):
                for name, row, rows in parts:
                    src = a[name]
                    dims = " ".join(f"a{i}" for i in range(len(src.shape)))
                    flat = src.rearrange(f"{dims} -> ({dims})") if len(src.shape) > 1 else src
                    sp.dma_start(rows_sb[row:row + rows, n, :], flat.rearrange("(r c) -> r c", c=P))\
                      .then_inc(table_in, 16)
            for c in CHUNKS[:10]:
                load(c)
            sp.wait_ge(pool_done, at("G_zero"))
            gate_weights(0)
            for c in CHUNKS[10:]:
                if c == ("up", 0, 0):
                    sp.wait_ge(pe_done, at("gate", 0, 7))
                    gate_weights(1)
                load(c)

            def expert_chunk(e, j, arrived_sem):
                slot = raw[:, j % RAW, :]
                if j < UP:
                    fc, half = j // 2, j % 2
                    dst = slot.rearrange("p (k w c) -> p k w c", k=4, w=2)
                    for w, name in enumerate(("moe_w1", "moe_w3")):
                        src = a[name][0].rearrange("e (k p) c -> (e k) p c", p=P)
                        src = src[bass.ds(e * KD + 4 * half, 4), :, 256 * fc:256 * fc + 256]
                        sp.dma_start(dst[:, :, w, :], src.rearrange("k p c -> p k c"))\
                          .then_inc(arrived_sem[j % RAW], 16)
                else:
                    src = a["moe_w2"][0].rearrange("e (k p) c -> (e k) p c", p=P)
                    src = src[bass.ds(e * KF + 2 * (j - UP), 2), :, :]
                    sp.dma_start(slot.rearrange("p (k c) -> p k c", k=2), src.rearrange("k p c -> p k c"))\
                      .then_inc(arrived_sem[j % RAW], 16)

            def experts(tag, arrived_sem):
                K = at("per_expert", tag, "dve")
                last = {j % RAW: j for j in range(PER_EXPERT)}
                for j in range(RAW):
                    expert_chunk(0, j, arrived_sem)

                def rest_of(e, shift):
                    for j in range(RAW, PER_EXPERT):
                        sp.wait_ge(dve_done, at("e_lo", tag, j - RAW) + shift)
                        expert_chunk(e, j, arrived_sem)
                with sp.Fori(0, NE - 1, 1) as e:
                    shift = e * K
                    rest_of(e, shift)
                    for j in range(RAW):
                        sp.wait_ge(dve_done, at("e_lo", tag, last[j]) + shift)
                        expert_chunk(e + 1, j, arrived_sem)
                rest_of(NE - 1, (NE - 1) * K)

            for c in CHUNKS[-RAW:]:
                sp.wait_ge(free_sem(c), at(*free_name(c)))
            sp.wait_ge(pe_done, at("mm", ORD[("w_out", 1, NWOUT - 1)]))
            sp.dma_start(rw[:, :, :], a["router_w"][0].rearrange("(k p) e -> p k e", p=P)).then_inc(rout_in, 16)
            sp.dma_start(rb[:, :], a["router_b"]).then_inc(rout_in, 16)
            experts("main", exp_in)
            sp.wait_ge(dve_done, at("most"))
            overflow = sp.value_load(most_i[0:1, 0:1], min_val=0, max_val=NX)
            with sp.If(overflow > CAP):
                sp.wait_ge(dve_done, at("experts_end", "main"))
                experts("more", ovf_in)
            sp.wait_ge(fin_dve, at("fin_out"))
            sp.dma_start(out[0].rearrange("(t p) c -> p t c", p=P), fo[:, :, :]).then_inc(stored, 16)
            sp.wait_ge(stored, 16)

        @block.gpsimd
        def _(pool):
            def own():
                if pool_n.n:
                    pool.wait_ge(pool_done, pool_n.n)

            for m, v in ((ident, 0.0), (ones_h, 0.0), (ones_d, 1.0 / D), (ones_c, 1.0 / 256), (eps, EPS)):
                own()
                nc.gpsimd.memset(m[:, :], v).then_inc(pool_done, pool_n())
            own()
            nc.gpsimd.affine_select(out=ident[:, :], in_=ident[:, :], compare_op=ALU.not_equal, fill=1.0, base=0,
                                    pattern=[[-1, P]], channel_multiplier=1).then_inc(pool_done, pool_n("ident"))
            for h in range(2):
                half = slice(64 * h, 64 * h + 64)
                own()
                nc.gpsimd.memset(ones_h[half, half], 1.0 / 64).then_inc(pool_done, pool_n())
            own()
            nc.gpsimd.memset(G[:, :, :], 0.0).then_inc(pool_done, pool_n("G_zero"))
            for l in range(2):
                pool.wait_ge(pe_done, at("tables") if l == 0 else at("mm", ORD[("down", 1, KD - 1)]))
                own()
                nc.gpsimd.memset(vp[:, :, :], 0.0).then_inc(pool_done, pool_n())
                own()
                nc.gpsimd.memset(sp_[:, :, :], 0.0).then_inc(pool_done, pool_n())
                own()
                nc.gpsimd.memset(cxp[:, :, :, :], 0.0).then_inc(pool_done, pool_n("padded", l))

            pool.wait_ge(pe_done, at("mm", ORD[("w_out", 1, NWOUT - 1)]))
            own()
            nc.gpsimd.memset(one[:, :], 1.0).then_inc(pool_done, pool_n())
            own()
            nc.gpsimd.memset(all1[:, :], 1.0).then_inc(pool_done, pool_n())
            own()
            nc.gpsimd.memset(before[:, :], 1.0).then_inc(pool_done, pool_n())
            own()
            nc.gpsimd.iota(iota_s[:, :], pattern=[[1, CAP]], base=0, channel_multiplier=0,
                           allow_small_or_imprecise_dtypes=True).then_inc(pool_done, pool_n())
            own()
            nc.gpsimd.iota(iota_e[:, :], pattern=[[1, NE]], base=0, channel_multiplier=0,
                           allow_small_or_imprecise_dtypes=True).then_inc(pool_done, pool_n())
            own()
            nc.gpsimd.affine_select(out=before[:, :], in_=before[:, :], compare_op=ALU.is_gt, fill=0.0, base=0,
                                    pattern=[[1, P]], channel_multiplier=-1).then_inc(pool_done, pool_n("routing"))

        @block.tensor
        def _(pe):
            def mm(dst, lhsT, rhs, first, last):
                return nc.tensor.matmul(dst, lhsT, rhs, start=first, stop=last)

            def split_mm(dst, w, x, first, last):
                mm(dst, w[0], x[0], first, False)
                mm(dst, w[0], x[1], False, False)
                return mm(dst, w[1], x[0], False, last)

            pe.wait_ge(table_in, 16 * sum(len(parts) for parts, _ in TABLES))
            pe.wait_ge(pool_done, at("ident"))
            for n, (_, rows) in enumerate(TABLES):
                i = nc.tensor.transpose(STAT[:, P * n:P * n + rows], rows_sb[0:rows, n, :], ident[0:rows, 0:rows])
            i.then_inc(pe_done, pe_n("tables"))
            for s in range(2):
                pe.wait_ge(raw_in[s], 16)
            for d in range(KD):
                if d >= 6:
                    pe.wait_ge(dve_done, at("xT", "in", d - 6))
                for s in range(2):
                    for t in range(2):
                        i = nc.tensor.transpose(bank[d % 6][:, P * (2 * s + t):P * (2 * s + t) + P],
                                                raw[:, s, D * t + P * d:D * t + P * d + P], ident[:, :])
                i.then_inc(pe_done, pe_n("xt", d))

            def modulation(l, j):
                c = ("mod", l, j)
                slot = POS[c] % RAW
                if j == 0 and l == 0:
                    pe.wait_ge(act_done, at("cc"))
                pe.wait_ge(raw_in[slot], arrived[c])
                for t in range(2):
                    o = 96 * l + 2 * (2 * j + t)
                    for k in range(KD):
                        i = mm(MOD[:, o:o + 2], raw[:, slot, 256 * k + P * t:256 * k + P * t + P], cc[:, k, :],
                               k == 0, k == KD - 1)
                i.then_inc(pe_done, pe_n("used", *c))

            def mean_square(l, w, ts, previous):
                previous()
                for d in range(KD):
                    pe.wait_ge(act_done, at("sq", l, w, d))
                    mm(STAT[:, ts], ones_d[:, :], sq[:, d % 2, ts], d == 0, d == KD - 1)\
                        .then_inc(pe_done, pe_n("ms", l, w, d))

            def take(c):
                s = ORD[c]
                pe.wait_ge(dve_done, at("lo", s))
                if s >= 3:
                    pe.wait_ge(*evacuated(SPLIT[s - 3]))
                return (w_hi[:, s % SPL, :], w_lo[:, s % SPL, :]), bank[2 * (s % 3):2 * (s % 3) + 2]

            def project(c, ts, ready):
                w, banks = take(c)
                for k in range(KD):
                    if ready:
                        pe.wait_ge(dve_done, at(*ready, k))
                    for t in range(2):
                        o = 256 * k + P * t
                        i = split_mm(banks[t][:, ts], (w[0][:, o:o + P], w[1][:, o:o + P]),
                                     (h_hi[:, k, ts], h_lo[:, k, ts]), k == 0, k == KD - 1)
                i.then_inc(pe_done, pe_n("mm", ORD[c]))

            for j in range(8):
                modulation(0, j)
            for l in range(2):
                ts = slice(lo[l], T)
                mean_square(l, 1, slice(0, T), lambda: pe.wait_ge(dve_done, at("PT")) if l == 0 else
                            pe.wait_ge(act_done, at("sd", 0, 2)))
                for n, c in enumerate(WIN_ORDER):
                    project(("w_in", l, c), slice(0, T) if c in (5, 6) else ts, ("h_lo", l, 1) if n == 0 else None)
                pe.wait_ge(dve_done, at("conf_u", l))
                for t in range(2):
                    i = mm(STAT[:, ts], ones_c[:, :], y[:, t, ts], t == 0, t == 1)
                i.then_inc(pe_done, pe_n("conf_mean", l))
                pe.wait_ge(gate_in, 8 * 16 * (l + 1))
                for q in range(8):
                    d, t = q // 4, q % 4
                    if q < 4:
                        pe.wait_ge(dve_done, at("xc", l, t))
                    if q < 3:
                        pe.wait_ge(*evacuated(("w_in", l, WIN_ORDER[6 + q])))
                    else:
                        pe.wait_ge(act_done, at("gate_read", l, q - 3))
                    for w in range(2):
                        i = mm(bank[2 * (q % 3) + w][:, :], G[:, 8 * d + 4 * w + t, :], xc[:, t, :], True, True)
                    i.then_inc(pe_done, pe_n("gate", l, q))
                if l == 0:
                    for j in range(8, 24):
                        modulation(0, j)
                for t in range(2):
                    pe.wait_ge(act_done, at("conf_sq", l, t))
                    i = mm(STAT[:, ts], ones_c[:, :], sq[:, t, ts], t == 0, t == 1)
                i.then_inc(pe_done, pe_n("conf_var", l))
                pe.wait_ge(act_done, at("gate_read", l, 7))
                for i8 in range(KD):
                    pe.wait_ge(act_done, at("head_sq", l, i8))
                    if i8 >= 2:
                        pe.wait_ge(act_done, at("head_sd", l, i8 - 2))
                    mm(bank[HEAD[i8 % 2]][:, ts], ones_h[:, :], sq[:, i8 % 2, ts], True, True)\
                        .then_inc(pe_done, pe_n("head_ms", l, i8))
                for c in range(NWOUT):
                    project(("w_out", l, c), ts, ("y_lo", l) if c == 0 else None)
                mean_square(l, 2, ts, lambda: None)
                if l == 1:
                    break
                mod = iter(range(24))
                for g in range(2):
                    for i11 in range(KG):
                        c = ("up", g, i11)
                        w, banks = take(c)
                        for k in range(KD):
                            if g == 0 and i11 == 0:
                                pe.wait_ge(dve_done, at("h_lo", 0, 2, k))
                            for v in range(2):
                                o = 256 * k + P * v
                                i = split_mm(banks[v][:, :], (w[0][:, o:o + P], w[1][:, o:o + P]),
                                             (h_hi[:, k, :], h_lo[:, k, :]), k == 0, k == KD - 1)
                        i.then_inc(pe_done, pe_n("mm", ORD[c]))
                        for j in [next(mod, None)]:
                            if j is not None:
                                modulation(1, j)
                    for d in range(KD):
                        c = ("down", g, d)
                        w, banks = take(c)
                        for k in range(KG):
                            if d == 0:
                                pe.wait_ge(dve_done, at("f_lo", g, k))
                            i = split_mm(banks[0][:, :], (w[0][:, P * k:P * k + P], w[1][:, P * k:P * k + P]),
                                         (f_hi[:, k, :], f_lo[:, k, :]), k == 0, k == KG - 1)
                        i.then_inc(pe_done, pe_n("mm", ORD[c]))
                        for j in [next(mod, None)]:
                            if j is not None:
                                modulation(1, j)

            pe.wait_ge(rout_in, 32)
            pe.wait_ge(pool_done, at("routing"))
            for t in range(2):
                for k in range(KD):
                    pe.wait_ge(act_done, at("h", k))
                    mm(MOD[:, LOGIT + NE * t:LOGIT + NE * t + NE], hT[:, k, P * t:P * t + P], rw[:, k, :], k == 0, False)
                i = mm(MOD[:, LOGIT + NE * t:LOGIT + NE * t + NE], one[:, :], rb[:, :], False, True)
            i.then_inc(pe_done, pe_n("logits"))
            pe.wait_ge(*evacuated(("w_out", 1, NWOUT - 1)))
            for t in range(2):
                for k in range(KD):
                    i = nc.tensor.transpose(bank[2 * t + k // 4][:, P * (k % 4):P * (k % 4) + P],
                                            hT[:, k, P * t:P * t + P], ident[:, :])
                i.then_inc(pe_done, pe_n("ht", t))
            pe.wait_ge(dve_done, at("mask"))
            mm(MOD[:, RANK:RANK + NE], before[:, :], mask[:, 0, :], True, True)
            mm(MOD[:, RANK + NE:RANK + 2 * NE], all1[:, :], mask[:, 0, :], True, False)
            mm(MOD[:, RANK + NE:RANK + 2 * NE], before[:, :], mask[:, 1, :], False, True)
            for t in range(2):
                i = mm(MOD[:, RANK + 2 * NE:RANK + 3 * NE], all1[:, :], mask[:, t, :], t == 0, t == 1)
            i.then_inc(pe_done, pe_n("rank"))

            def experts(tag):
                n0 = pe_n.n
                Kd, Ka = at("per_expert", tag, "dve"), at("per_expert", tag, "act")
                with pe.Fori(0, NE, 1) as e:
                    de, ae = e * Kd, e * Ka
                    pe.wait_ge(dve_done, at("e_sel", tag) + de)
                    for part, (src, b) in enumerate(((ht_hi, 6), (ht_lo, 4))):
                        for k in range(KD):
                            for t in range(2):
                                i = mm(bank[b + k // 4][:, P * (k % 4):P * (k % 4) + P],
                                       src[:, t, P * k:P * k + P], sel[:, t, :], t == 0, t == 1)
                        i.then_inc(pe_done, pe_n("e_gather", tag, part))
                    for t in range(2):
                        mm(bank[3][:, 256:257], sel[:, t, :].bitcast(F32), cw1[:, t, :], t == 0, t == 1)
                    for t in range(2):
                        i = nc.tensor.transpose(bank[2][:, P * t:P * t + P], sel[:, t, :].bitcast(F32), ident[:, :])
                    i.then_inc(pe_done, pe_n("e_turned", tag))

                    def turn(fc):
                        pe.wait_ge(dve_done, at("e_hid", tag, fc) + de)
                        if fc >= 2:
                            pe.wait_ge(dve_done, at("e_hd", tag, fc - 2) + de)
                        else:
                            pe.wait_ge(act_done, at("e_selT", tag) + ae)
                            pe.wait_ge(dve_done, at("e_slot_w", tag) + de)
                        for t in range(2):
                            o = 256 * fc + P * t
                            j = nc.tensor.transpose(bank[2 + fc % 2][:, P * t:P * t + P], hid[:, o:o + P], ident[:, :])
                        j.then_inc(pe_done, pe_n("e_turn", tag, fc))

                    pe.wait_ge(act_done, at("e_hc", tag) + ae)
                    pe.wait_ge(dve_done, at("e_hc", tag, "lo") + de)
                    for j in range(UP):
                        fc, s = j // 2, j % SPL
                        pe.wait_ge(dve_done, at("e_lo", tag, j) + de)
                        if j % 2 == 0 and fc >= 2:
                            pe.wait_ge(dve_done, at("e_hid", tag, fc - 2) + de)
                        for kk in range(4):
                            k, cols = 4 * (j % 2) + kk, slice(512 * kk, 512 * kk + 512)
                            i = split_mm(bank[fc % 2][:, :], (hc_hi[:, k, :], hc_lo[:, k, :]),
                                         (w_hi[:, s, cols], w_lo[:, s, cols]), k == 0, k == KD - 1)
                        i.then_inc(pe_done, pe_n("e_mm", tag, j))
                        if j % 2 and fc >= 1:
                            turn(fc - 1)
                    for j in range(UP, PER_EXPERT):
                        s = j % SPL
                        pe.wait_ge(dve_done, at("e_lo", tag, j) + de)
                        pe.wait_ge(dve_done, at("e_hd", tag, j - UP) + de)
                        for kk in range(2):
                            k = 2 * (j - UP) + kk
                            for half in range(2):
                                cols = slice(D * kk + 512 * half, D * kk + 512 * half + 512)
                                i = split_mm(bank[4 + half][:, :], (hd_hi[:, k, :], hd_lo[:, k, :]),
                                             (w_hi[:, s, cols], w_lo[:, s, cols]), k == 0, k == KF - 1)
                        i.then_inc(pe_done, pe_n("e_mm", tag, j))
                        if j == UP:
                            turn(DOWN - 1)
                    pe.wait_ge(dve_done, at("e_y", tag) + de)
                    for d in range(KD):
                        dst = bank[6 + d // 2 % 2][:, 256 * (d % 2):256 * (d % 2) + 256]
                        if d % 2 == 0 and d >= 4:
                            pe.wait_ge(dve_done, at("e_add", tag, d - 3) + de)
                        mm(dst, y_hi[:, P * d:P * d + P], selT[:, :], True, False)
                        mm(dst, y_lo[:, P * d:P * d + P], selT[:, :], False, True)\
                            .then_inc(pe_done, pe_n("e_back", tag, d))
                marks[("per_expert", tag, "pe")] = pe_n.n - n0
                pe_n.n = n0 + NE * (pe_n.n - n0)

            experts("main")
            pe.wait_ge(dve_done, at("most"))
            overflow = pe.value_load(most_i[0:1, 0:1], min_val=0, max_val=NX)
            with pe.If(overflow > CAP):
                experts("more")
            for d in range(KD):
                pe.wait_ge(fin_dve, at("fin_sq", d))
                i = mm(STAT[:, 0:NX], ones_d[:, :], fq[:, d, :], d == 0, d == KD - 1)
            i.then_inc(fin_pe, fpe_n("fin_ms"))
            for t in range(2):
                for d in range(KD):
                    pe.wait_ge(fin_dve, at("fin_y", d))
                    i = nc.tensor.transpose(bank[2 * t + d // 4][:, P * (d % 4):P * (d % 4) + P],
                                            fy[:, d, P * t:P * t + P], ident[:, :])
                i.then_inc(fin_pe, fpe_n("fin_turn", t))

        @block.scalar
        def _(act):
            def hi(s):
                if s >= len(SPLIT):
                    return
                c = SPLIT[s]
                n = width(c)
                act.wait_ge(raw_in[POS[c] % RAW], arrived[c])
                if s >= SPL:
                    act.wait_ge(pe_done, at("mm", s - SPL))
                nc.scalar.activation(w_hi[:, s % SPL, 0:n], raw[:, POS[c] % RAW, 0:n], ACT.Copy)\
                    .then_inc(act_done, act_n("hi", s))

            def squares(l, w, ts, ready):
                for d in range(KD):
                    act.wait_ge(dve_done, at("xT", *ready, d))
                    if d >= 2:
                        act.wait_ge(pe_done, at("ms", l, w, d - 2))
                    nc.scalar.activation(sq[:, d % 2, ts], xT[:, d, ts], ACT.Square)\
                        .then_inc(act_done, act_n("sq", l, w, d))
                act.wait_ge(pe_done, at("ms", l, w, KD - 1))
                nc.scalar.activation(rs[:, ts], STAT[:, ts], ACT.Sqrt, bias=eps[:, :])\
                    .then_inc(act_done, act_n("sd", l, w))

            def h_high(l, w, which, dst, name):
                for d in range(KD):
                    act.wait_ge(dve_done, at("t", l, w, d))
                    for s in which:
                        shift = modT[:, l, 8 * (0 if w == 1 else 3) + d, s:s + 1]
                        ap = dst[:, d, tok(s)] if name == "h_hi" else dst[:, d, :]
                        i = nc.scalar.activation(ap, tb[:, d % 2, tok(s)], ACT.Identity, bias=shift)
                        if s != which[-1]:
                            i.then_inc(act_done, act_n())
                    i.then_inc(act_done, act_n(*((name, l, w, d) if name == "h_hi" else (name, d))))

            act.wait_ge(dve_done, at("PT"))
            for s, name in enumerate(("c_ctx", "c")):
                i = nc.scalar.activation(cc[:, :, s], colv(name, 0, KD), ACT.Silu)
                i.then_inc(act_done, act_n(*(("cc",) if s else ())))
            act.wait_ge(dve_done, at("lam_abs"))
            nc.scalar.activation(lt[:, 0, :], lt[:, 0, :], ACT.Exp, scale=-1.0).then_inc(act_done, act_n("lam_exp"))

            for l in range(2):
                ts = slice(lo[l], T)
                squares(l, 1, slice(0, T), ("in",) if l == 0 else ("down", 1))
                h_high(l, 1, (0, 1), h_hi, "h_hi")
                if l == 0:
                    for s in range(SPL):
                        hi(s)
                for n, c in enumerate(WIN_ORDER):
                    s = ORD[("w_in", l, c)]
                    b = bank[2 * (s % 3):2 * (s % 3) + 2]
                    act.wait_ge(pe_done, at("mm", s))
                    hi(s + SPL)
                    for t in range(2):
                        last = ("evac", s) if t else ()
                        if c == 0:
                            i = nc.scalar.activation(tb[:, t, ts], b[t][:, ts], ACT.Copy)
                        elif c == 1:
                            i = nc.scalar.activation(sq[:, t, ts], b[t][:, ts], ACT.Tanh, scale=0.5)
                        elif c == 4:
                            i = nc.scalar.activation(sx[:, t, ts], b[t][:, ts], ACT.Copy)
                        elif c == 2:
                            i = nc.scalar.activation(y[:, 2 + t, ts], b[t][:, ts], ACT.Copy)
                        elif c in (5, 6):
                            if c == 5 and t == 0:
                                act.wait_ge(pool_done, at("padded", l))
                            i = nc.scalar.activation(cxp[:, 2 * (c - 5) + t, :, 2:2 + 256],
                                                     b[t][:, :].rearrange("p (s w) -> p s w", s=2), ACT.Copy)
                        elif c in (7, 8):
                            act.wait_ge(dve_done, at("xc", l, 3))
                            i = nc.scalar.activation(
                                cxp[:, 2 * (c - 7) + t, lo[l] // NC:2, 2:2 + 256],
                                b[t][:, ts].rearrange("p (s w) -> p s w", w=256), ACT.Gelu_apprx_tanh)
                        else:
                            continue
                        i.then_inc(act_done, act_n(*last))
                def gates(d, t):
                    q = 4 * d + t
                    act.wait_ge(pe_done, at("gate", l, q))
                    if d == 1:
                        act.wait_ge(dve_done, at("scan", l, 0, t))
                    else:
                        act.wait_ge(pe_done, at("mm", ORD[("w_in", l, WIN_ORDER[-1])]))
                    b = bank[2 * (q % 3):2 * (q % 3) + 2]
                    nc.scalar.activation(lr[:, t, :], b[0][:, :], ACT.Tanh, scale=0.5,
                                         bias=colv("lru_ba", 8 * l + q)).then_inc(act_done, act_n())
                    nc.scalar.activation(li[:, t, :], b[1][:, :], ACT.Tanh, scale=0.5,
                                         bias=colv("lru_bx", 8 * l + q)).then_inc(act_done, act_n("gate_read", l, q))
                    act.wait_ge(act_done, act_n.n - 1)
                    k = 8 * l + q
                    nc.scalar.activation(la[:, t, :], lr[:, t, :], ACT.Exp, scale=cln[:, k:k + 1],
                                         bias=cln[:, k:k + 1]).then_inc(act_done, act_n())
                    nc.scalar.activation(lr[:, t, :], lr[:, t, :], ACT.Tanh, scale=clp[:, k:k + 1],
                                         bias=clp[:, k:k + 1]).then_inc(act_done, act_n())
                    act.wait_ge(act_done, act_n.n - 1)
                    nc.scalar.activation(lm[:, t, :], la[:, t, :], ACT.Square).then_inc(act_done, act_n("a2", l, q))

                act.wait_ge(dve_done, at("clp"))
                for d in range(2):
                    for t in range(4):
                        gates(d, t)
                    for t in range(4):
                        act.wait_ge(dve_done, at("m", l, 4 * d + t))
                        nc.scalar.activation(lm[:, t, :], lm[:, t, :], ACT.Sqrt, scale=0.25)\
                            .then_inc(act_done, act_n("mult", l, 4 * d + t))
                for t in range(2):
                    act.wait_ge(dve_done, at("conf_c", l, t))
                    nc.scalar.activation(sq[:, t, ts], y[:, t, ts], ACT.Square)\
                        .then_inc(act_done, act_n("conf_sq", l, t))
                act.wait_ge(pe_done, at("conf_var", l))
                nc.scalar.activation(rs[:, ts], STAT[:, ts], ACT.Sqrt, bias=eps[:, :])\
                    .then_inc(act_done, act_n("conf_sd", l))
                for t in range(2):
                    act.wait_ge(dve_done, at("conf_n", l, t))
                    nc.scalar.activation(y[:, t, ts], y[:, t, ts], ACT.Silu, scale=colv("conf_ln_g", 2 * l + t),
                                         bias=colv("conf_ln_b", 2 * l + t)).then_inc(act_done, act_n("conf_y", l, t))

                def head_out(i8):
                    act.wait_ge(dve_done, at("y_n", l, i8))
                    nc.scalar.activation(h_hi[:, i8, ts], y[:, i8, ts], ACT.Copy, scale=colv("g_mix", 8 * l + i8))\
                        .then_inc(act_done, act_n("y_hi", l, i8))

                act.wait_ge(dve_done, at("y", l))
                act.wait_ge(act_done, act_n.n)
                for i8 in range(KD):
                    if i8 >= 2:
                        act.wait_ge(pe_done, at("head_ms", l, i8 - 2))
                    nc.scalar.activation(sq[:, i8 % 2, ts], y[:, i8, ts], ACT.Square)\
                        .then_inc(act_done, act_n("head_sq", l, i8))
                    if i8 >= 2:
                        head_out(i8 - 2)
                    act.wait_ge(pe_done, at("head_ms", l, i8))
                    nc.scalar.activation(tb[:, i8 % 2, ts], bank[HEAD[i8 % 2]][:, ts], ACT.Sqrt, bias=eps[:, :])\
                        .then_inc(act_done, act_n("head_sd", l, i8))
                head_out(KD - 2)
                head_out(KD - 1)
                for c in range(NWOUT):
                    s = ORD[("w_out", l, c)]
                    act.wait_ge(pe_done, at("mm", s))
                    hi(s + SPL)
                squares(l, 2, ts, ("w_out", l))
                if l == 1:
                    break
                h_high(l, 2, (0, 1), h_hi, "h_hi")
                for g in range(2):
                    for i11 in range(KG):
                        s = ORD[("up", g, i11)]
                        act.wait_ge(pe_done, at("mm", s))
                        hi(s + SPL)
                        if i11 >= 2:
                            act.wait_ge(dve_done, at("hid", g, i11 - 2))
                        nc.scalar.activation(tb[:, i11 % 2, :], bank[2 * (s % 3)][:, :], ACT.Silu)\
                            .then_inc(act_done, act_n("silu", g, i11))
                        act.wait_ge(dve_done, at("hid", g, i11))
                        nc.scalar.activation(f_hi[:, i11, :], sq[:, i11 % 2, :], ACT.Copy)\
                            .then_inc(act_done, act_n("f_hi", g, i11))
                    for d in range(KD):
                        s = ORD[("down", g, d)]
                        act.wait_ge(pe_done, at("mm", s))
                        hi(s + SPL)

            h_high(1, 2, (1,), hT, "h")
            for t in range(2):
                act.wait_ge(pe_done, at("ht", t))
                for half in range(2):
                    nc.scalar.activation(ht_hi[:, t, 512 * half:512 * half + 512], bank[2 * t + half][:, :], ACT.Copy)\
                        .then_inc(act_done, act_n("ht_hi", t, half))
            act.wait_ge(dve_done, at("gap"))
            nc.scalar.activation(pr[:, :, 1], pr[:, :, 0], ACT.Exp).then_inc(act_done, act_n("gap_exp"))

            def experts(tag, arrived_sem):
                n0 = act_n.n
                Kp, Kd = at("per_expert", tag, "pe"), at("per_expert", tag, "dve")
                with act.Fori(0, NE, 1) as e:
                    pp, de, ein = e * Kp, e * Kd, [e * e_level[s] for s in range(RAW)]

                    def e_hi(j):
                        if j >= PER_EXPERT:
                            return
                        act.wait_ge(arrived_sem[j % RAW], e_arrived[j] + ein[j % RAW])
                        if j >= SPL:
                            act.wait_ge(pe_done, at("e_mm", tag, j - SPL) + pp)
                        nc.scalar.activation(w_hi[:, j % SPL, :], raw[:, j % RAW, :], ACT.Copy)\
                            .then_inc(act_done, act_n("e_hi", tag, j))

                    for j in range(SPL):
                        e_hi(j)
                    act.wait_ge(pe_done, at("e_gather", tag, 0) + pp)
                    for half in range(2):
                        i = nc.scalar.activation(hc_hi[:, 4 * half:4 * half + 4, :],
                                                 bank[6 + half][:, :].rearrange("p (k c) -> p k c", c=CAP), ACT.Copy)
                        i.then_inc(act_done, act_n(*(("e_hc", tag) if half else ())))
                    act.wait_ge(pe_done, at("e_turned", tag) + pp)
                    nc.scalar.activation(selT[:, :], bank[2][:, 0:NX], ACT.Copy)\
                        .then_inc(act_done, act_n("e_selT", tag))

                    def hd_high(fc):
                        act.wait_ge(pe_done, at("e_turn", tag, fc) + pp)
                        nc.scalar.activation(hd_hi[:, 2 * fc:2 * fc + 2, :],
                                             bank[2 + fc % 2][:, 0:256].rearrange("p (k c) -> p k c", c=CAP), ACT.Copy)\
                            .then_inc(act_done, act_n("e_hd_hi", tag, fc))

                    for j in range(UP):
                        fc = j // 2
                        act.wait_ge(pe_done, at("e_mm", tag, j) + pp)
                        e_hi(j + SPL)
                        if j % 2:
                            if fc >= 2:
                                act.wait_ge(dve_done, at("e_hid", tag, fc - 2) + de)
                            nc.scalar.activation(gs[:, fc % 2, :], bank[fc % 2][:, 0:256], ACT.Silu)\
                                .then_inc(act_done, act_n("e_silu", tag, fc))
                            if fc >= 1:
                                hd_high(fc - 1)
                    for j in range(UP, PER_EXPERT):
                        act.wait_ge(pe_done, at("e_mm", tag, j) + pp)
                        e_hi(j + SPL)
                        if j == UP:
                            hd_high(DOWN - 1)
                    act.wait_ge(dve_done, at("e_slot_w", tag) + de)
                    for half in range(2):
                        nc.scalar.activation(y_hi[:, 512 * half:512 * half + 512], bank[4 + half][:, :], ACT.Copy,
                                             scale=slot_w[:, :]).then_inc(act_done, act_n("e_y_hi", tag, half))
                marks[("per_expert", tag, "act")] = act_n.n - n0
                act_n.n = n0 + NE * (act_n.n - n0)

            experts("main", exp_in)
            act.wait_ge(dve_done, at("most"))
            overflow = act.value_load(most_i[0:1, 0:1], min_val=0, max_val=NX)
            with act.If(overflow > CAP):
                experts("more", ovf_in)
            act.wait_ge(fin_pe, at("fin_ms"))
            nc.scalar.activation(rs[:, 0:NX], STAT[:, 0:NX], ACT.Sqrt, bias=eps[:, :])\
                .then_inc(fin_act, fact_n("fin_sd"))
            for t in range(2):
                act.wait_ge(fin_pe, at("fin_turn", t))
                nc.scalar.activation(fo[:, t, 0:512], bank[2 * t][:, :], ACT.Copy)\
                    .then_inc(fin_act, fact_n("fin_o", t))

        @block.vector
        def _(dve):
            V = nc.vector

            def own(back=0):
                dve.wait_ge(dve_done, dve_n.n - back)

            def low(s):
                if s >= len(SPLIT):
                    return
                n = width(SPLIT[s])
                dve.wait_ge(act_done, at("hi", s))
                V.tensor_tensor(w_lo[:, s % SPL, 0:n], raw[:, POS[SPLIT[s]] % RAW, 0:n],
                                w_hi[:, s % SPL, 0:n].bitcast(F32), ALU.subtract).then_inc(dve_done, dve_n("lo", s))

            def normed(l, w, which, low_part):
                ts = slice(lo[l] if w == 2 else 0, T)
                dve.wait_ge(act_done, at("sd", l, w))
                V.reciprocal(rs[:, ts], rs[:, ts]).then_inc(dve_done, dve_n())

                def t_of(d):
                    if d >= 2:
                        dve.wait_ge(act_done, at("h_hi", l, w, d - 2) if low_part else at("h", d - 2))
                        if low_part:
                            dve.wait_ge(dve_done, at("h_lo", l, w, d - 2))
                    for s in which:
                        i = V.scalar_tensor_tensor(tb[:, d % 2, tok(s)], xT[:, d, tok(s)], amp[:, l, w - 1, d, s:s + 1],
                                                   rs[:, tok(s)], ALU.mult, ALU.mult)
                        i.then_inc(dve_done, dve_n(*(("t", l, w, d) if s == which[-1] else ())))

                def lo_of(d):
                    dve.wait_ge(act_done, at("h_hi", l, w, d))
                    for s in which:
                        shift = modT[:, l, 8 * (0 if w == 1 else 3) + d, s:s + 1]
                        i = V.scalar_tensor_tensor(h_lo[:, d, tok(s)], tb[:, d % 2, tok(s)], shift,
                                                   h_hi[:, d, tok(s)].bitcast(F32), ALU.add, ALU.subtract)
                        i.then_inc(dve_done, dve_n(*(("h_lo", l, w, d) if s == which[-1] else ())))
                own()
                t_of(0)
                for d in range(KD):
                    if d + 1 < KD:
                        t_of(d + 1)
                    if low_part:
                        lo_of(d)

            def modulated(l, j0, j1):
                for s in range(2):
                    V.tensor_tensor(modT[:, l, j0:j1, s], MOD[:, 96 * l + s + 2 * j0:96 * l + 2 * j1:2],
                                    colv("b_mod", 48 * l + j0, j1 - j0), ALU.add).then_inc(dve_done, dve_n())

            def amplitude(l, w):
                j = 8 * (1 if w == 1 else 4)
                own()
                for s in range(2):
                    V.scalar_tensor_tensor(amp[:, l, w - 1, :, s], modT[:, l, j:j + 8, s], 1.0,
                                           colv(f"g_norm{w}", 8 * l, 8), ALU.add, ALU.mult)\
                        .then_inc(dve_done, dve_n())

            dve.wait_ge(pe_done, at("tables"))
            for n, (_, rows) in enumerate(TABLES):
                i = V.tensor_copy(PT[:, P * n:P * n + rows], STAT[:, P * n:P * n + rows])
                i.then_inc(dve_done, dve_n(*(("PT",) if n == 3 else ())))
            own()
            lam = colv("lru_lam", 0, 16)
            V.tensor_scalar(lt[:, 1, :], lam, -1.0, None, ALU.mult).then_inc(dve_done, dve_n())
            own()
            V.tensor_tensor(lt[:, 0, :], lam, lt[:, 1, :], ALU.max).then_inc(dve_done, dve_n("lam_abs"))
            for name, n in (("conf_w", 124), ("lru_ba", 16), ("lru_bx", 16)):
                V.tensor_scalar(colv(name, 0, n), colv(name, 0, n), 0.5, None, ALU.mult).then_inc(dve_done, dve_n())
            for d in range(KD):
                dve.wait_ge(pe_done, at("xt", d))
                V.tensor_copy(xT[:, d, :], bank[d % 6][:, :]).then_inc(dve_done, dve_n("xT", "in", d))
            dve.wait_ge(act_done, at("lam_exp"))
            V.tensor_scalar(lt[:, 2, :], lt[:, 0, :], 2.0, None, ALU.add).then_inc(dve_done, dve_n())
            own()
            V.reciprocal(lt[:, 2, :], lt[:, 2, :]).then_inc(dve_done, dve_n())
            own()
            V.tensor_tensor(lt[:, 0, :], lt[:, 0, :], lt[:, 2, :], ALU.mult).then_inc(dve_done, dve_n())
            own()
            V.tensor_tensor(lt[:, 2, :], lt[:, 0, :], lt[:, 0, :], ALU.mult).then_inc(dve_done, dve_n())
            own()
            V.tensor_scalar(lt[:, 3, :], lt[:, 2, :], 1.0 / 15, 1.0 / 13, ALU.mult, ALU.add).then_inc(dve_done, dve_n())
            for k in (11, 9, 7, 5, 3, 1):
                own()
                V.tensor_tensor(lt[:, 3, :], lt[:, 3, :], lt[:, 2, :], ALU.mult).then_inc(dve_done, dve_n())
                own()
                V.tensor_scalar(lt[:, 3, :], lt[:, 3, :], 1.0 / k, None, ALU.add).then_inc(dve_done, dve_n())
            own()
            V.scalar_tensor_tensor(lt[:, 3, :], lt[:, 3, :], 2.0, lt[:, 0, :], ALU.mult, ALU.mult)\
                .then_inc(dve_done, dve_n())
            own()
            V.scalar_tensor_tensor(lt[:, 3, :], lt[:, 1, :], 0.0, lt[:, 3, :], ALU.max, ALU.add)\
                .then_inc(dve_done, dve_n())
            own()
            V.tensor_scalar(clp[:, :], lt[:, 3, :], 4.0, None, ALU.mult).then_inc(dve_done, dve_n())
            V.tensor_scalar(cln[:, :], lt[:, 3, :], -4.0, None, ALU.mult).then_inc(dve_done, dve_n("clp"))
            dve.wait_ge(pe_done, at("used", "mod", 0, 7))
            modulated(0, 0, 16)
            amplitude(0, 1)

            for l in range(2):
                ts = slice(lo[l], T)
                st = streams[l]
                if l == 1:
                    modulated(1, 0, 48)
                    amplitude(1, 1)
                    amplitude(1, 2)
                normed(l, 1, (0, 1), True)
                if l == 0:
                    for s in range(SPL):
                        low(s)

                def conf_taps(k0, k1):
                    for k in range(k0, k1):
                        for t in range(2):
                            w = colv("conf_w", 62 * l + 2 * k + t)
                            for s in st:
                                out_v, in_v = grid(y[:, t, tok(s)], s), padded_v(t, s, k)
                                own(2 * len(st) - 1)
                                if k == 0:
                                    i = V.tensor_scalar(out_v, in_v, w, colv("conf_b", 2 * l + t), ALU.mult, ALU.add)
                                else:
                                    i = V.scalar_tensor_tensor(out_v, in_v, w, out_v, ALU.mult, ALU.add)
                                i.then_inc(dve_done, dve_n(*(("conf_u", l) if (k, t, s) == (CONF_K - 1, 1, 1) else ())))

                for n, c in enumerate(WIN_ORDER):
                    s0 = ORD[("w_in", l, c)]
                    b = bank[2 * (s0 % 3):2 * (s0 % 3) + 2]
                    dve.wait_ge(pe_done, at("mm", s0))
                    low(s0 + SPL)
                    if c == 1:
                        dve.wait_ge(pool_done, at("padded", l))
                        dve.wait_ge(act_done, at("evac", s0))
                        for t in range(2):
                            for s in st:
                                V.scalar_tensor_tensor(padded_v(t, s, CONF_PAD) if s else vp[:, t, CONF_PAD:CONF_PAD + NC],
                                                       grid(sq[:, t, tok(s)], s), 1.0, grid(tb[:, t, tok(s)], s),
                                                       ALU.add, ALU.mult).then_inc(dve_done, dve_n())
                        own()
                        conf_taps(0, 8)
                    elif c == 4:
                        conf_taps(8, 16)
                    elif c == 3:
                        dve.wait_ge(act_done, at("evac", ORD[("w_in", l, 4)]))
                        for t in range(2):
                            for s in st:
                                V.tensor_tensor(padded_s(t, s, 1), b[t][:, tok(s)], sx[:, t, tok(s)], ALU.mult)\
                                    .then_inc(dve_done, dve_n(*(("evac", s0) if (t, s) == (1, 1) else ())))
                        conf_taps(16, 24)
                    elif c == 2:
                        conf_taps(24, CONF_K)
                    elif c == 5:
                        for k in range(SCONV_K):
                            for t in range(2):
                                w = colv("sconv_w", 6 * l + 2 * k + t)
                                for s in st:
                                    own(2 * len(st) - 1)
                                    if k == 0:
                                        i = V.tensor_scalar(sx[:, t, tok(s)], padded_s(t, s, k), w, None, ALU.mult)
                                    else:
                                        i = V.scalar_tensor_tensor(sx[:, t, tok(s)], padded_s(t, s, k), w,
                                                                   sx[:, t, tok(s)], ALU.mult, ALU.add)
                                    i.then_inc(dve_done, dve_n())
                        own()
                        dve.wait_ge(act_done, at("evac", ORD[("w_in", l, 2)]))
                        V.tensor_tensor(y[:, 2:4, ts], y[:, 2:4, ts], sx[:, :, ts], ALU.mult).then_inc(dve_done, dve_n())
                    elif c == 6:
                        dve.wait_ge(act_done, at("evac", s0))
                        for k in range(LRU_K):
                            for t in range(4):
                                w = colv("lru_conv_w", 16 * l + 4 * k + t)
                                out_v = xc[:, t, :].rearrange("p (s w) -> p s w", s=2)
                                own(3)
                                if k == 0:
                                    i = V.tensor_scalar(out_v, cxp[:, t, :, k:k + 256], w,
                                                        colv("lru_conv_b", 4 * l + t), ALU.mult, ALU.add)
                                else:
                                    i = V.scalar_tensor_tensor(out_v, cxp[:, t, :, k:k + 256], w, out_v,
                                                               ALU.mult, ALU.add)
                                i.then_inc(dve_done, dve_n(*(("xc", l, t) if k == LRU_K - 1 else ())))
                dve.wait_ge(pe_done, at("conf_mean", l))
                for t in range(2):
                    V.tensor_tensor(y[:, t, ts], y[:, t, ts], STAT[:, ts], ALU.subtract)\
                        .then_inc(dve_done, dve_n("conf_c", l, t))
                for d in range(2):
                    for t in range(4):
                        q = 4 * d + t
                        dve.wait_ge(act_done, at("a2", l, q))
                        V.scalar_tensor_tensor(lm[:, t, :], lm[:, t, :], 1.0, lr[:, t, :], ALU.add, ALU.mult)\
                            .then_inc(dve_done, dve_n())
                        V.scalar_tensor_tensor(li[:, t, :], li[:, t, :], 1.0, xc[:, t, :], ALU.add, ALU.mult)\
                            .then_inc(dve_done, dve_n())
                        own(1)
                        V.tensor_scalar(lm[:, t, :], lm[:, t, :], 0.0, None, ALU.max)\
                            .then_inc(dve_done, dve_n("m", l, q))
                    for t in range(4):
                        dve.wait_ge(act_done, at("mult", l, 4 * d + t))
                        V.tensor_tensor(li[:, t, :], lm[:, t, :], li[:, t, :], ALU.mult).then_inc(dve_done, dve_n())
                        own()
                        if d == 0:
                            V.tensor_tensor_scan(y[:, 4 + t, :], la[:, t, :], li[:, t, :], 0.0, ALU.mult, ALU.add)\
                                .then_inc(dve_done, dve_n("scan", l, 0, t))
                            continue
                        for s in range(2):
                            V.tensor_tensor_scan(lr[:, t, tok(s)][:, ::-1], la[:, t, tok(s)][:, ::-1],
                                                 li[:, t, tok(s)][:, ::-1], lr[:, t, 0:1] if s else 0.0,
                                                 ALU.mult, ALU.add).then_inc(dve_done, dve_n())
                            own()
                        V.tensor_tensor(y[:, 4 + t, ts], y[:, 4 + t, ts], lr[:, t, ts], ALU.add)\
                            .then_inc(dve_done, dve_n())
                        own()
                        g_v = cxp[:, t, lo[l] // NC:2, 2:2 + 256]
                        y_v = y[:, 4 + t, ts].rearrange("p (s w) -> p s w", w=256)
                        if t == 0:
                            dve.wait_ge(act_done, at("evac", ORD[("w_in", l, 8)]))
                        V.tensor_tensor(y_v, y_v, g_v, ALU.mult)\
                            .then_inc(dve_done, dve_n(*(("y", l) if t == 3 else ())))
                if l == 0:
                    dve.wait_ge(pe_done, at("used", "mod", 0, 23))
                    modulated(0, 16, 48)
                    amplitude(0, 2)
                dve.wait_ge(act_done, at("conf_sd", l))
                V.reciprocal(rs[:, ts], rs[:, ts]).then_inc(dve_done, dve_n())
                own()
                for t in range(2):
                    V.tensor_tensor(y[:, t, ts], y[:, t, ts], rs[:, ts], ALU.mult)\
                        .then_inc(dve_done, dve_n("conf_n", l, t))
                for i8 in range(KD):
                    dve.wait_ge(act_done, at("head_sd", l, i8))
                    V.reciprocal(tb[:, i8 % 2, ts], tb[:, i8 % 2, ts]).then_inc(dve_done, dve_n())
                    own()
                    V.tensor_tensor(y[:, i8, ts], y[:, i8, ts], tb[:, i8 % 2, ts], ALU.mult)\
                        .then_inc(dve_done, dve_n("y_n", l, i8))
                    if i8 >= 1:
                        y_low(i8 - 1, l, ts, dve, V)
                y_low(KD - 1, l, ts, dve, V)
                for c in range(NWOUT):
                    s0 = ORD[("w_out", l, c)]
                    dve.wait_ge(pe_done, at("mm", s0))
                    low(s0 + SPL)
                    for t in range(2):
                        d = 2 * c + t
                        for s in st:
                            i = V.scalar_tensor_tensor(xT[:, d, tok(s)], bank[2 * (s0 % 3) + t][:, tok(s)],
                                                       modT[:, l, 16 + d, s:s + 1], xT[:, d, tok(s)],
                                                       ALU.mult, ALU.add)
                            i.then_inc(dve_done, dve_n(*(("xT", "w_out", l, d) if s == 1 else ())))
                own()
                if l == 1:
                    break
                normed(0, 2, (0, 1), True)
                for g in range(2):
                    for i11 in range(KG):
                        s0 = ORD[("up", g, i11)]
                        dve.wait_ge(pe_done, at("mm", s0))
                        low(s0 + SPL)
                        dve.wait_ge(act_done, at("silu", g, i11))
                        if i11 >= 2:
                            dve.wait_ge(dve_done, at("f_lo", g, i11 - 2))
                        V.tensor_tensor(sq[:, i11 % 2, :], tb[:, i11 % 2, :], bank[2 * (s0 % 3) + 1][:, :], ALU.mult)\
                            .then_inc(dve_done, dve_n("hid", g, i11))
                        dve.wait_ge(act_done, at("f_hi", g, i11))
                        V.tensor_tensor(f_lo[:, i11, :], sq[:, i11 % 2, :], f_hi[:, i11, :].bitcast(F32),
                                        ALU.subtract).then_inc(dve_done, dve_n("f_lo", g, i11))
                    for d in range(KD):
                        s0 = ORD[("down", g, d)]
                        dve.wait_ge(pe_done, at("mm", s0))
                        low(s0 + SPL)
                        for s in range(2):
                            i = V.scalar_tensor_tensor(xT[:, d, tok(s)], bank[2 * (s0 % 3)][:, tok(s)],
                                                       modT[:, 0, 40 + d, s:s + 1], xT[:, d, tok(s)],
                                                       ALU.mult, ALU.add)
                            i.then_inc(dve_done, dve_n(*(("xT", "down", g, d) if s == 1 else ())))
                own()

            normed(1, 2, (1,), False)
            dve.wait_ge(pe_done, at("logits"))
            V.tensor_copy(lg[:, :, :], MOD[:, LOGIT:LOGIT + 2 * NE].rearrange("p (t e) -> p t e", t=2))\
                .then_inc(dve_done, dve_n())
            own()
            for t in range(2):
                V.max(top[:, t, :], lg[:, t, :]).then_inc(dve_done, dve_n())
            own()
            for t in range(2):
                V.max_index(topi[:, t, :], top[:, t, :], lg[:, t, :]).then_inc(dve_done, dve_n())
            V.tensor_tensor(pr[:, :, 0], top[:, :, 1], top[:, :, 0], ALU.subtract).then_inc(dve_done, dve_n("gap"))
            own(1)
            V.tensor_copy(topf[:, :, :], topi[:, :, :]).then_inc(dve_done, dve_n())
            own()
            for j in range(2):
                for t in range(2):
                    V.tensor_scalar(oh[:, j, t, :], iota_e[:, :], topf[:, t, j:j + 1], None, ALU.is_equal)\
                        .then_inc(dve_done, dve_n())
            own()
            V.tensor_tensor(mask[:, :, :], oh[:, 0, :, :], oh[:, 1, :, :], ALU.add).then_inc(dve_done, dve_n("mask"))
            dve.wait_ge(act_done, at("gap_exp"))
            V.tensor_scalar(pr[:, :, 2], pr[:, :, 1], 1.0, None, ALU.add).then_inc(dve_done, dve_n())
            own()
            V.reciprocal(pr[:, :, 2], pr[:, :, 2]).then_inc(dve_done, dve_n())
            own()
            V.tensor_tensor(pr[:, :, 3], pr[:, :, 1], pr[:, :, 2], ALU.mult).then_inc(dve_done, dve_n())
            own()
            for t in range(2):
                V.tensor_scalar(comb[:, t, :], oh[:, 0, t, :], pr[:, t, 2:3], None, ALU.mult).then_inc(dve_done, dve_n())
            own()
            for t in range(2):
                V.scalar_tensor_tensor(comb[:, t, :], oh[:, 1, t, :], pr[:, t, 3:4], comb[:, t, :],
                                       ALU.mult, ALU.add).then_inc(dve_done, dve_n())
            dve.wait_ge(pe_done, at("rank"))
            V.scalar_tensor_tensor(pos[:, :, :], MOD[:, RANK:RANK + 2 * NE].rearrange("p (t e) -> p t e", t=2), 1.0,
                                   mask[:, :, :], ALU.add, ALU.mult).then_inc(dve_done, dve_n())
            own()
            V.tensor_scalar(pos[:, :, :], pos[:, :, :], -1.0, None, ALU.add).then_inc(dve_done, dve_n())
            V.reduce_max(most[:, :], MOD[:, RANK + 2 * NE:RANK + 3 * NE], AXX).then_inc(dve_done, dve_n())
            own()
            V.tensor_copy(most_i[:, :], most[:, :]).then_inc(dve_done, dve_n("most"))
            for t in range(2):
                for half in range(2):
                    cols = slice(512 * half, 512 * half + 512)
                    dve.wait_ge(act_done, at("ht_hi", t, half))
                    V.tensor_tensor(ht_lo[:, t, cols], bank[2 * t + half][:, :], ht_hi[:, t, cols].bitcast(F32),
                                    ALU.subtract).then_inc(dve_done, dve_n())

            def experts(tag):
                n0 = dve_n.n
                Kp, Ka, Kd = (at("per_expert", tag, x) for x in ("pe", "act", "dve"))
                with dve.Fori(0, NE, 1) as e:
                    pp, ae, de = e * Kp, e * Ka, e * Kd

                    def own_e():
                        dve.wait_ge(dve_done, dve_n.n + de)

                    def e_low(j):
                        if j >= PER_EXPERT:
                            return
                        dve.wait_ge(act_done, at("e_hi", tag, j) + ae)
                        V.tensor_tensor(w_lo[:, j % SPL, :], raw[:, j % RAW, :], w_hi[:, j % SPL, :].bitcast(F32),
                                        ALU.subtract).then_inc(dve_done, dve_n("e_lo", tag, j))

                    own_e()
                    V.tensor_scalar(pos1[:, :, :], pos[:, :, bass.ds(e, 1)], 0.0 if tag == "main" else -float(CAP), None,
                                    ALU.add).then_inc(dve_done, dve_n())
                    V.tensor_copy(cw1[:, :, :], comb[:, :, bass.ds(e, 1)]).then_inc(dve_done, dve_n())
                    own_e()
                    for t in range(2):
                        V.tensor_scalar(sel[:, t, :], iota_s[:, :], pos1[:, t, :], None, ALU.is_equal)\
                            .then_inc(dve_done, dve_n(*(("e_sel", tag) if t else ())))
                    for j in range(SPL):
                        e_low(j)
                    dve.wait_ge(pe_done, at("e_gather", tag, 1) + pp)
                    for half in range(2):
                        V.tensor_copy(hc_lo[:, 4 * half:4 * half + 4, :],
                                      bank[4 + half][:, :].rearrange("p (k c) -> p k c", c=CAP))\
                            .then_inc(dve_done, dve_n(*(("e_hc", tag, "lo") if half else ())))
                    dve.wait_ge(pe_done, at("e_turned", tag) + pp)
                    V.tensor_copy(slot_w[:, :], bank[3][:, 256:257]).then_inc(dve_done, dve_n("e_slot_w", tag))

                    def hd_low(fc):
                        dve.wait_ge(act_done, at("e_hd_hi", tag, fc) + ae)
                        V.tensor_tensor(hd_lo[:, 2 * fc:2 * fc + 2, :],
                                        bank[2 + fc % 2][:, 0:256].rearrange("p (k c) -> p k c", c=CAP),
                                        hd_hi[:, 2 * fc:2 * fc + 2, :].bitcast(F32), ALU.subtract)\
                            .then_inc(dve_done, dve_n("e_hd", tag, fc))

                    for j in range(UP):
                        fc = j // 2
                        dve.wait_ge(pe_done, at("e_mm", tag, j) + pp)
                        e_low(j + SPL)
                        if j % 2:
                            dve.wait_ge(act_done, at("e_silu", tag, fc) + ae)
                            V.tensor_tensor(hid[:, 256 * fc:256 * fc + 256], gs[:, fc % 2, :], bank[fc % 2][:, 256:512],
                                            ALU.mult).then_inc(dve_done, dve_n("e_hid", tag, fc))
                            if fc >= 1:
                                hd_low(fc - 1)
                    for j in range(UP, PER_EXPERT):
                        dve.wait_ge(pe_done, at("e_mm", tag, j) + pp)
                        e_low(j + SPL)
                        if j == UP:
                            hd_low(DOWN - 1)
                    for half in range(2):
                        cols = slice(512 * half, 512 * half + 512)
                        dve.wait_ge(act_done, at("e_y_hi", tag, half) + ae)
                        V.scalar_tensor_tensor(y_lo[:, cols], bank[4 + half][:, :], slot_w[:, :],
                                               y_hi[:, cols].bitcast(F32), ALU.mult, ALU.subtract)\
                            .then_inc(dve_done, dve_n(*(("e_y", tag) if half else ())))
                    for d in range(KD):
                        dve.wait_ge(pe_done, at("e_back", tag, d | 1) + pp)
                        V.scalar_tensor_tensor(xT[:, d, NC:T], bank[6 + d // 2 % 2][:, 256 * (d % 2):256 * (d % 2) + 256],
                                               modT[:, 1, 40 + d, 1:2], xT[:, d, NC:T], ALU.mult, ALU.add)\
                            .then_inc(dve_done, dve_n("e_add", tag, d))
                marks[("per_expert", tag, "dve")] = dve_n.n - n0
                dve_n.n = n0 + NE * (dve_n.n - n0)
                marks[("experts_end", tag)] = dve_n.n

            experts("main")
            own()
            overflow = dve.value_load(most_i[0:1, 0:1], min_val=0, max_val=NX)
            with dve.If(overflow > CAP):
                experts("more")
                own()
            for d in range(KD):
                V.tensor_tensor(fq[:, d, :], xT[:, d, NC:T], xT[:, d, NC:T], ALU.mult)\
                    .then_inc(fin_dve, fdve_n("fin_sq", d))
            dve.wait_ge(fin_act, at("fin_sd"))
            V.reciprocal(rs[:, 0:NX], rs[:, 0:NX]).then_inc(fin_dve, fdve_n())
            dve.wait_ge(fin_dve, fdve_n.n)
            for d in range(KD):
                V.scalar_tensor_tensor(fy[:, d, :], xT[:, d, NC:T], colv("g_final", d), rs[:, 0:NX],
                                       ALU.mult, ALU.mult).then_inc(fin_dve, fdve_n("fin_y", d))
            for t in range(2):
                dve.wait_ge(fin_act, at("fin_o", t))
                V.tensor_copy(fo[:, t, 512:D], bank[2 * t + 1][:, :])\
                    .then_inc(fin_dve, fdve_n(*(("fin_out",) if t else ())))


_INS = ["x", "c", "ctx", "c_ctx", "w_mod", "b_mod", "g_norm1", "g_norm2", "w_in", "conf_w", "conf_b", "conf_ln_g",
        "conf_ln_b", "sconv_w", "lru_conv_w", "lru_conv_b", "lru_wa", "lru_ba", "lru_wx", "lru_bx", "lru_lam",
        "g_mix", "w_out", "ffn_w1", "ffn_w3", "ffn_w2", "router_w", "router_b", "moe_w1", "moe_w3", "moe_w2",
        "g_final"]


def build(nc, shapes, known):
    aps = {n: nc.dram_tensor(f"in_{n}", shape, F32, kind="ExternalInput").ap() for n, shape in shapes.items()}
    out = nc.dram_tensor("out_0", (1, NX, D), F32, kind="ExternalOutput").ap()
    marks = {}
    program(nc, aps, out, known, marks)
    return marks


def kernel(**inputs):
    import numpy as np
    import concourse.bacc as bacc
    from concourse.bass_utils import run_bass_kernel_spmd

    arrays = {f"in_{n}": np.ascontiguousarray(inputs[n]) for n in _INS}
    shapes = {n: inputs[n].shape for n in _INS}
    marks = build(bacc.Bacc("TRN2", target_bir_lowering=False, num_devices=1), shapes, None)
    nc = bacc.Bacc("TRN2", target_bir_lowering=False, num_devices=1)
    build(nc, shapes, marks)
    r = run_bass_kernel_spmd(nc, [arrays], core_ids=[0])
    return r.results[0]["out_0"]
```

```python
import concourse.bass as bass
from concourse import mybir
from contextlib import ExitStack

F32 = mybir.dt.float32
F32R = mybir.dt.float32r
I32 = mybir.dt.int32
U32 = mybir.dt.uint32
ALU = mybir.AluOpType
ACT = mybir.ActivationFunctionType
AXX = mybir.AxisListType.X

P = 128
D = 1024
KD = D // P
NC = 256
NX = 256
T = NC + NX
GRID = 64
ROWS = NX // GRID
DFF = 2816
KF = DFF // P
KG = KF // 2
NE = 8
CAP = 128
MORE = 3
HEADS = D // 64
EPS = 1e-6
CONF_K, SCONV_K, LRU_K = 31, 3, 4
CONF_PAD = CONF_K // 2
CW = 2048
RAW = 5
SPL = 3
WIN_ORDER = [0, 1, 4, 3, 2, 5, 6, 7, 8]
NWIN, NWOUT = 9, 4
UP, DOWN = 2 * KF // 2, KF // 2
PER_EXPERT = UP + DOWN

COL = {}


def table(parts):
    row, out = 0, []
    for name, rows in parts:
        COL[name] = row
        out.append((name, row, rows))
        row += rows
    return out, row


TABLES = []
for _n, _parts in enumerate([
    [("c", 8), ("c_ctx", 8), ("g_norm1", 16), ("g_norm2", 16), ("g_final", 8), ("g_mix", 16),
     ("sconv_w", 12), ("lru_conv_w", 32)],
    [("conf_b", 4), ("conf_ln_g", 4), ("conf_ln_b", 4), ("lru_conv_b", 8), ("lru_ba", 16), ("lru_bx", 16),
     ("lru_lam", 16)],
    [("conf_w", 124)],
    [("b_mod", 96)],
]):
    _t, _rows = table(_parts)
    for _name, _row, _k in _t:
        COL[_name] = 128 * _n + _row
    TABLES.append((_t, _rows))


class Count:

    def __init__(self, marks):
        self.n, self.marks, self.again = 0, marks, False

    def __call__(self, *name):
        self.n += 1
        if name and not self.again:
            assert name not in self.marks
            self.marks[name] = self.n
        return 1


def schedule():
    chunks = [("x", 0), ("x", 1)] + [("mod", 0, j) for j in range(8)]
    for l in range(2):
        chunks += [("w_in", l, c) for c in WIN_ORDER]
        chunks += [("w_out", l, c) for c in range(SPL)]
        if l == 0:
            chunks += [("mod", 0, j) for j in range(8, 24)]
        chunks += [("w_out", l, c) for c in range(SPL, NWOUT)]
        if l == 0:
            mod = iter(range(24))
            for g in range(2):
                for i in range(KG):
                    chunks.append(("up", g, i))
                    chunks += [("mod", 1, j) for j in [next(mod, None)] if j is not None]
                for d in range(KD):
                    chunks.append(("down", g, d))
                    chunks += [("mod", 1, j) for j in [next(mod, None)] if j is not None]
    return chunks


CHUNKS = schedule()
SPLIT = [c for c in CHUNKS if c[0] in ("w_in", "w_out", "up", "down")]
POS = {c: n for n, c in enumerate(CHUNKS)}
ORD = {c: n for n, c in enumerate(SPLIT)}


def width(c):
    return KG * P if c[0] == "down" else CW


def program(nc, a, out, known, marks):
    def at(*name):
        return known[name] if known else 1

    ctx = ExitStack()
    with ctx:
        def sem(name):
            return ctx.enter_context(nc.semaphore(name))

        cursor = [-(-nc.sbuf_base // 64) * 64]

        def sb(name, shape, dt=F32):
            size = 4
            for s in shape[1:]:
                size *= s
            t = nc.alloc_sbuf_tensor_at(name, shape, dt, offset=cursor[0])
            cursor[0] += -(-size // 32) * 32
            return t

        ident = sb("ident", [P, P])
        ones_d = sb("ones_d", [P, P])
        ones_c = sb("ones_c", [P, P])
        ones_h = sb("ones_h", [P, KD, HEADS])
        eps = sb("eps", [P, 1])
        PT = sb("PT", [P, 4 * P])
        cc = sb("cc", [P, KD, 2])
        modT = sb("modT", [P, 2, 48, 2])
        amp = sb("amp", [P, 2, 2, KD, 2])
        clp = sb("clp", [P, 16])
        cln = sb("cln", [P, 16])
        lt = sb("lt", [P, 4, 16])
        xT = sb("xT", [P, KD, T])
        raw = sb("raw", [P, RAW, CW])
        w_hi = sb("w_hi", [P, SPL, CW], F32R)
        w_lo = sb("w_lo", [P, SPL, CW], F32R)
        G = sb("G", [P, 16, P])
        tb = sb("tb", [P, 2, T])
        sq = sb("sq", [P, 2, T])
        rs = sb("rs", [P, T])
        area = cursor[0]

        h_hi = sb("h_hi", [P, KD, T], F32R)
        h_lo = sb("h_lo", [P, KD, T], F32R)
        rest = cursor[0]
        cxp = sb("cxp", [P, 4, 2, 260])
        xc = sb("xc", [P, 4, T])
        vp = sb("vp", [P, 2, NC + 2 * CONF_PAD + ROWS * (GRID + 2 * CONF_PAD)])
        sx = sb("sx", [P, 2, T])
        spread = nc.alloc_sbuf_tensor_at("spread", [HEADS, KD, P], F32, offset=cursor[0] - 8 * T)
        sp_ = sb("sp_", [P, 2, NC + 2 + NX + 2 * GRID])
        y = sb("y", [P, KD, T])
        assert cursor[0] <= nc.sbuf_usable_end, cursor[0]
        cursor[0] = area
        lr = sb("lr", [P, 4, T])
        li = sb("li", [P, 4, T])
        la = sb("la", [P, 4, T])
        lm = sb("lm", [P, 4, T])
        cursor[0] = rest
        rows_sb = sb("rows_sb", [P, 4, P])
        cursor[0] = rest
        f_hi = sb("f_hi", [P, KG, T], F32R)
        f_lo = sb("f_lo", [P, KG, T], F32R)
        cursor[0] = area
        hT = sb("hT", [P, KD, NX])
        ht_hi = sb("ht_hi", [P, 2, D], F32R)
        ht_lo = sb("ht_lo", [P, 2, D], F32R)
        sel = sb("sel", [P, 2, CAP], F32R)
        selT = sb("selT", [P, NX], F32R)
        hc_hi = sb("hc_hi", [P, KD, CAP], F32R)
        hc_lo = sb("hc_lo", [P, KD, CAP], F32R)
        gs = sb("gs", [P, 2, 256])
        hid = sb("hid", [P, DFF])
        hd_hi = sb("hd_hi", [P, KF, CAP], F32R)
        hd_lo = sb("hd_lo", [P, KF, CAP], F32R)
        y_hi = sb("y_hi", [P, D], F32R)
        y_lo = sb("y_lo", [P, D], F32R)
        rw = sb("rw", [P, KD, NE])
        rb = sb("rb", [1, NE])
        one = sb("one", [1, P])
        before = sb("before", [P, P])
        all1 = sb("all1", [P, P])
        iota_s = sb("iota_s", [P, CAP])
        iota_e = sb("iota_e", [P, NE])
        lg = sb("lg", [P, 2, NE])
        top = sb("top", [P, 2, 8])
        topi = sb("topi", [P, 2, 8], U32)
        topf = sb("topf", [P, 2, 8])
        pr = sb("pr", [P, 2, 4])
        oh = sb("oh", [P, 2, 2, NE])
        mask = sb("mask", [P, 2, NE])
        comb = sb("comb", [P, 2, NE])
        pos = sb("pos", [P, 2, NE])
        pos1 = sb("pos1", [P, 2, 1])
        cw1 = sb("cw1", [P, 2, 1])
        slot_w = sb("slot_w", [P, 1])
        full = sb("full", [P, NE])
        rev = sb("rev", [P, NE])
        again = sb("again", [P, 2, 8])
        again_i = sb("again_i", [P, 2, 8], I32)
        assert cursor[0] <= nc.sbuf_usable_end, cursor[0]
        cursor[0] = area
        fq = sb("fq", [P, KD, NX])
        fy = sb("fy", [P, KD, NX])
        fo = sb("fo", [P, 2, D])

        bank = [ctx.enter_context(nc.psum_tensor(f"bank{i}", [P, 512], F32)) for i in range(8)]
        MOD, STAT = bank[6], bank[7]

        pe_done, act_done, dve_done, pool_done = sem("pe_done"), sem("act_done"), sem("dve_done"), sem("pool_done")
        table_in, gate_in, rout_in, stored = sem("table_in"), sem("gate_in"), sem("rout_in"), sem("stored")
        raw_in = [sem(f"raw_in{s}") for s in range(RAW)]
        exp_in = [sem(f"exp_in{s}") for s in range(RAW)]
        fin_dve, fin_act, fin_pe = sem("fin_dve"), sem("fin_act"), sem("fin_pe")

        arrived, level = {}, [0] * RAW
        for n, c in enumerate(CHUNKS):
            level[n % RAW] += 32 if c[0] == "up" else 16
            arrived[c] = level[n % RAW]
        e_arrived, e_level = [], [0] * RAW
        for j in range(PER_EXPERT):
            e_level[j % RAW] += 32 if j < UP else 16
            e_arrived.append(e_level[j % RAW])

        def free_name(c):
            if c[0] == "x":
                return ("xt", KD - 1)
            return ("lo", ORD[c]) if c in ORD else ("used",) + c

        def free_sem(c):
            return dve_done if c in ORD else pe_done

        lo = [0, NC]
        streams = [(0, 1), (1,)]

        def tok(s):
            return slice(s * NC, (s + 1) * NC)

        def colv(name, i, n=1):
            return PT[:, COL[name] + i:COL[name] + i + n]

        def vp_x(t, k):
            v = vp[:, t, NC + 2 * CONF_PAD:].rearrange("p (r w) -> p r w", r=ROWS)
            return v[:, :, k:k + GRID]

        def padded_v(t, s, k):
            return vp[:, t, k:k + NC] if s == 0 else vp_x(t, k)

        def padded_s(t, s, k):
            o = k if s == 0 else NC + 2 + GRID * k
            return sp_[:, t, o:o + 256]

        def grid(ap, s):
            return ap if s == 0 else ap.rearrange("p (r w) -> p r w", r=ROWS)

        def weights(c):
            l = c[1]
            if c[0] == "mod":
                return a["w_mod"][l].rearrange("(k p) c -> p k c", p=P)[:, :, 256 * c[2]:256 * c[2] + 256]
            if c[0] == "w_in":
                return a["w_in"][l].rearrange("(k p) c -> p k c", p=P)[:, :, 256 * c[2]:256 * c[2] + 256]
            if c[0] == "w_out":
                return a["w_out"][l].rearrange("(k p) c -> p k c", p=P)[:, :, 256 * c[2]:256 * c[2] + 256]
            if c[0] == "down":
                w = a["ffn_w2"][0].rearrange("(k p) c -> p k c", p=P)
                return w[:, KG * l:KG * l + KG, P * c[2]:P * c[2] + P]
            return (a["ctx"] if l == 0 else a["x"])[0].rearrange("(t p) c -> p t c", p=P)

        pe_n, act_n, dve_n, pool_n = (Count(marks) for _ in range(4))
        fpe_n, fact_n, fdve_n = (Count(marks) for _ in range(3))
        LOGIT, RANK = 256, 288

        def evacuated(c):
            if c[0] == "w_in" and c[2] != 3:
                return act_done, at("evac", ORD[c])
            if c[0] == "w_in":
                return dve_done, at("evac", ORD[c])
            if c[0] == "w_out":
                return dve_done, at("xT", "w_out", c[1], 2 * c[2] + 1)
            if c[0] == "up":
                return dve_done, at("hid", c[1], c[2])
            return dve_done, at("xT", "down", c[1], c[2])

        def y_low(i8, l, ts, dve, V):
            dve.wait_ge(act_done, at("y_hi", l, i8))
            V.scalar_tensor_tensor(h_lo[:, i8, ts], y[:, i8, ts], colv("g_mix", 8 * l + i8),
                                   h_hi[:, i8, ts].bitcast(F32), ALU.mult, ALU.subtract)\
                .then_inc(dve_done, dve_n("y_lo", l, i8))

        block = ctx.enter_context(nc.Block())

        @block.sync
        def _(sp):
            def load(c):
                n = POS[c]
                slot = raw[:, n % RAW, :]
                if n >= RAW:
                    sp.wait_ge(free_sem(CHUNKS[n - RAW]), at(*free_name(CHUNKS[n - RAW])))
                if c[0] == "up":
                    dst = slot.rearrange("p (k w c) -> p k w c", k=KD, w=2)
                    f = P * (KG * c[1] + c[2])
                    for w, name in enumerate(("ffn_w1", "ffn_w3")):
                        src = a[name][0].rearrange("(k p) c -> p k c", p=P)[:, :, f:f + P]
                        sp.dma_start(dst[:, :, w, :], src).then_inc(raw_in[n % RAW], 16)
                else:
                    k = {"x": 2, "down": KG}.get(c[0], KD)
                    dst = slot[:, 0:width(c)].rearrange("p (k c) -> p k c", k=k)
                    sp.dma_start(dst, weights(c)).then_inc(raw_in[n % RAW], 16)

            def gate_weights(l):
                for w, name in enumerate(("lru_wa", "lru_wx")):
                    for d in range(2):
                        src = a[name][l, d].rearrange("(t u) i j -> u i t j", u=2)
                        for u in range(2):
                            half = slice(64 * u, 64 * u + 64)
                            sp.dma_start(G[half, 8 * d + 4 * w:8 * d + 4 * w + 4, half], src[u])\
                              .then_inc(gate_in, 16)

            for n, (parts, _) in enumerate(TABLES):
                for name, row, rows in parts:
                    src = a[name]
                    dims = " ".join(f"a{i}" for i in range(len(src.shape)))
                    flat = src.rearrange(f"{dims} -> ({dims})") if len(src.shape) > 1 else src
                    sp.dma_start(rows_sb[row:row + rows, n, :], flat.rearrange("(r c) -> r c", c=P))\
                      .then_inc(table_in, 16)
            for c in CHUNKS[:10]:
                load(c)
            sp.wait_ge(pool_done, at("G_zero"))
            gate_weights(0)
            for c in CHUNKS[10:]:
                if c == ("up", 0, 0):
                    sp.wait_ge(pe_done, at("gate", 0, 7))
                    gate_weights(1)
                load(c)

            def expert_chunk(e, j):
                slot = raw[:, j % RAW, :]
                if j < UP:
                    fc, half = j // 2, j % 2
                    dst = slot.rearrange("p (k w c) -> p k w c", k=4, w=2)
                    for w, name in enumerate(("moe_w1", "moe_w3")):
                        src = a[name][0].rearrange("e (k p) c -> (e k) p c", p=P)
                        src = src[bass.ds(e * KD + 4 * half, 4), :, 256 * fc:256 * fc + 256]
                        sp.dma_start(dst[:, :, w, :], src.rearrange("k p c -> p k c"))\
                          .then_inc(exp_in[j % RAW], 16)
                else:
                    src = a["moe_w2"][0].rearrange("e (k p) c -> (e k) p c", p=P)
                    src = src[bass.ds(e * KF + 2 * (j - UP), 2), :, :]
                    sp.dma_start(slot.rearrange("p (k c) -> p k c", k=2), src.rearrange("k p c -> p k c"))\
                      .then_inc(exp_in[j % RAW], 16)

            K = at("per_expert", "dve")
            last = {j % RAW: j for j in range(PER_EXPERT)}

            def rest_of(e, shift):
                for j in range(RAW, PER_EXPERT):
                    sp.wait_ge(dve_done, at("e_lo", j - RAW) + shift)
                    expert_chunk(e, j)

            def first_of(e, shift):
                for j in range(RAW):
                    sp.wait_ge(dve_done, at("e_lo", last[j]) + shift)
                    expert_chunk(e, j)

            for c in CHUNKS[-RAW:]:
                sp.wait_ge(free_sem(c), at(*free_name(c)))
            sp.wait_ge(pe_done, at("mm", ORD[("w_out", 1, NWOUT - 1)]))
            sp.dma_start(rw[:, :, :], a["router_w"][0].rearrange("(k p) e -> p k e", p=P)).then_inc(rout_in, 16)
            sp.dma_start(rb[:, :], a["router_b"]).then_inc(rout_in, 16)
            for j in range(RAW):
                expert_chunk(0, j)
            with sp.Fori(0, NE - 1, 1) as e:
                rest_of(e, e * K)
                first_of(e + 1, e * K)
            rest_of(NE - 1, (NE - 1) * K)
            sp.wait_ge(dve_done, at("again"))
            with sp.Fori(0, MORE, 1) as r:
                e = sp.value_load(again_i[0:1, 1, bass.ds(r, 1)], min_val=0, max_val=NE - 1)
                left = sp.value_load(again_i[0:1, 0, bass.ds(r, 1)], min_val=0, max_val=NE)
                with sp.If(left > 0):
                    first_of(e, (NE - 1 + r) * K)
                    rest_of(e, (NE + r) * K)
                sp.nop()
            sp.wait_ge(fin_dve, at("fin_out"))
            sp.dma_start(out[0].rearrange("(t p) c -> p t c", p=P), fo[:, :, :]).then_inc(stored, 16)
            sp.wait_ge(stored, 16)

        @block.gpsimd
        def _(pool):
            def own():
                if pool_n.n:
                    pool.wait_ge(pool_done, pool_n.n)

            for m, v in ((ident, 0.0), (ones_d, 1.0 / D), (ones_c, 1.0 / 256), (eps, EPS)):
                own()
                nc.gpsimd.memset(m[:, :], v).then_inc(pool_done, pool_n())
            own()
            nc.gpsimd.affine_select(out=ident[:, :], in_=ident[:, :], compare_op=ALU.not_equal, fill=1.0, base=0,
                                    pattern=[[-1, P]], channel_multiplier=1).then_inc(pool_done, pool_n("ident"))
            own()
            nc.gpsimd.memset(ones_h[:, :, :], 0.0).then_inc(pool_done, pool_n())
            flat = ones_h[:, :, :].rearrange("p k h -> p (k h)")
            for h in range(2):
                own()
                nc.gpsimd.memset(flat[64 * h:64 * h + 64, h:h + (HEADS + 2) * (KD - 1) + 1:HEADS + 2], 1.0 / 64)\
                    .then_inc(pool_done, pool_n())
            own()
            nc.gpsimd.memset(G[:, :, :], 0.0).then_inc(pool_done, pool_n("G_zero"))
            for l in range(2):
                pool.wait_ge(pe_done, at("tables") if l == 0 else at("mm", ORD[("down", 1, KD - 1)]))
                own()
                nc.gpsimd.memset(vp[:, :, :], 0.0).then_inc(pool_done, pool_n())
                own()
                nc.gpsimd.memset(sp_[:, :, :], 0.0).then_inc(pool_done, pool_n())
                own()
                nc.gpsimd.memset(cxp[:, :, :, :], 0.0).then_inc(pool_done, pool_n("padded", l))
                pool.wait_ge(dve_done, at("sx_read", l))
                own()
                nc.gpsimd.memset(spread[:, :, :], 0.0).then_inc(pool_done, pool_n())
                own()
                view = spread[:, :, :].rearrange("q k (h c) -> q k h c", h=2)
                nc.gpsimd.affine_select(out=view, in_=view, compare_op=ALU.not_equal, fill=1.0, base=0,
                                        pattern=[[-2, KD], [-1, 2], [0, 64]], channel_multiplier=1)\
                    .then_inc(pool_done, pool_n("spread", l))

            pool.wait_ge(pe_done, at("mm", ORD[("w_out", 1, NWOUT - 1)]))
            own()
            nc.gpsimd.memset(one[:, :], 1.0).then_inc(pool_done, pool_n())
            own()
            nc.gpsimd.memset(all1[:, :], 1.0).then_inc(pool_done, pool_n())
            own()
            nc.gpsimd.memset(before[:, :], 1.0).then_inc(pool_done, pool_n())
            own()
            nc.gpsimd.iota(iota_s[:, :], pattern=[[1, CAP]], base=0, channel_multiplier=0,
                           allow_small_or_imprecise_dtypes=True).then_inc(pool_done, pool_n())
            own()
            nc.gpsimd.iota(iota_e[:, :], pattern=[[1, NE]], base=0, channel_multiplier=0,
                           allow_small_or_imprecise_dtypes=True).then_inc(pool_done, pool_n())
            own()
            nc.gpsimd.affine_select(out=before[:, :], in_=before[:, :], compare_op=ALU.is_gt, fill=0.0, base=0,
                                    pattern=[[1, P]], channel_multiplier=-1).then_inc(pool_done, pool_n("routing"))

        @block.tensor
        def _(pe):
            def mm(dst, lhsT, rhs, first, last):
                return nc.tensor.matmul(dst, lhsT, rhs, start=first, stop=last)

            def split_mm(dst, w, x, first, last):
                mm(dst, w[0], x[0], first, False)
                mm(dst, w[0], x[1], False, False)
                return mm(dst, w[1], x[0], False, last)

            pe.wait_ge(table_in, 16 * sum(len(parts) for parts, _ in TABLES))
            pe.wait_ge(pool_done, at("ident"))
            for n, (_, rows) in enumerate(TABLES):
                i = nc.tensor.transpose(STAT[:, P * n:P * n + rows], rows_sb[0:rows, n, :], ident[0:rows, 0:rows])
            i.then_inc(pe_done, pe_n("tables"))
            for s in range(2):
                pe.wait_ge(raw_in[s], 16)
            for d in range(KD):
                if d >= 6:
                    pe.wait_ge(dve_done, at("xT", "in", d - 6))
                for s in range(2):
                    for t in range(2):
                        i = nc.tensor.transpose(bank[d % 6][:, P * (2 * s + t):P * (2 * s + t) + P],
                                                raw[:, s, D * t + P * d:D * t + P * d + P], ident[:, :])
                i.then_inc(pe_done, pe_n("xt", d))

            def modulation(l, j):
                c = ("mod", l, j)
                slot = POS[c] % RAW
                if j == 0 and l == 0:
                    pe.wait_ge(act_done, at("cc"))
                pe.wait_ge(raw_in[slot], arrived[c])
                for t in range(2):
                    o = 96 * l + 2 * (2 * j + t)
                    for k in range(KD):
                        i = mm(MOD[:, o:o + 2], raw[:, slot, 256 * k + P * t:256 * k + P * t + P], cc[:, k, :],
                               k == 0, k == KD - 1)
                i.then_inc(pe_done, pe_n("used", *c))

            def mean_square(l, w, ts, previous):
                previous()
                for d in range(KD):
                    pe.wait_ge(act_done, at("sq", l, w, d))
                    mm(STAT[:, ts], ones_d[:, :], sq[:, d % 2, ts], d == 0, d == KD - 1)\
                        .then_inc(pe_done, pe_n("ms", l, w, d))

            def take(c):
                s = ORD[c]
                pe.wait_ge(dve_done, at("lo", s))
                if s >= 3:
                    pe.wait_ge(*evacuated(SPLIT[s - 3]))
                return (w_hi[:, s % SPL, :], w_lo[:, s % SPL, :]), bank[2 * (s % 3):2 * (s % 3) + 2]

            def project(c, ts, ready):
                w, banks = take(c)
                for k in range(KD):
                    if ready:
                        pe.wait_ge(dve_done, at(*ready, k))
                    for t in range(2):
                        o = 256 * k + P * t
                        i = split_mm(banks[t][:, ts], (w[0][:, o:o + P], w[1][:, o:o + P]),
                                     (h_hi[:, k, ts], h_lo[:, k, ts]), k == 0, k == KD - 1)
                i.then_inc(pe_done, pe_n("mm", ORD[c]))

            for j in range(8):
                modulation(0, j)
            for l in range(2):
                ts = slice(lo[l], T)
                mean_square(l, 1, slice(0, T), lambda: pe.wait_ge(dve_done, at("PT")) if l == 0 else
                            pe.wait_ge(act_done, at("sd", 0, 2)))
                for n, c in enumerate(WIN_ORDER):
                    project(("w_in", l, c), slice(0, T) if c in (5, 6) else ts, ("h_lo", l, 1) if n == 0 else None)
                pe.wait_ge(dve_done, at("conf_u", l))
                for t in range(2):
                    i = mm(STAT[:, ts], ones_c[:, :], y[:, t, ts], t == 0, t == 1)
                i.then_inc(pe_done, pe_n("conf_mean", l))
                pe.wait_ge(gate_in, 8 * 16 * (l + 1))
                for q in range(8):
                    d, t = q // 4, q % 4
                    if q < 4:
                        pe.wait_ge(dve_done, at("xc", l, t))
                    if q < 3:
                        pe.wait_ge(*evacuated(("w_in", l, WIN_ORDER[6 + q])))
                    else:
                        pe.wait_ge(act_done, at("gate_read", l, q - 3))
                    for w in range(2):
                        i = mm(bank[2 * (q % 3) + w][:, :], G[:, 8 * d + 4 * w + t, :], xc[:, t, :], True, True)
                    i.then_inc(pe_done, pe_n("gate", l, q))
                    if q == 5:
                        pe.wait_ge(dve_done, at("conf_c", l, 1))
                        for v in range(2):
                            pe.wait_ge(act_done, at("conf_sq", l, v))
                            i = mm(STAT[:, ts], ones_c[:, :], sq[:, v, ts], v == 0, v == 1)
                        i.then_inc(pe_done, pe_n("conf_var", l))
                    if l == 0 and q >= 3:
                        for j in range(8 + 3 * (q - 3), 8 + 3 * (q - 3) + 3):
                            modulation(0, j)
                if l == 0:
                    modulation(0, 23)
                for i8 in range(KD):
                    pe.wait_ge(act_done, at("head_sq", l, i8))
                    if i8 == 0:
                        pe.wait_ge(act_done, at("conf_sd", l))
                    mm(STAT[0:HEADS, ts], ones_h[:, i8, :], sq[:, i8 % 2, ts], i8 == 0, i8 == KD - 1)\
                        .then_inc(pe_done, pe_n("head_ms", l, i8))
                pe.wait_ge(dve_done, at("head_r", l))
                pe.wait_ge(act_done, at("gate_read", l, 7))
                pe.wait_ge(pool_done, at("spread", l))
                for i8 in range(KD):
                    if i8 >= 4:
                        pe.wait_ge(dve_done, at("y_n", l, i8 - 4))
                    mm(bank[2 + i8 % 4][:, ts], spread[:, i8, :], rs[0:HEADS, ts], True, True)\
                        .then_inc(pe_done, pe_n("head_f", l, i8))
                for c in range(NWOUT):
                    project(("w_out", l, c), ts, ("y_lo", l) if c == 0 else None)
                mean_square(l, 2, ts, lambda: pe.wait_ge(act_done, at("head_sd", l)))
                if l == 1:
                    break
                mod = iter(range(24))
                for g in range(2):
                    for i11 in range(KG):
                        c = ("up", g, i11)
                        w, banks = take(c)
                        for k in range(KD):
                            if g == 0 and i11 == 0:
                                pe.wait_ge(dve_done, at("h_lo", 0, 2, k))
                            for v in range(2):
                                o = 256 * k + P * v
                                i = split_mm(banks[v][:, :], (w[0][:, o:o + P], w[1][:, o:o + P]),
                                             (h_hi[:, k, :], h_lo[:, k, :]), k == 0, k == KD - 1)
                        i.then_inc(pe_done, pe_n("mm", ORD[c]))
                        for j in [next(mod, None)]:
                            if j is not None:
                                modulation(1, j)
                    for d in range(KD):
                        c = ("down", g, d)
                        w, banks = take(c)
                        for k in range(KG):
                            if d == 0:
                                pe.wait_ge(dve_done, at("f_lo", g, k))
                            i = split_mm(banks[0][:, :], (w[0][:, P * k:P * k + P], w[1][:, P * k:P * k + P]),
                                         (f_hi[:, k, :], f_lo[:, k, :]), k == 0, k == KG - 1)
                        i.then_inc(pe_done, pe_n("mm", ORD[c]))
                        for j in [next(mod, None)]:
                            if j is not None:
                                modulation(1, j)

            pe.wait_ge(rout_in, 32)
            pe.wait_ge(pool_done, at("routing"))
            for t in range(2):
                for k in range(KD):
                    pe.wait_ge(act_done, at("h", k))
                    mm(MOD[:, LOGIT + NE * t:LOGIT + NE * t + NE], hT[:, k, P * t:P * t + P], rw[:, k, :], k == 0, False)
                i = mm(MOD[:, LOGIT + NE * t:LOGIT + NE * t + NE], one[:, :], rb[:, :], False, True)
            i.then_inc(pe_done, pe_n("logits"))
            pe.wait_ge(*evacuated(("w_out", 1, NWOUT - 1)))
            for t in range(2):
                for k in range(KD):
                    i = nc.tensor.transpose(bank[2 * t + k // 4][:, P * (k % 4):P * (k % 4) + P],
                                            hT[:, k, P * t:P * t + P], ident[:, :])
                i.then_inc(pe_done, pe_n("ht", t))
            pe.wait_ge(dve_done, at("mask"))
            mm(MOD[:, RANK:RANK + NE], before[:, :], mask[:, 0, :], True, True)
            mm(MOD[:, RANK + NE:RANK + 2 * NE], all1[:, :], mask[:, 0, :], True, False)
            mm(MOD[:, RANK + NE:RANK + 2 * NE], before[:, :], mask[:, 1, :], False, True)
            for t in range(2):
                i = mm(MOD[:, RANK + 2 * NE:RANK + 3 * NE], all1[:, :], mask[:, t, :], t == 0, t == 1)
            i.then_inc(pe_done, pe_n("rank"))

            Kd, Ka = at("per_expert", "dve"), at("per_expert", "act")

            def expert(turn_no):
                de, ae = turn_no * Kd, turn_no * Ka
                pe.wait_ge(dve_done, at("e_sel") + de)
                for part, (src, b) in enumerate(((ht_hi, 6), (ht_lo, 4))):
                    for k in range(KD):
                        for t in range(2):
                            i = mm(bank[b + k // 4][:, P * (k % 4):P * (k % 4) + P],
                                   src[:, t, P * k:P * k + P], sel[:, t, :], t == 0, t == 1)
                    i.then_inc(pe_done, pe_n("e_gather", part))
                for t in range(2):
                    mm(bank[3][:, 256:257], sel[:, t, :].bitcast(F32), cw1[:, t, :], t == 0, t == 1)
                for t in range(2):
                    i = nc.tensor.transpose(bank[2][:, P * t:P * t + P], sel[:, t, :].bitcast(F32), ident[:, :])
                i.then_inc(pe_done, pe_n("e_turned"))

                def turn(fc):
                    pe.wait_ge(dve_done, at("e_hid", fc) + de)
                    if fc >= 2:
                        pe.wait_ge(dve_done, at("e_hd", fc - 2) + de)
                    else:
                        pe.wait_ge(act_done, at("e_selT") + ae)
                        pe.wait_ge(dve_done, at("e_slot_w") + de)
                    for t in range(2):
                        o = 256 * fc + P * t
                        j = nc.tensor.transpose(bank[2 + fc % 2][:, P * t:P * t + P], hid[:, o:o + P], ident[:, :])
                    j.then_inc(pe_done, pe_n("e_turn", fc))

                pe.wait_ge(act_done, at("e_hc") + ae)
                pe.wait_ge(dve_done, at("e_hc_lo") + de)
                for j in range(UP):
                    fc, s = j // 2, j % SPL
                    pe.wait_ge(dve_done, at("e_lo", j) + de)
                    if j % 2 == 0 and fc >= 2:
                        pe.wait_ge(dve_done, at("e_hid", fc - 2) + de)
                    for kk in range(4):
                        k, cols = 4 * (j % 2) + kk, slice(512 * kk, 512 * kk + 512)
                        i = split_mm(bank[fc % 2][:, :], (hc_hi[:, k, :], hc_lo[:, k, :]),
                                     (w_hi[:, s, cols], w_lo[:, s, cols]), k == 0, k == KD - 1)
                    i.then_inc(pe_done, pe_n("e_mm", j))
                    if j % 2 and fc >= 1:
                        turn(fc - 1)
                for j in range(UP, PER_EXPERT):
                    s = j % SPL
                    pe.wait_ge(dve_done, at("e_lo", j) + de)
                    pe.wait_ge(dve_done, at("e_hd", j - UP) + de)
                    for kk in range(2):
                        k = 2 * (j - UP) + kk
                        for half in range(2):
                            cols = slice(D * kk + 512 * half, D * kk + 512 * half + 512)
                            i = split_mm(bank[4 + half][:, :], (hd_hi[:, k, :], hd_lo[:, k, :]),
                                         (w_hi[:, s, cols], w_lo[:, s, cols]), k == 0, k == KF - 1)
                    i.then_inc(pe_done, pe_n("e_mm", j))
                    if j == UP:
                        turn(DOWN - 1)
                pe.wait_ge(dve_done, at("e_y") + de)
                for d in range(KD):
                    dst = bank[6 + d // 2 % 2][:, 256 * (d % 2):256 * (d % 2) + 256]
                    if d % 2 == 0 and d >= 4:
                        pe.wait_ge(dve_done, at("e_add", d - 3) + de)
                    mm(dst, y_hi[:, P * d:P * d + P], selT[:, :], True, False)
                    mm(dst, y_lo[:, P * d:P * d + P], selT[:, :], False, True)\
                        .then_inc(pe_done, pe_n("e_back", d))

            n0 = pe_n.n
            with pe.Fori(0, NE, 1) as e:
                expert(e)
            marks[("per_expert", "pe")] = pe_n.n - n0
            pe_n.n, pe_n.again = n0, True
            pe.wait_ge(dve_done, at("again"))
            with pe.Fori(0, MORE, 1) as r:
                left = pe.value_load(again_i[0:1, 0, bass.ds(r, 1)], min_val=0, max_val=NE)
                with pe.If(left > 0):
                    expert(r + NE)
                pe.nop()
            for d in range(KD):
                pe.wait_ge(fin_dve, at("fin_sq", d))
                i = mm(STAT[:, 0:NX], ones_d[:, :], fq[:, d, :], d == 0, d == KD - 1)
            i.then_inc(fin_pe, fpe_n("fin_ms"))
            for t in range(2):
                for d in range(KD):
                    pe.wait_ge(fin_dve, at("fin_y", d))
                    i = nc.tensor.transpose(bank[2 * t + d // 4][:, P * (d % 4):P * (d % 4) + P],
                                            fy[:, d, P * t:P * t + P], ident[:, :])
                i.then_inc(fin_pe, fpe_n("fin_turn", t))

        @block.scalar
        def _(act):
            def hi(s):
                if s >= len(SPLIT):
                    return
                c = SPLIT[s]
                n = width(c)
                act.wait_ge(raw_in[POS[c] % RAW], arrived[c])
                if s >= SPL:
                    act.wait_ge(pe_done, at("mm", s - SPL))
                nc.scalar.activation(w_hi[:, s % SPL, 0:n], raw[:, POS[c] % RAW, 0:n], ACT.Copy)\
                    .then_inc(act_done, act_n("hi", s))

            def squares(l, w, ts, ready):
                for d in range(KD):
                    act.wait_ge(dve_done, at("xT", *ready, d))
                    if d >= 2:
                        act.wait_ge(pe_done, at("ms", l, w, d - 2))
                    nc.scalar.activation(sq[:, d % 2, ts], xT[:, d, ts], ACT.Square)\
                        .then_inc(act_done, act_n("sq", l, w, d))
                act.wait_ge(pe_done, at("ms", l, w, KD - 1))
                nc.scalar.activation(rs[:, ts], STAT[:, ts], ACT.Sqrt, bias=eps[:, :])\
                    .then_inc(act_done, act_n("sd", l, w))

            def h_high(l, w, which, dst, name):
                for d in range(KD):
                    act.wait_ge(dve_done, at("t", l, w, d))
                    for s in which:
                        shift = modT[:, l, 8 * (0 if w == 1 else 3) + d, s:s + 1]
                        ap = dst[:, d, tok(s)] if name == "h_hi" else dst[:, d, :]
                        i = nc.scalar.activation(ap, tb[:, d % 2, tok(s)], ACT.Identity, bias=shift)
                        if s != which[-1]:
                            i.then_inc(act_done, act_n())
                    i.then_inc(act_done, act_n(*((name, l, w, d) if name == "h_hi" else (name, d))))

            act.wait_ge(dve_done, at("PT"))
            for s, name in enumerate(("c_ctx", "c")):
                i = nc.scalar.activation(cc[:, :, s], colv(name, 0, KD), ACT.Silu)
                i.then_inc(act_done, act_n(*(("cc",) if s else ())))
            act.wait_ge(dve_done, at("lam_abs"))
            nc.scalar.activation(lt[:, 0, :], lt[:, 0, :], ACT.Exp, scale=-1.0).then_inc(act_done, act_n("lam_exp"))

            for l in range(2):
                ts = slice(lo[l], T)
                squares(l, 1, slice(0, T), ("in",) if l == 0 else ("down", 1))
                h_high(l, 1, (0, 1), h_hi, "h_hi")
                if l == 0:
                    for s in range(SPL):
                        hi(s)
                for n, c in enumerate(WIN_ORDER):
                    s = ORD[("w_in", l, c)]
                    b = bank[2 * (s % 3):2 * (s % 3) + 2]
                    act.wait_ge(pe_done, at("mm", s))
                    hi(s + SPL)
                    for t in range(2):
                        last = ("evac", s) if t else ()
                        if c == 0:
                            i = nc.scalar.activation(tb[:, t, ts], b[t][:, ts], ACT.Copy)
                        elif c == 1:
                            i = nc.scalar.activation(sq[:, t, ts], b[t][:, ts], ACT.Tanh, scale=0.5)
                        elif c == 4:
                            i = nc.scalar.activation(sx[:, t, ts], b[t][:, ts], ACT.Copy)
                        elif c == 2:
                            i = nc.scalar.activation(y[:, 2 + t, ts], b[t][:, ts], ACT.Copy)
                        elif c in (5, 6):
                            if c == 5 and t == 0:
                                act.wait_ge(pool_done, at("padded", l))
                            i = nc.scalar.activation(cxp[:, 2 * (c - 5) + t, :, 2:2 + 256],
                                                     b[t][:, :].rearrange("p (s w) -> p s w", s=2), ACT.Copy)
                        elif c in (7, 8):
                            act.wait_ge(dve_done, at("xc", l, 3))
                            i = nc.scalar.activation(
                                cxp[:, 2 * (c - 7) + t, lo[l] // NC:2, 2:2 + 256],
                                b[t][:, ts].rearrange("p (s w) -> p s w", w=256), ACT.Gelu_apprx_tanh)
                        else:
                            continue
                        i.then_inc(act_done, act_n(*last))
                def gates(d, t):
                    q = 4 * d + t
                    act.wait_ge(pe_done, at("gate", l, q))
                    if d == 1:
                        act.wait_ge(dve_done, at("scan", l, 0, t))
                    else:
                        act.wait_ge(pe_done, at("mm", ORD[("w_in", l, WIN_ORDER[-1])]))
                    b = bank[2 * (q % 3):2 * (q % 3) + 2]
                    nc.scalar.activation(lr[:, t, :], b[0][:, :], ACT.Tanh, scale=0.5,
                                         bias=colv("lru_ba", 8 * l + q)).then_inc(act_done, act_n())
                    nc.scalar.activation(li[:, t, :], b[1][:, :], ACT.Tanh, scale=0.5,
                                         bias=colv("lru_bx", 8 * l + q)).then_inc(act_done, act_n("gate_read", l, q))
                    act.wait_ge(act_done, act_n.n - 1)
                    k = 8 * l + q
                    nc.scalar.activation(la[:, t, :], lr[:, t, :], ACT.Exp, scale=cln[:, k:k + 1],
                                         bias=cln[:, k:k + 1]).then_inc(act_done, act_n())
                    nc.scalar.activation(lr[:, t, :], lr[:, t, :], ACT.Tanh, scale=clp[:, k:k + 1],
                                         bias=clp[:, k:k + 1]).then_inc(act_done, act_n())
                    act.wait_ge(act_done, act_n.n - 1)
                    nc.scalar.activation(lm[:, t, :], la[:, t, :], ACT.Square).then_inc(act_done, act_n("a2", l, q))

                act.wait_ge(dve_done, at("clp"))
                for d in range(2):
                    for t in range(4):
                        gates(d, t)
                    if d == 0:
                        for t in range(2):
                            act.wait_ge(dve_done, at("conf_c", l, t))
                            nc.scalar.activation(sq[:, t, ts], y[:, t, ts], ACT.Square)\
                                .then_inc(act_done, act_n("conf_sq", l, t))
                    for t in range(4):
                        act.wait_ge(dve_done, at("m", l, 4 * d + t))
                        nc.scalar.activation(lm[:, t, :], lm[:, t, :], ACT.Sqrt, scale=0.25)\
                            .then_inc(act_done, act_n("mult", l, 4 * d + t))
                act.wait_ge(pe_done, at("conf_var", l))
                nc.scalar.activation(rs[:, ts], STAT[:, ts], ACT.Sqrt, bias=eps[:, :])\
                    .then_inc(act_done, act_n("conf_sd", l))
                for t in range(2):
                    act.wait_ge(dve_done, at("conf_n", l, t))
                    nc.scalar.activation(y[:, t, ts], y[:, t, ts], ACT.Silu, scale=colv("conf_ln_g", 2 * l + t),
                                         bias=colv("conf_ln_b", 2 * l + t)).then_inc(act_done, act_n("conf_y", l, t))

                def head_out(i8):
                    act.wait_ge(dve_done, at("y_n", l, i8))
                    nc.scalar.activation(h_hi[:, i8, ts], y[:, i8, ts], ACT.Copy, scale=colv("g_mix", 8 * l + i8))\
                        .then_inc(act_done, act_n("y_hi", l, i8))

                act.wait_ge(act_done, act_n.n)
                for i8 in range(KD):
                    act.wait_ge(dve_done, at("y", l, max(i8 - 4, 0)))
                    if i8 >= 2:
                        act.wait_ge(pe_done, at("head_ms", l, i8 - 2))
                    nc.scalar.activation(sq[:, i8 % 2, ts], y[:, i8, ts], ACT.Square)\
                        .then_inc(act_done, act_n("head_sq", l, i8))
                act.wait_ge(pe_done, at("head_ms", l, KD - 1))
                nc.scalar.activation(rs[0:HEADS, ts], STAT[0:HEADS, ts], ACT.Sqrt, bias=eps[0:HEADS, :])\
                    .then_inc(act_done, act_n("head_sd", l))
                for i8 in range(KD):
                    head_out(i8)
                for c in range(NWOUT):
                    s = ORD[("w_out", l, c)]
                    act.wait_ge(pe_done, at("mm", s))
                    hi(s + SPL)
                squares(l, 2, ts, ("w_out", l))
                if l == 1:
                    break
                h_high(l, 2, (0, 1), h_hi, "h_hi")
                for g in range(2):
                    for i11 in range(KG):
                        s = ORD[("up", g, i11)]
                        act.wait_ge(pe_done, at("mm", s))
                        hi(s + SPL)
                        if i11 >= 2:
                            act.wait_ge(dve_done, at("hid", g, i11 - 2))
                        nc.scalar.activation(tb[:, i11 % 2, :], bank[2 * (s % 3)][:, :], ACT.Silu)\
                            .then_inc(act_done, act_n("silu", g, i11))
                        act.wait_ge(dve_done, at("hid", g, i11))
                        nc.scalar.activation(f_hi[:, i11, :], sq[:, i11 % 2, :], ACT.Copy)\
                            .then_inc(act_done, act_n("f_hi", g, i11))
                    for d in range(KD):
                        s = ORD[("down", g, d)]
                        act.wait_ge(pe_done, at("mm", s))
                        hi(s + SPL)

            h_high(1, 2, (1,), hT, "h")
            for t in range(2):
                act.wait_ge(pe_done, at("ht", t))
                for half in range(2):
                    nc.scalar.activation(ht_hi[:, t, 512 * half:512 * half + 512], bank[2 * t + half][:, :], ACT.Copy)\
                        .then_inc(act_done, act_n("ht_hi", t, half))
            act.wait_ge(dve_done, at("gap"))
            nc.scalar.activation(pr[:, :, 1], pr[:, :, 0], ACT.Exp).then_inc(act_done, act_n("gap_exp"))

            Kp, Kd = at("per_expert", "pe"), at("per_expert", "dve")

            def expert(turn_no):
                pp, de, ein = turn_no * Kp, turn_no * Kd, [turn_no * e_level[s] for s in range(RAW)]

                def e_hi(j):
                    if j >= PER_EXPERT:
                        return
                    act.wait_ge(exp_in[j % RAW], e_arrived[j] + ein[j % RAW])
                    if j >= SPL:
                        act.wait_ge(pe_done, at("e_mm", j - SPL) + pp)
                    nc.scalar.activation(w_hi[:, j % SPL, :], raw[:, j % RAW, :], ACT.Copy)\
                        .then_inc(act_done, act_n("e_hi", j))

                for j in range(SPL):
                    e_hi(j)
                act.wait_ge(pe_done, at("e_gather", 0) + pp)
                for half in range(2):
                    i = nc.scalar.activation(hc_hi[:, 4 * half:4 * half + 4, :],
                                             bank[6 + half][:, :].rearrange("p (k c) -> p k c", c=CAP), ACT.Copy)
                    i.then_inc(act_done, act_n(*(("e_hc",) if half else ())))
                act.wait_ge(pe_done, at("e_turned") + pp)
                nc.scalar.activation(selT[:, :], bank[2][:, 0:NX], ACT.Copy)\
                    .then_inc(act_done, act_n("e_selT"))

                def hd_high(fc):
                    act.wait_ge(pe_done, at("e_turn", fc) + pp)
                    nc.scalar.activation(hd_hi[:, 2 * fc:2 * fc + 2, :],
                                         bank[2 + fc % 2][:, 0:256].rearrange("p (k c) -> p k c", c=CAP), ACT.Copy)\
                        .then_inc(act_done, act_n("e_hd_hi", fc))

                for j in range(UP):
                    fc = j // 2
                    act.wait_ge(pe_done, at("e_mm", j) + pp)
                    e_hi(j + SPL)
                    if j % 2:
                        if fc >= 2:
                            act.wait_ge(dve_done, at("e_hid", fc - 2) + de)
                        nc.scalar.activation(gs[:, fc % 2, :], bank[fc % 2][:, 0:256], ACT.Silu)\
                            .then_inc(act_done, act_n("e_silu", fc))
                        if fc >= 1:
                            hd_high(fc - 1)
                for j in range(UP, PER_EXPERT):
                    act.wait_ge(pe_done, at("e_mm", j) + pp)
                    e_hi(j + SPL)
                    if j == UP:
                        hd_high(DOWN - 1)
                act.wait_ge(dve_done, at("e_slot_w") + de)
                for half in range(2):
                    nc.scalar.activation(y_hi[:, 512 * half:512 * half + 512], bank[4 + half][:, :], ACT.Copy,
                                         scale=slot_w[:, :]).then_inc(act_done, act_n("e_y_hi", half))

            n0 = act_n.n
            with act.Fori(0, NE, 1) as e:
                expert(e)
            marks[("per_expert", "act")] = act_n.n - n0
            act_n.n, act_n.again = n0, True
            act.wait_ge(dve_done, at("again"))
            with act.Fori(0, MORE, 1) as r:
                left = act.value_load(again_i[0:1, 0, bass.ds(r, 1)], min_val=0, max_val=NE)
                with act.If(left > 0):
                    expert(r + NE)
                act.nop()
            act.wait_ge(fin_pe, at("fin_ms"))
            nc.scalar.activation(rs[:, 0:NX], STAT[:, 0:NX], ACT.Sqrt, bias=eps[:, :])\
                .then_inc(fin_act, fact_n("fin_sd"))
            for t in range(2):
                act.wait_ge(fin_pe, at("fin_turn", t))
                nc.scalar.activation(fo[:, t, 0:512], bank[2 * t][:, :], ACT.Copy)\
                    .then_inc(fin_act, fact_n("fin_o", t))

        @block.vector
        def _(dve):
            V = nc.vector

            def own(back=0):
                dve.wait_ge(dve_done, dve_n.n - back)

            def low(s):
                if s >= len(SPLIT):
                    return
                n = width(SPLIT[s])
                dve.wait_ge(act_done, at("hi", s))
                V.tensor_tensor(w_lo[:, s % SPL, 0:n], raw[:, POS[SPLIT[s]] % RAW, 0:n],
                                w_hi[:, s % SPL, 0:n].bitcast(F32), ALU.subtract).then_inc(dve_done, dve_n("lo", s))

            def normed(l, w, which, low_part):
                ts = slice(lo[l] if w == 2 else 0, T)
                dve.wait_ge(act_done, at("sd", l, w))
                V.reciprocal(rs[:, ts], rs[:, ts]).then_inc(dve_done, dve_n())

                def t_of(d):
                    if d >= 2:
                        dve.wait_ge(act_done, at("h_hi", l, w, d - 2) if low_part else at("h", d - 2))
                        if low_part:
                            dve.wait_ge(dve_done, at("h_lo", l, w, d - 2))
                    for s in which:
                        i = V.scalar_tensor_tensor(tb[:, d % 2, tok(s)], xT[:, d, tok(s)], amp[:, l, w - 1, d, s:s + 1],
                                                   rs[:, tok(s)], ALU.mult, ALU.mult)
                        i.then_inc(dve_done, dve_n(*(("t", l, w, d) if s == which[-1] else ())))

                def lo_of(d):
                    dve.wait_ge(act_done, at("h_hi", l, w, d))
                    for s in which:
                        shift = modT[:, l, 8 * (0 if w == 1 else 3) + d, s:s + 1]
                        i = V.scalar_tensor_tensor(h_lo[:, d, tok(s)], tb[:, d % 2, tok(s)], shift,
                                                   h_hi[:, d, tok(s)].bitcast(F32), ALU.add, ALU.subtract)
                        i.then_inc(dve_done, dve_n(*(("h_lo", l, w, d) if s == which[-1] else ())))
                own()
                t_of(0)
                for d in range(KD):
                    if d + 1 < KD:
                        t_of(d + 1)
                    if low_part:
                        lo_of(d)

            def modulated(l, j0, j1):
                for s in range(2):
                    V.tensor_tensor(modT[:, l, j0:j1, s], MOD[:, 96 * l + s + 2 * j0:96 * l + 2 * j1:2],
                                    colv("b_mod", 48 * l + j0, j1 - j0), ALU.add).then_inc(dve_done, dve_n())

            def amplitude(l, w):
                j = 8 * (1 if w == 1 else 4)
                own()
                for s in range(2):
                    V.scalar_tensor_tensor(amp[:, l, w - 1, :, s], modT[:, l, j:j + 8, s], 1.0,
                                           colv(f"g_norm{w}", 8 * l, 8), ALU.add, ALU.mult)\
                        .then_inc(dve_done, dve_n())

            dve.wait_ge(pe_done, at("tables"))
            for n, (_, rows) in enumerate(TABLES):
                i = V.tensor_copy(PT[:, P * n:P * n + rows], STAT[:, P * n:P * n + rows])
                i.then_inc(dve_done, dve_n(*(("PT",) if n == 3 else ())))
            own()
            lam = colv("lru_lam", 0, 16)
            V.tensor_scalar(lt[:, 1, :], lam, -1.0, None, ALU.mult).then_inc(dve_done, dve_n())
            own()
            V.tensor_tensor(lt[:, 0, :], lam, lt[:, 1, :], ALU.max).then_inc(dve_done, dve_n("lam_abs"))
            for name, n in (("conf_w", 124), ("lru_ba", 16), ("lru_bx", 16)):
                V.tensor_scalar(colv(name, 0, n), colv(name, 0, n), 0.5, None, ALU.mult).then_inc(dve_done, dve_n())
            for d in range(KD):
                dve.wait_ge(pe_done, at("xt", d))
                V.tensor_copy(xT[:, d, :], bank[d % 6][:, :]).then_inc(dve_done, dve_n("xT", "in", d))
            dve.wait_ge(act_done, at("lam_exp"))
            V.tensor_scalar(lt[:, 2, :], lt[:, 0, :], 2.0, None, ALU.add).then_inc(dve_done, dve_n())
            own()
            V.reciprocal(lt[:, 2, :], lt[:, 2, :]).then_inc(dve_done, dve_n())
            own()
            V.tensor_tensor(lt[:, 0, :], lt[:, 0, :], lt[:, 2, :], ALU.mult).then_inc(dve_done, dve_n())
            own()
            V.tensor_tensor(lt[:, 2, :], lt[:, 0, :], lt[:, 0, :], ALU.mult).then_inc(dve_done, dve_n())
            own()
            V.tensor_scalar(lt[:, 3, :], lt[:, 2, :], 1.0 / 15, 1.0 / 13, ALU.mult, ALU.add).then_inc(dve_done, dve_n())
            for k in (11, 9, 7, 5, 3, 1):
                own()
                V.tensor_tensor(lt[:, 3, :], lt[:, 3, :], lt[:, 2, :], ALU.mult).then_inc(dve_done, dve_n())
                own()
                V.tensor_scalar(lt[:, 3, :], lt[:, 3, :], 1.0 / k, None, ALU.add).then_inc(dve_done, dve_n())
            own()
            V.scalar_tensor_tensor(lt[:, 3, :], lt[:, 3, :], 2.0, lt[:, 0, :], ALU.mult, ALU.mult)\
                .then_inc(dve_done, dve_n())
            own()
            V.scalar_tensor_tensor(lt[:, 3, :], lt[:, 1, :], 0.0, lt[:, 3, :], ALU.max, ALU.add)\
                .then_inc(dve_done, dve_n())
            own()
            V.tensor_scalar(clp[:, :], lt[:, 3, :], 4.0, None, ALU.mult).then_inc(dve_done, dve_n())
            V.tensor_scalar(cln[:, :], lt[:, 3, :], -4.0, None, ALU.mult).then_inc(dve_done, dve_n("clp"))
            dve.wait_ge(pe_done, at("used", "mod", 0, 7))
            modulated(0, 0, 16)
            amplitude(0, 1)

            for l in range(2):
                ts = slice(lo[l], T)
                st = streams[l]
                if l == 1:
                    modulated(1, 0, 48)
                    amplitude(1, 1)
                    amplitude(1, 2)
                normed(l, 1, (0, 1), True)
                if l == 0:
                    for s in range(SPL):
                        low(s)

                def conf_taps(k0, k1):
                    for k in range(k0, k1):
                        for t in range(2):
                            w = colv("conf_w", 62 * l + 2 * k + t)
                            for s in st:
                                out_v, in_v = grid(y[:, t, tok(s)], s), padded_v(t, s, k)
                                own(2 * len(st) - 1)
                                if k == 0:
                                    i = V.tensor_scalar(out_v, in_v, w, colv("conf_b", 2 * l + t), ALU.mult, ALU.add)
                                else:
                                    i = V.scalar_tensor_tensor(out_v, in_v, w, out_v, ALU.mult, ALU.add)
                                i.then_inc(dve_done, dve_n(*(("conf_u", l) if (k, t, s) == (CONF_K - 1, 1, 1) else ())))

                for n, c in enumerate(WIN_ORDER):
                    s0 = ORD[("w_in", l, c)]
                    b = bank[2 * (s0 % 3):2 * (s0 % 3) + 2]
                    dve.wait_ge(pe_done, at("mm", s0))
                    low(s0 + SPL)
                    if c == 1:
                        dve.wait_ge(pool_done, at("padded", l))
                        dve.wait_ge(act_done, at("evac", s0))
                        for t in range(2):
                            for s in st:
                                V.scalar_tensor_tensor(padded_v(t, s, CONF_PAD) if s else vp[:, t, CONF_PAD:CONF_PAD + NC],
                                                       grid(sq[:, t, tok(s)], s), 1.0, grid(tb[:, t, tok(s)], s),
                                                       ALU.add, ALU.mult).then_inc(dve_done, dve_n())
                        own()
                        conf_taps(0, 8)
                    elif c == 4:
                        conf_taps(8, 16)
                    elif c == 3:
                        dve.wait_ge(act_done, at("evac", ORD[("w_in", l, 4)]))
                        for t in range(2):
                            for s in st:
                                V.tensor_tensor(padded_s(t, s, 1), b[t][:, tok(s)], sx[:, t, tok(s)], ALU.mult)\
                                    .then_inc(dve_done, dve_n(*(("evac", s0) if (t, s) == (1, 1) else ())))
                        conf_taps(16, 24)
                    elif c == 2:
                        conf_taps(24, CONF_K)
                    elif c == 5:
                        for k in range(SCONV_K):
                            for t in range(2):
                                w = colv("sconv_w", 6 * l + 2 * k + t)
                                for s in st:
                                    own(2 * len(st) - 1)
                                    if k == 0:
                                        i = V.tensor_scalar(sx[:, t, tok(s)], padded_s(t, s, k), w, None, ALU.mult)
                                    else:
                                        i = V.scalar_tensor_tensor(sx[:, t, tok(s)], padded_s(t, s, k), w,
                                                                   sx[:, t, tok(s)], ALU.mult, ALU.add)
                                    i.then_inc(dve_done, dve_n())
                        own()
                        dve.wait_ge(act_done, at("evac", ORD[("w_in", l, 2)]))
                        V.tensor_tensor(y[:, 2:4, ts], y[:, 2:4, ts], sx[:, :, ts], ALU.mult)\
                            .then_inc(dve_done, dve_n("sx_read", l))
                    elif c == 6:
                        dve.wait_ge(act_done, at("evac", s0))
                        for k in range(LRU_K):
                            for t in range(4):
                                w = colv("lru_conv_w", 16 * l + 4 * k + t)
                                out_v = xc[:, t, :].rearrange("p (s w) -> p s w", s=2)
                                own(3)
                                if k == 0:
                                    i = V.tensor_scalar(out_v, cxp[:, t, :, k:k + 256], w,
                                                        colv("lru_conv_b", 4 * l + t), ALU.mult, ALU.add)
                                else:
                                    i = V.scalar_tensor_tensor(out_v, cxp[:, t, :, k:k + 256], w, out_v,
                                                               ALU.mult, ALU.add)
                                i.then_inc(dve_done, dve_n(*(("xc", l, t) if k == LRU_K - 1 else ())))
                dve.wait_ge(pe_done, at("conf_mean", l))
                for t in range(2):
                    V.tensor_tensor(y[:, t, ts], y[:, t, ts], STAT[:, ts], ALU.subtract)\
                        .then_inc(dve_done, dve_n("conf_c", l, t))
                for d in range(2):
                    for t in range(4):
                        q = 4 * d + t
                        dve.wait_ge(act_done, at("a2", l, q))
                        V.scalar_tensor_tensor(lm[:, t, :], lm[:, t, :], 1.0, lr[:, t, :], ALU.add, ALU.mult)\
                            .then_inc(dve_done, dve_n())
                        V.scalar_tensor_tensor(li[:, t, :], li[:, t, :], 1.0, xc[:, t, :], ALU.add, ALU.mult)\
                            .then_inc(dve_done, dve_n())
                        own(1)
                        V.tensor_scalar(lm[:, t, :], lm[:, t, :], 0.0, None, ALU.max)\
                            .then_inc(dve_done, dve_n("m", l, q))
                    for t in range(4):
                        dve.wait_ge(act_done, at("mult", l, 4 * d + t))
                        V.tensor_tensor(li[:, t, :], lm[:, t, :], li[:, t, :], ALU.mult).then_inc(dve_done, dve_n())
                        own()
                        if d == 0:
                            V.tensor_tensor_scan(y[:, 4 + t, :], la[:, t, :], li[:, t, :], 0.0, ALU.mult, ALU.add)\
                                .then_inc(dve_done, dve_n("scan", l, 0, t))
                            continue
                        for s in range(2):
                            V.tensor_tensor_scan(lr[:, t, tok(s)][:, ::-1], la[:, t, tok(s)][:, ::-1],
                                                 li[:, t, tok(s)][:, ::-1], lr[:, t, 0:1] if s else 0.0,
                                                 ALU.mult, ALU.add).then_inc(dve_done, dve_n())
                            own()
                        V.tensor_tensor(y[:, 4 + t, ts], y[:, 4 + t, ts], lr[:, t, ts], ALU.add)\
                            .then_inc(dve_done, dve_n())
                        own()
                        g_v = cxp[:, t, lo[l] // NC:2, 2:2 + 256]
                        y_v = y[:, 4 + t, ts].rearrange("p (s w) -> p s w", w=256)
                        if t == 0:
                            dve.wait_ge(act_done, at("evac", ORD[("w_in", l, 8)]))
                        V.tensor_tensor(y_v, y_v, g_v, ALU.mult)\
                            .then_inc(dve_done, dve_n("y", l, t))
                dve.wait_ge(act_done, at("conf_sd", l))
                V.reciprocal(rs[:, ts], rs[:, ts]).then_inc(dve_done, dve_n())
                own()
                for t in range(2):
                    V.tensor_tensor(y[:, t, ts], y[:, t, ts], rs[:, ts], ALU.mult)\
                        .then_inc(dve_done, dve_n("conf_n", l, t))
                if l == 0:
                    dve.wait_ge(pe_done, at("used", "mod", 0, 23))
                    modulated(0, 16, 48)
                    amplitude(0, 2)
                dve.wait_ge(act_done, at("head_sd", l))
                V.reciprocal(rs[0:HEADS, ts], rs[0:HEADS, ts]).then_inc(dve_done, dve_n("head_r", l))
                for i8 in range(KD):
                    dve.wait_ge(pe_done, at("head_f", l, i8))
                    V.tensor_tensor(y[:, i8, ts], y[:, i8, ts], bank[2 + i8 % 4][:, ts], ALU.mult)\
                        .then_inc(dve_done, dve_n("y_n", l, i8))
                    if i8 >= 1:
                        y_low(i8 - 1, l, ts, dve, V)
                y_low(KD - 1, l, ts, dve, V)
                for c in range(NWOUT):
                    s0 = ORD[("w_out", l, c)]
                    dve.wait_ge(pe_done, at("mm", s0))
                    low(s0 + SPL)
                    for t in range(2):
                        d = 2 * c + t
                        for s in st:
                            i = V.scalar_tensor_tensor(xT[:, d, tok(s)], bank[2 * (s0 % 3) + t][:, tok(s)],
                                                       modT[:, l, 16 + d, s:s + 1], xT[:, d, tok(s)],
                                                       ALU.mult, ALU.add)
                            i.then_inc(dve_done, dve_n(*(("xT", "w_out", l, d) if s == 1 else ())))
                own()
                if l == 1:
                    break
                normed(0, 2, (0, 1), True)
                for g in range(2):
                    for i11 in range(KG):
                        s0 = ORD[("up", g, i11)]
                        dve.wait_ge(pe_done, at("mm", s0))
                        low(s0 + SPL)
                        dve.wait_ge(act_done, at("silu", g, i11))
                        if i11 >= 2:
                            dve.wait_ge(dve_done, at("f_lo", g, i11 - 2))
                        V.tensor_tensor(sq[:, i11 % 2, :], tb[:, i11 % 2, :], bank[2 * (s0 % 3) + 1][:, :], ALU.mult)\
                            .then_inc(dve_done, dve_n("hid", g, i11))
                        dve.wait_ge(act_done, at("f_hi", g, i11))
                        V.tensor_tensor(f_lo[:, i11, :], sq[:, i11 % 2, :], f_hi[:, i11, :].bitcast(F32),
                                        ALU.subtract).then_inc(dve_done, dve_n("f_lo", g, i11))
                    for d in range(KD):
                        s0 = ORD[("down", g, d)]
                        dve.wait_ge(pe_done, at("mm", s0))
                        low(s0 + SPL)
                        for s in range(2):
                            i = V.scalar_tensor_tensor(xT[:, d, tok(s)], bank[2 * (s0 % 3)][:, tok(s)],
                                                       modT[:, 0, 40 + d, s:s + 1], xT[:, d, tok(s)],
                                                       ALU.mult, ALU.add)
                            i.then_inc(dve_done, dve_n(*(("xT", "down", g, d) if s == 1 else ())))
                own()

            normed(1, 2, (1,), False)
            dve.wait_ge(pe_done, at("logits"))
            V.tensor_copy(lg[:, :, :], MOD[:, LOGIT:LOGIT + 2 * NE].rearrange("p (t e) -> p t e", t=2))\
                .then_inc(dve_done, dve_n())
            own()
            for t in range(2):
                V.max(top[:, t, :], lg[:, t, :]).then_inc(dve_done, dve_n())
            own()
            for t in range(2):
                V.max_index(topi[:, t, :], top[:, t, :], lg[:, t, :]).then_inc(dve_done, dve_n())
            V.tensor_tensor(pr[:, :, 0], top[:, :, 1], top[:, :, 0], ALU.subtract).then_inc(dve_done, dve_n("gap"))
            own(1)
            V.tensor_copy(topf[:, :, :], topi[:, :, :]).then_inc(dve_done, dve_n())
            own()
            for j in range(2):
                for t in range(2):
                    V.tensor_scalar(oh[:, j, t, :], iota_e[:, :], topf[:, t, j:j + 1], None, ALU.is_equal)\
                        .then_inc(dve_done, dve_n())
            own()
            V.tensor_tensor(mask[:, :, :], oh[:, 0, :, :], oh[:, 1, :, :], ALU.add).then_inc(dve_done, dve_n("mask"))
            dve.wait_ge(act_done, at("gap_exp"))
            V.tensor_scalar(pr[:, :, 2], pr[:, :, 1], 1.0, None, ALU.add).then_inc(dve_done, dve_n())
            own()
            V.reciprocal(pr[:, :, 2], pr[:, :, 2]).then_inc(dve_done, dve_n())
            own()
            V.tensor_tensor(pr[:, :, 3], pr[:, :, 1], pr[:, :, 2], ALU.mult).then_inc(dve_done, dve_n())
            own()
            for t in range(2):
                V.tensor_scalar(comb[:, t, :], oh[:, 0, t, :], pr[:, t, 2:3], None, ALU.mult).then_inc(dve_done, dve_n())
            own()
            for t in range(2):
                V.scalar_tensor_tensor(comb[:, t, :], oh[:, 1, t, :], pr[:, t, 3:4], comb[:, t, :],
                                       ALU.mult, ALU.add).then_inc(dve_done, dve_n())
            dve.wait_ge(pe_done, at("rank"))
            V.scalar_tensor_tensor(pos[:, :, :], MOD[:, RANK:RANK + 2 * NE].rearrange("p (t e) -> p t e", t=2), 1.0,
                                   mask[:, :, :], ALU.add, ALU.mult).then_inc(dve_done, dve_n())
            own()
            V.tensor_scalar(pos[:, :, :], pos[:, :, :], -1.0, None, ALU.add).then_inc(dve_done, dve_n())
            V.tensor_scalar(rev[:, :], iota_e[:, :], -1.0, float(NE), ALU.mult, ALU.add).then_inc(dve_done, dve_n())
            own()
            V.scalar_tensor_tensor(full[:, :], MOD[:, RANK + 2 * NE:RANK + 3 * NE], float(CAP), rev[:, :],
                                   ALU.is_gt, ALU.mult).then_inc(dve_done, dve_n())
            own()
            V.max(again[:, 0, :], full[:, :]).then_inc(dve_done, dve_n())
            own()
            V.tensor_scalar(again[:, 1, :], again[:, 0, :], -1.0, float(NE), ALU.mult, ALU.add)\
                .then_inc(dve_done, dve_n())
            own()
            V.tensor_scalar(again[:, 1, :], again[:, 1, :], float(NE - 1), None, ALU.min).then_inc(dve_done, dve_n())
            own()
            V.tensor_copy(again_i[:, :, :], again[:, :, :]).then_inc(dve_done, dve_n("again"))
            for t in range(2):
                for half in range(2):
                    cols = slice(512 * half, 512 * half + 512)
                    dve.wait_ge(act_done, at("ht_hi", t, half))
                    V.tensor_tensor(ht_lo[:, t, cols], bank[2 * t + half][:, :], ht_hi[:, t, cols].bitcast(F32),
                                    ALU.subtract).then_inc(dve_done, dve_n())

            Kp, Ka, Kd = (at("per_expert", x) for x in ("pe", "act", "dve"))

            def expert(e, slot0, turn_no):
                pp, ae, de = turn_no * Kp, turn_no * Ka, turn_no * Kd

                def own_e():
                    dve.wait_ge(dve_done, dve_n.n + de)

                def e_low(j):
                    if j >= PER_EXPERT:
                        return
                    dve.wait_ge(act_done, at("e_hi", j) + ae)
                    V.tensor_tensor(w_lo[:, j % SPL, :], raw[:, j % RAW, :], w_hi[:, j % SPL, :].bitcast(F32),
                                    ALU.subtract).then_inc(dve_done, dve_n("e_lo", j))

                own_e()
                V.tensor_scalar(pos1[:, :, :], pos[:, :, bass.ds(e, 1)], -float(slot0), None,
                                ALU.add).then_inc(dve_done, dve_n())
                V.tensor_copy(cw1[:, :, :], comb[:, :, bass.ds(e, 1)]).then_inc(dve_done, dve_n())
                own_e()
                for t in range(2):
                    V.tensor_scalar(sel[:, t, :], iota_s[:, :], pos1[:, t, :], None, ALU.is_equal)\
                        .then_inc(dve_done, dve_n(*(("e_sel",) if t else ())))
                for j in range(SPL):
                    e_low(j)
                dve.wait_ge(pe_done, at("e_gather", 1) + pp)
                for half in range(2):
                    V.tensor_copy(hc_lo[:, 4 * half:4 * half + 4, :],
                                  bank[4 + half][:, :].rearrange("p (k c) -> p k c", c=CAP))\
                        .then_inc(dve_done, dve_n(*(("e_hc_lo",) if half else ())))
                dve.wait_ge(pe_done, at("e_turned") + pp)
                V.tensor_copy(slot_w[:, :], bank[3][:, 256:257]).then_inc(dve_done, dve_n("e_slot_w"))

                def hd_low(fc):
                    dve.wait_ge(act_done, at("e_hd_hi", fc) + ae)
                    V.tensor_tensor(hd_lo[:, 2 * fc:2 * fc + 2, :],
                                    bank[2 + fc % 2][:, 0:256].rearrange("p (k c) -> p k c", c=CAP),
                                    hd_hi[:, 2 * fc:2 * fc + 2, :].bitcast(F32), ALU.subtract)\
                        .then_inc(dve_done, dve_n("e_hd", fc))

                for j in range(UP):
                    fc = j // 2
                    dve.wait_ge(pe_done, at("e_mm", j) + pp)
                    e_low(j + SPL)
                    if j % 2:
                        dve.wait_ge(act_done, at("e_silu", fc) + ae)
                        V.tensor_tensor(hid[:, 256 * fc:256 * fc + 256], gs[:, fc % 2, :], bank[fc % 2][:, 256:512],
                                        ALU.mult).then_inc(dve_done, dve_n("e_hid", fc))
                        if fc >= 1:
                            hd_low(fc - 1)
                for j in range(UP, PER_EXPERT):
                    dve.wait_ge(pe_done, at("e_mm", j) + pp)
                    e_low(j + SPL)
                    if j == UP:
                        hd_low(DOWN - 1)
                for half in range(2):
                    cols = slice(512 * half, 512 * half + 512)
                    dve.wait_ge(act_done, at("e_y_hi", half) + ae)
                    V.scalar_tensor_tensor(y_lo[:, cols], bank[4 + half][:, :], slot_w[:, :],
                                           y_hi[:, cols].bitcast(F32), ALU.mult, ALU.subtract)\
                        .then_inc(dve_done, dve_n(*(("e_y",) if half else ())))
                for d in range(KD):
                    dve.wait_ge(pe_done, at("e_back", d | 1) + pp)
                    V.scalar_tensor_tensor(xT[:, d, NC:T], bank[6 + d // 2 % 2][:, 256 * (d % 2):256 * (d % 2) + 256],
                                           modT[:, 1, 40 + d, 1:2], xT[:, d, NC:T], ALU.mult, ALU.add)\
                        .then_inc(dve_done, dve_n("e_add", d))
                own_e()
                V.memset(slot_w[:, :], 0.0).then_inc(dve_done, dve_n())

            n0 = dve_n.n
            with dve.Fori(0, NE, 1) as e:
                expert(e, 0, e)
            K = dve_n.n - n0
            marks[("per_expert", "dve")] = K
            dve.wait_ge(dve_done, n0 + NE * K)
            dve_n.n, dve_n.again = n0, True
            with dve.Fori(0, MORE, 1) as r:
                e = dve.value_load(again_i[0:1, 1, bass.ds(r, 1)], min_val=0, max_val=NE - 1)
                left = dve.value_load(again_i[0:1, 0, bass.ds(r, 1)], min_val=0, max_val=NE)
                with dve.If(left > 0):
                    expert(e, CAP, r + NE)
                dve.nop()
            for d in range(KD):
                V.tensor_tensor(fq[:, d, :], xT[:, d, NC:T], xT[:, d, NC:T], ALU.mult)\
                    .then_inc(fin_dve, fdve_n("fin_sq", d))
            dve.wait_ge(fin_act, at("fin_sd"))
            V.reciprocal(rs[:, 0:NX], rs[:, 0:NX]).then_inc(fin_dve, fdve_n())
            dve.wait_ge(fin_dve, fdve_n.n)
            for d in range(KD):
                V.scalar_tensor_tensor(fy[:, d, :], xT[:, d, NC:T], colv("g_final", d), rs[:, 0:NX],
                                       ALU.mult, ALU.mult).then_inc(fin_dve, fdve_n("fin_y", d))
            for t in range(2):
                dve.wait_ge(fin_act, at("fin_o", t))
                V.tensor_copy(fo[:, t, 512:D], bank[2 * t + 1][:, :])\
                    .then_inc(fin_dve, fdve_n(*(("fin_out",) if t else ())))


_INS = ["x", "c", "ctx", "c_ctx", "w_mod", "b_mod", "g_norm1", "g_norm2", "w_in", "conf_w", "conf_b", "conf_ln_g",
        "conf_ln_b", "sconv_w", "lru_conv_w", "lru_conv_b", "lru_wa", "lru_ba", "lru_wx", "lru_bx", "lru_lam",
        "g_mix", "w_out", "ffn_w1", "ffn_w3", "ffn_w2", "router_w", "router_b", "moe_w1", "moe_w3", "moe_w2",
        "g_final"]


def build(nc, shapes, known):
    aps = {n: nc.dram_tensor(f"in_{n}", shape, F32, kind="ExternalInput").ap() for n, shape in shapes.items()}
    out = nc.dram_tensor("out_0", (1, NX, D), F32, kind="ExternalOutput").ap()
    marks = {}
    program(nc, aps, out, known, marks)
    return marks


def kernel(**inputs):
    import numpy as np
    import concourse.bacc as bacc
    from concourse.bass_utils import run_bass_kernel_spmd

    arrays = {f"in_{n}": np.ascontiguousarray(inputs[n]) for n in _INS}
    shapes = {n: inputs[n].shape for n in _INS}
    marks = build(bacc.Bacc("TRN2", target_bir_lowering=False, num_devices=1), shapes, None)
    nc = bacc.Bacc("TRN2", target_bir_lowering=False, num_devices=1)
    build(nc, shapes, marks)
    r = run_bass_kernel_spmd(nc, [arrays], core_ids=[0])
    return r.results[0]["out_0"]
```

```python
import concourse.bass as bass
from concourse import mybir
from contextlib import ExitStack

F32 = mybir.dt.float32
F32R = mybir.dt.float32r
I32 = mybir.dt.int32
U32 = mybir.dt.uint32
ALU = mybir.AluOpType
ACT = mybir.ActivationFunctionType
AXX = mybir.AxisListType.X

P = 128
D = 1024
KD = D // P
NC = 256
NX = 256
T = NC + NX
GRID = 64
ROWS = NX // GRID
DFF = 2816
KF = DFF // P
KG = KF // 2
NE = 8
CAP = 128
MORE = 3
TURNS = NE + MORE + 1
HEADS = D // 64
EPS = 1e-6
CONF_K, SCONV_K, LRU_K = 31, 3, 4
CONF_PAD = CONF_K // 2
CW = 2048
RAW = 5
SPL = 3
WIN_ORDER = [0, 1, 4, 3, 2, 5, 6, 7, 8]
NWIN, NWOUT = 9, 4
UP, DOWN = 2 * KF // 2, KF // 2
PER_EXPERT = UP + DOWN
NORM1, FIRST = 8, 13
IN_FFN = 11
MOD_AT = [{0: [13], 1: [14], 2: [15], 3: [16, 17], 4: [18, 19], 5: [20, 21], 6: [22], 7: [23]},
          {-1: [11, 12, 13, 14], 3: [15], 6: [16, 17], 7: [18, 19], 8: [20, 21, 22, 23]}]
E_SLOT = [s for n in (5, 5, 4, 5, 5, 4, 5) for s in range(n)]
assert len(E_SLOT) == PER_EXPERT and max(E_SLOT) < RAW
GATHER = UP + 2

COL = {}


def table(parts):
    row, out = 0, []
    for name, rows in parts:
        COL[name] = row
        out.append((name, row, rows))
        row += rows
    return out, row


TABLES = []
for _n, _parts in enumerate([
    [("c", 8), ("c_ctx", 8), ("g_norm1", 16), ("g_norm2", 16), ("g_final", 8), ("g_mix", 16),
     ("sconv_w", 12), ("lru_conv_w", 32)],
    [("conf_b", 4), ("conf_ln_g", 4), ("conf_ln_b", 4), ("lru_conv_b", 8), ("lru_ba", 16), ("lru_bx", 16),
     ("lru_lam", 16)],
    [("conf_w", 124)],
    [("b_mod", 96)],
]):
    _t, _rows = table(_parts)
    for _name, _row, _k in _t:
        COL[_name] = 128 * _n + _row
    TABLES.append((_t, _rows))


class Count:

    def __init__(self, marks):
        self.n, self.marks, self.again = 0, marks, False

    def __call__(self, *name):
        self.n += 1
        if name and not self.again:
            assert name not in self.marks
            self.marks[name] = self.n
        return 1


def schedule():
    chunks = [("x", 0), ("x", 1)] + [("mod", 0, j) for j in range(NORM1)]
    chunks += [("w_in", 0, c) for c in WIN_ORDER[:SPL]] + [("mod", 0, j) for j in range(NORM1, FIRST)]
    for l in range(2):
        chunks += [("w_in", l, c) for c in WIN_ORDER[SPL if l == 0 else 0:]]
        chunks += [("w_out", l, c) for c in range(SPL)]
        chunks += [("mod", l, j) for j in range(IN_FFN if l else FIRST, 24)]
        chunks += [("w_out", l, c) for c in range(SPL, NWOUT)]
        if l == 0:
            mod = iter(range(IN_FFN))
            for g in range(2):
                for i in range(KG):
                    chunks.append(("up", g, i))
                    chunks += [("mod", 1, j) for j in [next(mod, None)] if j is not None]
                for d in range(KD):
                    chunks.append(("down", g, d))
                    chunks += [("mod", 1, j) for j in [next(mod, None)] if j is not None]
    return chunks


CHUNKS = schedule()
SPLIT = [c for c in CHUNKS if c[0] in ("w_in", "w_out", "up", "down")]
POS = {c: n for n, c in enumerate(CHUNKS)}
ORD = {c: n for n, c in enumerate(SPLIT)}


def width(c):
    return KG * P if c[0] == "down" else CW


def program(nc, a, out, known, marks):
    def at(*name):
        return known[name] if known else 1

    ctx = ExitStack()
    with ctx:
        def sem(name):
            return ctx.enter_context(nc.semaphore(name))

        cursor = [-(-nc.sbuf_base // 64) * 64]

        def sb(name, shape, dt=F32):
            size = 4
            for s in shape[1:]:
                size *= s
            t = nc.alloc_sbuf_tensor_at(name, shape, dt, offset=cursor[0])
            cursor[0] += -(-size // 32) * 32
            return t

        ident = sb("ident", [P, P])
        ones_d = sb("ones_d", [P, P])
        ones_c = sb("ones_c", [P, P])
        ones_h = sb("ones_h", [P, KD, HEADS])
        eps = sb("eps", [P, 1])
        PT = sb("PT", [P, 4 * P])
        cc = sb("cc", [P, KD, 2])
        modT = sb("modT", [P, 2, 48, 2])
        mrow = sb("mrow", [2, 2, 256])
        amp = sb("amp", [P, 2, 2, KD, 2])
        clp = sb("clp", [P, 16])
        cln = sb("cln", [P, 16])
        lt = sb("lt", [P, 4, 16])
        xT = sb("xT", [P, KD, T])
        raw = sb("raw", [P, RAW, CW])
        w_hi = sb("w_hi", [P, SPL, CW], F32R)
        w_lo = sb("w_lo", [P, SPL, CW], F32R)
        gates_at = cursor[0]
        G = sb("G", [P, 16, P])
        tb = sb("tb", [P, 2, T])
        sq = sb("sq", [P, 2, T])
        rs = sb("rs", [P, T])
        area = cursor[0]

        h_hi = sb("h_hi", [P, KD, T], F32R)
        h_lo = sb("h_lo", [P, KD, T], F32R)
        rest = cursor[0]
        cxp = sb("cxp", [P, 4, 2, 260])
        xc = sb("xc", [P, 4, T])
        vp = sb("vp", [P, 2, NC + 2 * CONF_PAD + ROWS * (GRID + 2 * CONF_PAD)])
        sx = sb("sx", [P, 2, T])
        spread = nc.alloc_sbuf_tensor_at("spread", [HEADS, KD, P], F32, offset=cursor[0] - 8 * T)
        sp_ = sb("sp_", [P, 2, NC + 2 + NX + 2 * GRID])
        y = sb("y", [P, KD, T])
        assert cursor[0] <= nc.sbuf_usable_end, cursor[0]
        cursor[0] = area
        lr = sb("lr", [P, 4, T])
        li = sb("li", [P, 4, T])
        la = sb("la", [P, 4, T])
        lm = sb("lm", [P, 4, T])
        cursor[0] = rest
        rows_sb = sb("rows_sb", [P, 4, P])
        cursor[0] = rest
        f_hi = sb("f_hi", [P, KG, T], F32R)
        f_lo = sb("f_lo", [P, KG, T], F32R)
        cursor[0] = area
        hT = sb("hT", [P, KD, NX])
        ht_hi = sb("ht_hi", [P, 2, D], F32R)
        ht_lo = sb("ht_lo", [P, 2, D], F32R)
        sel = sb("sel", [P, 2, CAP], F32R)
        selT = sb("selT", [P, NX], F32R)
        hc_hi = sb("hc_hi", [P, KD, CAP], F32R)
        hc_lo = sb("hc_lo", [P, KD, CAP], F32R)
        gs = sb("gs", [P, 2, 256])
        hid = sb("hid", [P, DFF])
        hd_hi = sb("hd_hi", [P, KF, CAP], F32R)
        hd_lo = sb("hd_lo", [P, KF, CAP], F32R)
        y_hi = sb("y_hi", [P, D], F32R)
        y_lo = sb("y_lo", [P, D], F32R)
        rw = sb("rw", [P, KD, NE])
        rb = sb("rb", [1, NE])
        iota_e = sb("iota_e", [P, NE])
        lg = sb("lg", [P, 2, NE])
        top = sb("top", [P, 2, 8])
        topi = sb("topi", [P, 2, 8], U32)
        topf = sb("topf", [P, 2, 8])
        pr = sb("pr", [P, 2, 4])
        oh = sb("oh", [P, 2, 2, NE])
        mask = sb("mask", [P, 2, NE])
        comb = sb("comb", [P, 2, TURNS])
        pos = sb("pos", [P, 2, TURNS])
        pos1 = sb("pos1", [P, 2, 1])
        cw1 = sb("cw1", [P, 2, 1])
        warm = sb("warm", [P, 1])
        slot_w = sb("slot_w", [P, 1])
        full = sb("full", [P, NE])
        rev = sb("rev", [P, NE])
        again = sb("again", [P, 2, 8])
        again_i = sb("again_i", [P, 2, 8], I32)
        assert cursor[0] <= nc.sbuf_usable_end, cursor[0]
        cursor[0] = gates_at
        one = sb("one", [1, P])
        before = sb("before", [P, P])
        all1 = sb("all1", [P, P])
        iota_s = sb("iota_s", [P, CAP])
        cursor[0] = area
        fq = sb("fq", [P, KD, NX])
        fy = sb("fy", [P, KD, NX])
        fo = sb("fo", [P, 2, D])

        bank = [ctx.enter_context(nc.psum_tensor(f"bank{i}", [P, 512], F32)) for i in range(8)]
        MOD, STAT = bank[6], bank[7]

        pe_done, act_done, dve_done, pool_done = sem("pe_done"), sem("act_done"), sem("dve_done"), sem("pool_done")
        table_in, gate_in, rout_in, stored = sem("table_in"), sem("gate_in"), sem("rout_in"), sem("stored")
        raw_in = [sem(f"raw_in{s}") for s in range(RAW)]
        exp_in = [sem(f"exp_in{s}") for s in range(RAW)]
        fin_dve, fin_act, fin_pe = sem("fin_dve"), sem("fin_act"), sem("fin_pe")

        arrived, level = {}, [0] * RAW
        for n, c in enumerate(CHUNKS):
            level[n % RAW] += 32 if c[0] == "up" else 16
            arrived[c] = level[n % RAW]
        e_arrived, e_level = [], [0] * RAW
        for j in range(PER_EXPERT):
            e_level[E_SLOT[j]] += 32 if j < UP else 16
            e_arrived.append(e_level[E_SLOT[j]])

        def free_name(c):
            if c[0] == "x":
                return ("xt", KD - 1)
            return ("lo", ORD[c]) if c in ORD else ("used",) + c

        def free_sem(c):
            return dve_done if c in ORD else pe_done

        lo = [0, NC]
        streams = [(0, 1), (1,)]

        def tok(s):
            return slice(s * NC, (s + 1) * NC)

        def colv(name, i, n=1):
            return PT[:, COL[name] + i:COL[name] + i + n]

        def vp_x(t, k):
            v = vp[:, t, NC + 2 * CONF_PAD:].rearrange("p (r w) -> p r w", r=ROWS)
            return v[:, :, k:k + GRID]

        def padded_v(t, s, k):
            return vp[:, t, k:k + NC] if s == 0 else vp_x(t, k)

        def padded_s(t, s, k):
            o = k if s == 0 else NC + 2 + GRID * k
            return sp_[:, t, o:o + 256]

        def grid(ap, s):
            return ap if s == 0 else ap.rearrange("p (r w) -> p r w", r=ROWS)

        def weights(c):
            l = c[1]
            if c[0] == "mod":
                return a["w_mod"][l].rearrange("(k p) c -> p k c", p=P)[:, :, 256 * c[2]:256 * c[2] + 256]
            if c[0] == "w_in":
                return a["w_in"][l].rearrange("(k p) c -> p k c", p=P)[:, :, 256 * c[2]:256 * c[2] + 256]
            if c[0] == "w_out":
                return a["w_out"][l].rearrange("(k p) c -> p k c", p=P)[:, :, 256 * c[2]:256 * c[2] + 256]
            if c[0] == "down":
                w = a["ffn_w2"][0].rearrange("(k p) c -> p k c", p=P)
                return w[:, KG * l:KG * l + KG, P * c[2]:P * c[2] + P]
            return (a["ctx"] if l == 0 else a["x"])[0].rearrange("(t p) c -> p t c", p=P)

        pe_n, act_n, dve_n, pool_n = (Count(marks) for _ in range(4))
        fpe_n, fact_n, fdve_n = (Count(marks) for _ in range(3))
        LOGIT, RANK = 256, 288

        def mod_rows(l, j):
            return bank[j % 6][0:2, 0:256] if l == 0 and j < FIRST else MOD[0:2, 256:512]

        def evacuated(c):
            if c[0] == "w_in" and c[2] != 3:
                return act_done, at("evac", ORD[c])
            if c[0] == "w_in":
                return dve_done, at("evac", ORD[c])
            if c[0] == "w_out":
                return dve_done, at("xT", "w_out", c[1], 2 * c[2] + 1)
            if c[0] == "up":
                return dve_done, at("hid", c[1], c[2])
            return dve_done, at("xT", "down", c[1], c[2])

        def y_low(i8, l, ts, dve, V):
            dve.wait_ge(act_done, at("y_hi", l, i8))
            V.scalar_tensor_tensor(h_lo[:, i8, ts], y[:, i8, ts], colv("g_mix", 8 * l + i8),
                                   h_hi[:, i8, ts].bitcast(F32), ALU.mult, ALU.subtract)\
                .then_inc(dve_done, dve_n("y_lo", l, i8))

        block = ctx.enter_context(nc.Block())

        @block.sync
        def _(sp):
            def load(c):
                n = POS[c]
                slot = raw[:, n % RAW, :]
                if n >= RAW:
                    sp.wait_ge(free_sem(CHUNKS[n - RAW]), at(*free_name(CHUNKS[n - RAW])))
                if c[0] == "up":
                    dst = slot.rearrange("p (k w c) -> p k w c", k=KD, w=2)
                    f = P * (KG * c[1] + c[2])
                    for w, name in enumerate(("ffn_w1", "ffn_w3")):
                        src = a[name][0].rearrange("(k p) c -> p k c", p=P)[:, :, f:f + P]
                        sp.dma_start(dst[:, :, w, :], src).then_inc(raw_in[n % RAW], 16)
                else:
                    k = {"x": 2, "down": KG}.get(c[0], KD)
                    dst = slot[:, 0:width(c)].rearrange("p (k c) -> p k c", k=k)
                    sp.dma_start(dst, weights(c)).then_inc(raw_in[n % RAW], 16)

            def gate_weights(l):
                for w, name in enumerate(("lru_wa", "lru_wx")):
                    for d in range(2):
                        src = a[name][l, d].rearrange("(t u) i j -> u i t j", u=2)
                        for u in range(2):
                            half = slice(64 * u, 64 * u + 64)
                            sp.dma_start(G[half, 8 * d + 4 * w:8 * d + 4 * w + 4, half], src[u])\
                              .then_inc(gate_in, 16)

            for n, (parts, _) in enumerate(TABLES):
                for name, row, rows in parts:
                    src = a[name]
                    dims = " ".join(f"a{i}" for i in range(len(src.shape)))
                    flat = src.rearrange(f"{dims} -> ({dims})") if len(src.shape) > 1 else src
                    sp.dma_start(rows_sb[row:row + rows, n, :], flat.rearrange("(r c) -> r c", c=P))\
                      .then_inc(table_in, 16)
            for c in CHUNKS[:2 + FIRST]:
                load(c)
            sp.wait_ge(pool_done, at("G_zero"))
            gate_weights(0)
            for c in CHUNKS[2 + FIRST:]:
                if c == ("up", 0, 0):
                    sp.wait_ge(pe_done, at("gate", 0, 7))
                    gate_weights(1)
                load(c)

            def expert_chunk(e, j):
                slot = raw[:, E_SLOT[j], :]
                if j < UP:
                    fc, half = j // 2, j % 2
                    dst = slot.rearrange("p (k w c) -> p k w c", k=4, w=2)
                    for w, name in enumerate(("moe_w1", "moe_w3")):
                        src = a[name][0].rearrange("e (k p) c -> (e k) p c", p=P)
                        src = src[bass.ds(e * KD + 4 * half, 4), :, 256 * fc:256 * fc + 256]
                        sp.dma_start(dst[:, :, w, :], src.rearrange("k p c -> p k c"))\
                          .then_inc(exp_in[E_SLOT[j]], 16)
                else:
                    src = a["moe_w2"][0].rearrange("e (k p) c -> (e k) p c", p=P)
                    src = src[bass.ds(e * KF + 2 * (j - UP), 2), :, :]
                    sp.dma_start(slot.rearrange("p (k c) -> p k c", k=2), src.rearrange("k p c -> p k c"))\
                      .then_inc(exp_in[E_SLOT[j]], 16)

            K = at("per_expert", "dve")
            last = {E_SLOT[j]: j for j in range(PER_EXPERT)}

            def slot_free(j, shift):
                before = max([i for i in range(j) if E_SLOT[i] == E_SLOT[j]], default=None)
                if before is None:
                    sp.wait_ge(dve_done, at("e_lo", last[E_SLOT[j]]) - K + shift)
                elif before < SPL:
                    sp.wait_ge(dve_done, at("next_lo", before) - K + shift)
                else:
                    sp.wait_ge(dve_done, at("e_lo", before) + shift)

            def chunks(e, j0, j1, shift):
                for j in range(j0, j1):
                    slot_free(j, shift)
                    expert_chunk(e, j)

            for c in CHUNKS[-RAW:]:
                sp.wait_ge(free_sem(c), at(*free_name(c)))
            sp.wait_ge(pe_done, at("mm", ORD[("w_out", 1, NWOUT - 1)]))
            sp.dma_start(rw[:, :, :], a["router_w"][0].rearrange("(k p) e -> p k e", p=P)).then_inc(rout_in, 16)
            sp.dma_start(rb[:, :], a["router_b"]).then_inc(rout_in, 16)
            for j in range(RAW):
                expert_chunk(0, j)
            sp.wait_ge(dve_done, at("first_lo", SPL - 1))
            with sp.Fori(0, NE - 1, 1) as e:
                chunks(e, RAW, PER_EXPERT, e * K)
                chunks(e + 1, 0, RAW, (e + 1) * K)
            chunks(NE - 1, RAW, PER_EXPERT, (NE - 1) * K)
            sp.wait_ge(dve_done, at("again"))
            e = sp.value_load(again_i[0:1, 1, 0:1], min_val=0, max_val=NE - 1)
            chunks(e, 0, SPL, NE * K)
            with sp.Fori(0, MORE, 1) as r:
                e = sp.value_load(again_i[0:1, 1, bass.ds(r, 1)], min_val=0, max_val=NE - 1)
                after = sp.value_load(again_i[0:1, 1, bass.ds(r + 1, 1)], min_val=0, max_val=NE - 1)
                left = sp.value_load(again_i[0:1, 0, bass.ds(r, 1)], min_val=0, max_val=NE)
                with sp.If(left > 0):
                    chunks(e, SPL, PER_EXPERT, (NE + r) * K)
                    chunks(after, 0, SPL, (NE + 1 + r) * K)
                sp.nop()
            sp.wait_ge(fin_dve, at("fin_out"))
            sp.dma_start(out[0].rearrange("(t p) c -> p t c", p=P), fo[:, :, :]).then_inc(stored, 16)
            sp.wait_ge(stored, 16)

        @block.gpsimd
        def _(pool):
            def own():
                if pool_n.n:
                    pool.wait_ge(pool_done, pool_n.n)

            for m, v in ((ident, 0.0), (ones_d, 1.0 / D), (ones_c, 1.0 / 256), (eps, EPS)):
                own()
                nc.gpsimd.memset(m[:, :], v).then_inc(pool_done, pool_n())
            own()
            nc.gpsimd.affine_select(out=ident[:, :], in_=ident[:, :], compare_op=ALU.not_equal, fill=1.0, base=0,
                                    pattern=[[-1, P]], channel_multiplier=1).then_inc(pool_done, pool_n("ident"))
            own()
            nc.gpsimd.memset(ones_h[:, :, :], 0.0).then_inc(pool_done, pool_n())
            flat = ones_h[:, :, :].rearrange("p k h -> p (k h)")
            for h in range(2):
                own()
                nc.gpsimd.memset(flat[64 * h:64 * h + 64, h:h + (HEADS + 2) * (KD - 1) + 1:HEADS + 2], 1.0 / 64)\
                    .then_inc(pool_done, pool_n())
            own()
            nc.gpsimd.memset(G[:, :, :], 0.0).then_inc(pool_done, pool_n("G_zero"))
            for l in range(2):
                pool.wait_ge(pe_done, at("tables") if l == 0 else at("mm", ORD[("down", 1, KD - 1)]))
                own()
                nc.gpsimd.memset(vp[:, :, :], 0.0).then_inc(pool_done, pool_n())
                own()
                nc.gpsimd.memset(sp_[:, :, :], 0.0).then_inc(pool_done, pool_n())
                own()
                nc.gpsimd.memset(cxp[:, :, :, :], 0.0).then_inc(pool_done, pool_n("padded", l))
                pool.wait_ge(dve_done, at("sx_read", l))
                own()
                nc.gpsimd.memset(spread[:, :, :], 0.0).then_inc(pool_done, pool_n())
                own()
                view = spread[:, :, :].rearrange("q k (h c) -> q k h c", h=2)
                nc.gpsimd.affine_select(out=view, in_=view, compare_op=ALU.not_equal, fill=1.0, base=0,
                                        pattern=[[-2, KD], [-1, 2], [0, 64]], channel_multiplier=1)\
                    .then_inc(pool_done, pool_n("spread", l))

            pool.wait_ge(pe_done, at("mm", ORD[("w_out", 1, NWOUT - 1)]))
            own()
            nc.gpsimd.memset(one[:, :], 1.0).then_inc(pool_done, pool_n())
            own()
            nc.gpsimd.memset(all1[:, :], 1.0).then_inc(pool_done, pool_n())
            own()
            nc.gpsimd.memset(before[:, :], 1.0).then_inc(pool_done, pool_n())
            own()
            nc.gpsimd.iota(iota_s[:, :], pattern=[[1, CAP]], base=0, channel_multiplier=0,
                           allow_small_or_imprecise_dtypes=True).then_inc(pool_done, pool_n())
            own()
            nc.gpsimd.iota(iota_e[:, :], pattern=[[1, NE]], base=0, channel_multiplier=0,
                           allow_small_or_imprecise_dtypes=True).then_inc(pool_done, pool_n())
            own()
            nc.gpsimd.affine_select(out=before[:, :], in_=before[:, :], compare_op=ALU.is_gt, fill=0.0, base=0,
                                    pattern=[[1, P]], channel_multiplier=-1).then_inc(pool_done, pool_n("routing"))

        @block.tensor
        def _(pe):
            def mm(dst, lhsT, rhs, first, last):
                return nc.tensor.matmul(dst, lhsT, rhs, start=first, stop=last)

            def split_mm(dst, w, x, first, last):
                mm(dst, w[0], x[0], first, False)
                mm(dst, w[0], x[1], False, False)
                return mm(dst, w[1], x[0], False, last)

            pe.wait_ge(table_in, 16 * sum(len(parts) for parts, _ in TABLES))
            pe.wait_ge(pool_done, at("ident"))
            for n, (_, rows) in enumerate(TABLES):
                i = nc.tensor.transpose(STAT[:, P * n:P * n + rows], rows_sb[0:rows, n, :], ident[0:rows, 0:rows])
            i.then_inc(pe_done, pe_n("tables"))
            for s in range(2):
                pe.wait_ge(raw_in[s], 16)
            for d in range(KD):
                if d >= 6:
                    pe.wait_ge(dve_done, at("xT", "in", d - 6))
                for s in range(2):
                    for t in range(2):
                        i = nc.tensor.transpose(bank[d % 6][:, P * (2 * s + t):P * (2 * s + t) + P],
                                                raw[:, s, D * t + P * d:D * t + P * d + P], ident[:, :])
                i.then_inc(pe_done, pe_n("xt", d))

            rows_left = []

            def columns():
                if rows_left:
                    l, j = rows_left.pop()
                    pe.wait_ge(dve_done, at("mod_row", l, j))
                    for t in range(2):
                        o = 96 * l + 2 * (2 * j + t)
                        i = nc.tensor.transpose(MOD[:, o:o + 2], mrow[:, j % 2, P * t:P * t + P], ident[0:2, 0:2])
                    i.then_inc(pe_done, pe_n("mod_col", l, j))

            def modulation(l, j):
                c = ("mod", l, j)
                slot = POS[c] % RAW
                at_start = l == 0 and j < FIRST
                if not at_start or j == NORM1:
                    columns()
                if j == 0 and l == 0:
                    pe.wait_ge(act_done, at("cc"))
                    pe.wait_ge(dve_done, at("xT", "in", KD - 1))
                pe.wait_ge(raw_in[slot], arrived[c])
                for k in range(KD):
                    i = mm(mod_rows(l, j), cc[:, k, :], raw[:, slot, 256 * k:256 * k + 256], k == 0, k == KD - 1)
                i.then_inc(pe_done, pe_n("used", *c))
                if at_start:
                    columns()
                rows_left.append((l, j))

            def mean_square(l, w, ts, previous):
                previous()
                for d in range(KD):
                    pe.wait_ge(act_done, at("sq", l, w, d))
                    mm(STAT[:, ts], ones_d[:, :], sq[:, d % 2, ts], d == 0, d == KD - 1)\
                        .then_inc(pe_done, pe_n("ms", l, w, d))

            def take(c):
                s = ORD[c]
                pe.wait_ge(dve_done, at("lo", s))
                if s >= 3:
                    pe.wait_ge(*evacuated(SPLIT[s - 3]))
                return (w_hi[:, s % SPL, :], w_lo[:, s % SPL, :]), bank[2 * (s % 3):2 * (s % 3) + 2]

            def project(c, ts, ready):
                w, banks = take(c)
                for k in range(KD):
                    if ready:
                        pe.wait_ge(dve_done, at(*ready, k))
                    for t in range(2):
                        o = 256 * k + P * t
                        i = split_mm(banks[t][:, ts], (w[0][:, o:o + P], w[1][:, o:o + P]),
                                     (h_hi[:, k, ts], h_lo[:, k, ts]), k == 0, k == KD - 1)
                i.then_inc(pe_done, pe_n("mm", ORD[c]))

            for l in range(2):
                ts = slice(lo[l], T)
                mean_square(l, 1, slice(0, T), lambda: pe.wait_ge(dve_done, at("PT")) if l == 0 else
                            pe.wait_ge(act_done, at("sd", 0, 2)))
                if l == 0:
                    for j in range(FIRST):
                        modulation(0, j)
                columns()
                for n, c in enumerate(WIN_ORDER):
                    project(("w_in", l, c), slice(0, T) if c in (5, 6) else ts, ("h_lo", l, 1) if n == 0 else None)
                for j in MOD_AT[l].get(-1, []):
                    modulation(l, j)
                pe.wait_ge(gate_in, 8 * 16 * (l + 1))
                for q in range(8):
                    d, t = q // 4, q % 4
                    if q < 4:
                        pe.wait_ge(dve_done, at("xc", l, t))
                    if q < 3:
                        pe.wait_ge(*evacuated(("w_in", l, WIN_ORDER[6 + q])))
                    else:
                        pe.wait_ge(act_done, at("gate_read", l, q - 3))
                    for w in range(2):
                        i = mm(bank[2 * (q % 3) + w][:, :], G[:, 8 * d + 4 * w + t, :], xc[:, t, :], True, True)
                    i.then_inc(pe_done, pe_n("gate", l, q))
                    if q == 3:
                        pe.wait_ge(dve_done, at("conf_u", l))
                        for v in range(2):
                            i = mm(STAT[:, ts], ones_c[:, :], y[:, v, ts], v == 0, v == 1)
                        i.then_inc(pe_done, pe_n("conf_mean", l))
                    if q == 5:
                        pe.wait_ge(dve_done, at("conf_c", l, 1))
                        for v in range(2):
                            pe.wait_ge(act_done, at("conf_sq", l, v))
                            i = mm(STAT[:, ts], ones_c[:, :], sq[:, v, ts], v == 0, v == 1)
                        i.then_inc(pe_done, pe_n("conf_var", l))
                    for j in MOD_AT[l].get(q, []):
                        modulation(l, j)
                for j in MOD_AT[l].get(8, []):
                    modulation(l, j)
                columns()
                for i8 in range(KD):
                    pe.wait_ge(act_done, at("head_sq", l, i8))
                    if i8 == 0:
                        pe.wait_ge(act_done, at("conf_sd", l))
                    mm(STAT[0:HEADS, ts], ones_h[:, i8, :], sq[:, i8 % 2, ts], i8 == 0, i8 == KD - 1)\
                        .then_inc(pe_done, pe_n("head_ms", l, i8))
                pe.wait_ge(dve_done, at("head_r", l))
                pe.wait_ge(act_done, at("gate_read", l, 7))
                pe.wait_ge(pool_done, at("spread", l))
                for i8 in range(KD):
                    if i8 >= 4:
                        pe.wait_ge(dve_done, at("y_n", l, i8 - 4))
                    mm(bank[2 + i8 % 4][:, ts], spread[:, i8, :], rs[0:HEADS, ts], True, True)\
                        .then_inc(pe_done, pe_n("head_f", l, i8))
                for c in range(NWOUT):
                    project(("w_out", l, c), ts, ("y_lo", l) if c == 0 else None)
                mean_square(l, 2, ts, lambda: pe.wait_ge(act_done, at("head_sd", l)))
                if l == 1:
                    break
                mod = iter(range(IN_FFN))
                for g in range(2):
                    for i11 in range(KG):
                        c = ("up", g, i11)
                        w, banks = take(c)
                        for k in range(KD):
                            if g == 0 and i11 == 0:
                                pe.wait_ge(dve_done, at("h_lo", 0, 2, k))
                            for v in range(2):
                                o = 256 * k + P * v
                                i = split_mm(banks[v][:, :], (w[0][:, o:o + P], w[1][:, o:o + P]),
                                             (h_hi[:, k, :], h_lo[:, k, :]), k == 0, k == KD - 1)
                        i.then_inc(pe_done, pe_n("mm", ORD[c]))
                        j = next(mod, None)
                        if j is None:
                            columns()
                        else:
                            modulation(1, j)
                    for d in range(KD):
                        c = ("down", g, d)
                        w, banks = take(c)
                        for k in range(KG):
                            if d == 0:
                                pe.wait_ge(dve_done, at("f_lo", g, k))
                            i = split_mm(banks[0][:, :], (w[0][:, P * k:P * k + P], w[1][:, P * k:P * k + P]),
                                         (f_hi[:, k, :], f_lo[:, k, :]), k == 0, k == KG - 1)
                        i.then_inc(pe_done, pe_n("mm", ORD[c]))
                        j = next(mod, None)
                        if j is None:
                            columns()
                        else:
                            modulation(1, j)

            pe.wait_ge(rout_in, 32)
            pe.wait_ge(pool_done, at("routing"))
            for t in range(2):
                for k in range(KD):
                    pe.wait_ge(act_done, at("h", k))
                    mm(MOD[:, LOGIT + NE * t:LOGIT + NE * t + NE], hT[:, k, P * t:P * t + P], rw[:, k, :], k == 0, False)
                i = mm(MOD[:, LOGIT + NE * t:LOGIT + NE * t + NE], one[:, :], rb[:, :], False, True)
            i.then_inc(pe_done, pe_n("logits"))
            pe.wait_ge(*evacuated(("w_out", 1, NWOUT - 1)))
            for t in range(2):
                for k in range(KD):
                    i = nc.tensor.transpose(bank[2 * t + k // 4][:, P * (k % 4):P * (k % 4) + P],
                                            hT[:, k, P * t:P * t + P], ident[:, :])
                i.then_inc(pe_done, pe_n("ht", t))
            pe.wait_ge(dve_done, at("mask"))
            mm(MOD[:, RANK:RANK + NE], before[:, :], mask[:, 0, :], True, True)
            mm(MOD[:, RANK + NE:RANK + 2 * NE], all1[:, :], mask[:, 0, :], True, False)
            mm(MOD[:, RANK + NE:RANK + 2 * NE], before[:, :], mask[:, 1, :], False, True)
            for t in range(2):
                i = mm(MOD[:, RANK + 2 * NE:RANK + 3 * NE], all1[:, :], mask[:, t, :], t == 0, t == 1)
            i.then_inc(pe_done, pe_n("rank"))

            Kd, Ka = at("per_expert", "dve"), at("per_expert", "act")

            def gather(name):
                for part, (src, b) in enumerate(((ht_hi, 6), (ht_lo, 0))):
                    for k in range(KD):
                        for t in range(2):
                            i = mm(bank[b + k // 4][:, P * (k % 4):P * (k % 4) + P],
                                   src[:, t, P * k:P * k + P], sel[:, t, :], t == 0, t == 1)
                    i.then_inc(pe_done, pe_n(name, part))

            def expert(turn_no):
                de, ae = turn_no * Kd, turn_no * Ka

                def turn(fc):
                    pe.wait_ge(dve_done, at("e_hid", fc) + de)
                    if fc >= 2:
                        pe.wait_ge(dve_done, at("e_hd", fc - 2) + de)
                    else:
                        pe.wait_ge(act_done, at("e_selT") + ae)
                        pe.wait_ge(dve_done, at("e_slot_w") + de)
                    for t in range(2):
                        o = 256 * fc + P * t
                        j = nc.tensor.transpose(bank[2 + fc % 2][:, P * t:P * t + P], hid[:, o:o + P], ident[:, :])
                    j.then_inc(pe_done, pe_n("e_turn", fc))

                pe.wait_ge(act_done, at("next_hc") - Ka + ae)
                pe.wait_ge(dve_done, at("next_hc_lo") - Kd + de)
                for j in range(UP):
                    fc, s = j // 2, j % SPL
                    pe.wait_ge(dve_done, at("next_lo", j) - Kd + de if j < SPL else at("e_lo", j) + de)
                    if j % 2 == 0 and fc >= 2:
                        pe.wait_ge(dve_done, at("e_hid", fc - 2) + de)
                    for kk in range(4):
                        k, cols = 4 * (j % 2) + kk, slice(512 * kk, 512 * kk + 512)
                        i = split_mm(bank[fc % 2][:, :], (hc_hi[:, k, :], hc_lo[:, k, :]),
                                     (w_hi[:, s, cols], w_lo[:, s, cols]), k == 0, k == KD - 1)
                    i.then_inc(pe_done, pe_n("e_mm", j))
                    if j == 1:
                        pe.wait_ge(dve_done, at("e_add", KD - 1) - Kd + de)
                        for t in range(2):
                            mm(bank[3][:, 256:257], sel[:, t, :].bitcast(F32), cw1[:, t, :], t == 0, t == 1)
                        for t in range(2):
                            i = nc.tensor.transpose(bank[2][:, P * t:P * t + P], sel[:, t, :].bitcast(F32), ident[:, :])
                        i.then_inc(pe_done, pe_n("e_turned"))
                    elif j % 2:
                        turn(fc - 1)
                for j in range(UP, PER_EXPERT):
                    s = j % SPL
                    pe.wait_ge(dve_done, at("e_lo", j) + de)
                    pe.wait_ge(dve_done, at("e_hd", j - UP) + de)
                    for kk in range(2):
                        k = 2 * (j - UP) + kk
                        for half in range(2):
                            cols = slice(D * kk + 512 * half, D * kk + 512 * half + 512)
                            i = split_mm(bank[4 + half][:, :], (hd_hi[:, k, :], hd_lo[:, k, :]),
                                         (w_hi[:, s, cols], w_lo[:, s, cols]), k == 0, k == KF - 1)
                    i.then_inc(pe_done, pe_n("e_mm", j))
                    if j == UP:
                        turn(DOWN - 1)
                    if j == GATHER:
                        pe.wait_ge(dve_done, at("next_sel") + de)
                        gather("next_gather")
                for d in range(KD):
                    dst = bank[(6, 7, 2, 3)[d // 2]][:, 256 * (d % 2):256 * (d % 2) + 256]
                    if d % 4 == 0:
                        pe.wait_ge(dve_done, at("e_y", d // 4) + de)
                    if d == 0:
                        pe.wait_ge(act_done, at("next_hc") + ae)
                    mm(dst, y_hi[:, P * d:P * d + P], selT[:, :], True, False)
                    mm(dst, y_lo[:, P * d:P * d + P], selT[:, :], False, True)\
                        .then_inc(pe_done, pe_n("e_back", d))

            pe.wait_ge(dve_done, at("first_sel"))
            gather("first_gather")
            pe.wait_ge(act_done, at("first_hc"))
            pe.wait_ge(dve_done, at("first_hc_lo"))
            n0 = pe_n.n
            with pe.Fori(0, NE, 1) as e:
                expert(e)
            marks[("per_expert", "pe")] = pe_n.n - n0
            pe_n.n, pe_n.again = n0, True
            pe.wait_ge(dve_done, at("again"))
            with pe.Fori(0, MORE, 1) as r:
                left = pe.value_load(again_i[0:1, 0, bass.ds(r, 1)], min_val=0, max_val=NE)
                with pe.If(left > 0):
                    expert(r + NE)
                pe.nop()
            for d in range(KD):
                pe.wait_ge(fin_dve, at("fin_sq", d))
                i = mm(STAT[:, 0:NX], ones_d[:, :], fq[:, d, :], d == 0, d == KD - 1)
            i.then_inc(fin_pe, fpe_n("fin_ms"))
            for t in range(2):
                for d in range(KD):
                    pe.wait_ge(fin_dve, at("fin_y", d))
                    i = nc.tensor.transpose(bank[2 * t + d // 4][:, P * (d % 4):P * (d % 4) + P],
                                            fy[:, d, P * t:P * t + P], ident[:, :])
                i.then_inc(fin_pe, fpe_n("fin_turn", t))

        @block.scalar
        def _(act):
            def hi(s):
                if s >= len(SPLIT):
                    return
                c = SPLIT[s]
                n = width(c)
                act.wait_ge(raw_in[POS[c] % RAW], arrived[c])
                if s >= SPL:
                    act.wait_ge(pe_done, at("mm", s - SPL))
                nc.scalar.activation(w_hi[:, s % SPL, 0:n], raw[:, POS[c] % RAW, 0:n], ACT.Copy)\
                    .then_inc(act_done, act_n("hi", s))

            def squares(l, w, ts, ready):
                for d in range(KD):
                    act.wait_ge(dve_done, at("xT", *ready, d))
                    if d >= 2:
                        act.wait_ge(pe_done, at("ms", l, w, d - 2))
                    nc.scalar.activation(sq[:, d % 2, ts], xT[:, d, ts], ACT.Square)\
                        .then_inc(act_done, act_n("sq", l, w, d))
                act.wait_ge(pe_done, at("ms", l, w, KD - 1))
                nc.scalar.activation(rs[:, ts], STAT[:, ts], ACT.Sqrt, bias=eps[:, :])\
                    .then_inc(act_done, act_n("sd", l, w))

            def h_high(l, w, which, dst, name):
                for d in range(KD):
                    act.wait_ge(dve_done, at("t", l, w, d))
                    for s in which:
                        shift = modT[:, l, 8 * (0 if w == 1 else 3) + d, s:s + 1]
                        ap = dst[:, d, tok(s)] if name == "h_hi" else dst[:, d, :]
                        i = nc.scalar.activation(ap, tb[:, d % 2, tok(s)], ACT.Identity, bias=shift)
                        if s != which[-1]:
                            i.then_inc(act_done, act_n())
                    i.then_inc(act_done, act_n(*((name, l, w, d) if name == "h_hi" else (name, d))))

            act.wait_ge(dve_done, at("PT"))
            for s, name in enumerate(("c_ctx", "c")):
                i = nc.scalar.activation(cc[:, :, s], colv(name, 0, KD), ACT.Silu)
                i.then_inc(act_done, act_n(*(("cc",) if s else ())))
            act.wait_ge(dve_done, at("lam_abs"))
            nc.scalar.activation(lt[:, 0, :], lt[:, 0, :], ACT.Exp, scale=-1.0).then_inc(act_done, act_n("lam_exp"))

            for l in range(2):
                ts = slice(lo[l], T)
                squares(l, 1, slice(0, T), ("in",) if l == 0 else ("down", 1))
                if l == 0:
                    for s in range(SPL):
                        hi(s)
                h_high(l, 1, (0, 1), h_hi, "h_hi")
                for n, c in enumerate(WIN_ORDER):
                    s = ORD[("w_in", l, c)]
                    b = bank[2 * (s % 3):2 * (s % 3) + 2]
                    act.wait_ge(pe_done, at("mm", s))
                    hi(s + SPL)
                    for t in range(2):
                        last = ("evac", s) if t else ()
                        if c == 0:
                            i = nc.scalar.activation(tb[:, t, ts], b[t][:, ts], ACT.Copy)
                        elif c == 1:
                            i = nc.scalar.activation(sq[:, t, ts], b[t][:, ts], ACT.Tanh, scale=0.5)
                        elif c == 4:
                            i = nc.scalar.activation(sx[:, t, ts], b[t][:, ts], ACT.Copy)
                        elif c == 2:
                            i = nc.scalar.activation(y[:, 2 + t, ts], b[t][:, ts], ACT.Copy)
                        elif c in (5, 6):
                            if c == 5 and t == 0:
                                act.wait_ge(pool_done, at("padded", l))
                            i = nc.scalar.activation(cxp[:, 2 * (c - 5) + t, :, 2:2 + 256],
                                                     b[t][:, :].rearrange("p (s w) -> p s w", s=2), ACT.Copy)
                        elif c in (7, 8):
                            act.wait_ge(dve_done, at("xc", l, 3))
                            i = nc.scalar.activation(
                                cxp[:, 2 * (c - 7) + t, lo[l] // NC:2, 2:2 + 256],
                                b[t][:, ts].rearrange("p (s w) -> p s w", w=256), ACT.Gelu_apprx_tanh)
                        else:
                            continue
                        i.then_inc(act_done, act_n(*last))
                def gates(d, t):
                    q = 4 * d + t
                    act.wait_ge(pe_done, at("gate", l, q))
                    if d == 1:
                        act.wait_ge(dve_done, at("scan", l, 0, t))
                    else:
                        act.wait_ge(pe_done, at("mm", ORD[("w_in", l, WIN_ORDER[-1])]))
                    b = bank[2 * (q % 3):2 * (q % 3) + 2]
                    nc.scalar.activation(lr[:, t, :], b[0][:, :], ACT.Tanh, scale=0.5,
                                         bias=colv("lru_ba", 8 * l + q)).then_inc(act_done, act_n())
                    nc.scalar.activation(li[:, t, :], b[1][:, :], ACT.Tanh, scale=0.5,
                                         bias=colv("lru_bx", 8 * l + q)).then_inc(act_done, act_n("gate_read", l, q))
                    act.wait_ge(act_done, act_n.n - 1)
                    k = 8 * l + q
                    nc.scalar.activation(la[:, t, :], lr[:, t, :], ACT.Exp, scale=cln[:, k:k + 1],
                                         bias=cln[:, k:k + 1]).then_inc(act_done, act_n())
                    nc.scalar.activation(lr[:, t, :], lr[:, t, :], ACT.Tanh, scale=clp[:, k:k + 1],
                                         bias=clp[:, k:k + 1]).then_inc(act_done, act_n())
                    act.wait_ge(act_done, act_n.n - 1)
                    nc.scalar.activation(lm[:, t, :], la[:, t, :], ACT.Square).then_inc(act_done, act_n("a2", l, q))

                act.wait_ge(dve_done, at("clp"))
                for d in range(2):
                    for t in range(4):
                        gates(d, t)
                    for t in range(4):
                        act.wait_ge(dve_done, at("m", l, 4 * d + t))
                        nc.scalar.activation(lm[:, t, :], lm[:, t, :], ACT.Sqrt, scale=0.25)\
                            .then_inc(act_done, act_n("mult", l, 4 * d + t))
                    if d == 0:
                        for t in range(2):
                            act.wait_ge(dve_done, at("conf_c", l, t))
                            nc.scalar.activation(sq[:, t, ts], y[:, t, ts], ACT.Square)\
                                .then_inc(act_done, act_n("conf_sq", l, t))
                act.wait_ge(pe_done, at("conf_var", l))
                nc.scalar.activation(rs[:, ts], STAT[:, ts], ACT.Sqrt, bias=eps[:, :])\
                    .then_inc(act_done, act_n("conf_sd", l))
                for t in range(2):
                    act.wait_ge(dve_done, at("conf_n", l, t))
                    nc.scalar.activation(y[:, t, ts], y[:, t, ts], ACT.Silu, scale=colv("conf_ln_g", 2 * l + t),
                                         bias=colv("conf_ln_b", 2 * l + t)).then_inc(act_done, act_n("conf_y", l, t))

                def head_out(i8):
                    act.wait_ge(dve_done, at("y_n", l, i8))
                    nc.scalar.activation(h_hi[:, i8, ts], y[:, i8, ts], ACT.Copy, scale=colv("g_mix", 8 * l + i8))\
                        .then_inc(act_done, act_n("y_hi", l, i8))

                act.wait_ge(act_done, act_n.n)
                for i8 in range(KD):
                    act.wait_ge(dve_done, at("y", l, max(i8 - 4, 0)))
                    if i8 >= 2:
                        act.wait_ge(pe_done, at("head_ms", l, i8 - 2))
                    nc.scalar.activation(sq[:, i8 % 2, ts], y[:, i8, ts], ACT.Square)\
                        .then_inc(act_done, act_n("head_sq", l, i8))
                act.wait_ge(pe_done, at("head_ms", l, KD - 1))
                nc.scalar.activation(rs[0:HEADS, ts], STAT[0:HEADS, ts], ACT.Sqrt, bias=eps[0:HEADS, :])\
                    .then_inc(act_done, act_n("head_sd", l))
                for i8 in range(KD):
                    head_out(i8)
                for c in range(NWOUT):
                    s = ORD[("w_out", l, c)]
                    act.wait_ge(pe_done, at("mm", s))
                    hi(s + SPL)
                squares(l, 2, ts, ("w_out", l))
                if l == 1:
                    break
                h_high(l, 2, (0, 1), h_hi, "h_hi")
                for g in range(2):
                    for i11 in range(KG):
                        s = ORD[("up", g, i11)]
                        act.wait_ge(pe_done, at("mm", s))
                        if i11 >= 2:
                            act.wait_ge(dve_done, at("hid", g, i11 - 2))
                        nc.scalar.activation(tb[:, i11 % 2, :], bank[2 * (s % 3)][:, :], ACT.Silu)\
                            .then_inc(act_done, act_n("silu", g, i11))
                        act.wait_ge(dve_done, at("hid", g, i11))
                        nc.scalar.activation(f_hi[:, i11, :], sq[:, i11 % 2, :], ACT.Copy)\
                            .then_inc(act_done, act_n("f_hi", g, i11))
                        hi(s + SPL)
                    for d in range(KD):
                        s = ORD[("down", g, d)]
                        act.wait_ge(pe_done, at("mm", s))
                        hi(s + SPL)

            h_high(1, 2, (1,), hT, "h")
            for t in range(2):
                act.wait_ge(pe_done, at("ht", t))
                for half in range(2):
                    nc.scalar.activation(ht_hi[:, t, 512 * half:512 * half + 512], bank[2 * t + half][:, :], ACT.Copy)\
                        .then_inc(act_done, act_n("ht_hi", t, half))
            act.wait_ge(dve_done, at("gap"))
            nc.scalar.activation(pr[:, :, 1], pr[:, :, 0], ACT.Exp).then_inc(act_done, act_n("gap_exp"))

            Kp, Kd, Ka = (at("per_expert", x) for x in ("pe", "dve", "act"))

            def e_hi(j, shift, level, name):
                act.wait_ge(exp_in[E_SLOT[j]], e_arrived[j] + level)
                if name != "first_hi":
                    act.wait_ge(pe_done, at("e_mm", (j - SPL) % PER_EXPERT) + shift)
                nc.scalar.activation(w_hi[:, j % SPL, :], raw[:, E_SLOT[j], :], ACT.Copy)\
                    .then_inc(act_done, act_n(name, j))

            def gathered(shift, which, name):
                act.wait_ge(pe_done, at(which, 0) + shift)
                for half in range(2):
                    nc.scalar.activation(hc_hi[:, 4 * half:4 * half + 4, :],
                                         bank[6 + half][:, :].rearrange("p (k c) -> p k c", c=CAP), ACT.Copy)\
                        .then_inc(act_done, act_n(*((name,) if half else ())))

            def expert(turn_no):
                pp, de = turn_no * Kp, turn_no * Kd
                act.wait_ge(act_done, at("table") - Ka + turn_no * Ka)
                nc.scalar.activation(warm[:, :], eps[:, :], ACT.Silu).then_inc(act_done, act_n("table"))

                def hd_high(fc):
                    act.wait_ge(pe_done, at("e_turn", fc) + pp)
                    nc.scalar.activation(hd_hi[:, 2 * fc:2 * fc + 2, :],
                                         bank[2 + fc % 2][:, 0:256].rearrange("p (k c) -> p k c", c=CAP), ACT.Copy)\
                        .then_inc(act_done, act_n("e_hd_hi", fc))

                for j in range(PER_EXPERT):
                    fc, n = j // 2, j + SPL
                    act.wait_ge(pe_done, at("e_mm", j) + pp)
                    if j == PER_EXPERT - 1:
                        act.wait_ge(dve_done, at("e_slot_w") + de)
                        for half in range(2):
                            nc.scalar.activation(y_hi[:, 512 * half:512 * half + 512], bank[4 + half][:, :], ACT.Copy,
                                                 scale=slot_w[:, :]).then_inc(act_done, act_n("e_y_hi", half))
                    if n < PER_EXPERT:
                        e_hi(n, pp, turn_no * e_level[E_SLOT[n]], "e_hi")
                    else:
                        n -= PER_EXPERT
                        e_hi(n, pp, (turn_no + 1) * e_level[E_SLOT[n]], "next_hi")
                    if j == 1:
                        act.wait_ge(pe_done, at("e_turned") + pp)
                        nc.scalar.activation(selT[:, :], bank[2][:, 0:NX], ACT.Copy)\
                            .then_inc(act_done, act_n("e_selT"))
                    if j % 2 and j < UP:
                        if fc >= 2:
                            act.wait_ge(dve_done, at("e_hid", fc - 2) + de)
                        nc.scalar.activation(gs[:, fc % 2, :], bank[fc % 2][:, 0:256], ACT.Silu)\
                            .then_inc(act_done, act_n("e_silu", fc))
                        if fc >= 1:
                            hd_high(fc - 1)
                    if j == UP:
                        hd_high(DOWN - 1)
                    if j == GATHER + 1:
                        gathered(pp, "next_gather", "next_hc")

            for j in range(SPL):
                e_hi(j, 0, 0, "first_hi")
            gathered(0, "first_gather", "first_hc")
            n0 = act_n.n
            with act.Fori(0, NE, 1) as e:
                expert(e)
            marks[("per_expert", "act")] = act_n.n - n0
            act_n.n, act_n.again = n0, True
            act.wait_ge(dve_done, at("again"))
            with act.Fori(0, MORE, 1) as r:
                left = act.value_load(again_i[0:1, 0, bass.ds(r, 1)], min_val=0, max_val=NE)
                with act.If(left > 0):
                    expert(r + NE)
                act.nop()
            act.wait_ge(fin_pe, at("fin_ms"))
            nc.scalar.activation(rs[:, 0:NX], STAT[:, 0:NX], ACT.Sqrt, bias=eps[:, :])\
                .then_inc(fin_act, fact_n("fin_sd"))
            for t in range(2):
                act.wait_ge(fin_pe, at("fin_turn", t))
                nc.scalar.activation(fo[:, t, 0:512], bank[2 * t][:, :], ACT.Copy)\
                    .then_inc(fin_act, fact_n("fin_o", t))

        @block.vector
        def _(dve):
            V = nc.vector

            def own(back=0):
                dve.wait_ge(dve_done, dve_n.n - back)

            def low(s):
                if s >= len(SPLIT):
                    return
                n = width(SPLIT[s])
                dve.wait_ge(act_done, at("hi", s))
                V.tensor_tensor(w_lo[:, s % SPL, 0:n], raw[:, POS[SPLIT[s]] % RAW, 0:n],
                                w_hi[:, s % SPL, 0:n].bitcast(F32), ALU.subtract).then_inc(dve_done, dve_n("lo", s))

            def inverse_rms(l, w):
                ts = slice(lo[l] if w == 2 else 0, T)
                dve.wait_ge(act_done, at("sd", l, w))
                V.reciprocal(rs[:, ts], rs[:, ts]).then_inc(dve_done, dve_n())

            def normed(l, w, which, low_part):
                def t_of(d):
                    if d >= 2:
                        dve.wait_ge(act_done, at("h_hi", l, w, d - 2) if low_part else at("h", d - 2))
                        if low_part:
                            dve.wait_ge(dve_done, at("h_lo", l, w, d - 2))
                    for s in which:
                        i = V.scalar_tensor_tensor(tb[:, d % 2, tok(s)], xT[:, d, tok(s)], amp[:, l, w - 1, d, s:s + 1],
                                                   rs[:, tok(s)], ALU.mult, ALU.mult)
                        i.then_inc(dve_done, dve_n(*(("t", l, w, d) if s == which[-1] else ())))

                def lo_of(d):
                    dve.wait_ge(act_done, at("h_hi", l, w, d))
                    for s in which:
                        shift = modT[:, l, 8 * (0 if w == 1 else 3) + d, s:s + 1]
                        i = V.scalar_tensor_tensor(h_lo[:, d, tok(s)], tb[:, d % 2, tok(s)], shift,
                                                   h_hi[:, d, tok(s)].bitcast(F32), ALU.add, ALU.subtract)
                        i.then_inc(dve_done, dve_n(*(("h_lo", l, w, d) if s == which[-1] else ())))
                own()
                t_of(0)
                for d in range(KD):
                    if d + 1 < KD:
                        t_of(d + 1)
                    if low_part:
                        lo_of(d)
                    if (l, w) == (0, 1) and d in (0, 2):
                        low(1 + d // 2)
                    if (l, w) == (0, 1) and 1 <= d <= FIRST - NORM1:
                        mod_row(0, NORM1 + d - 1)

            def mod_row(l, j):
                dve.wait_ge(pe_done, at("used", "mod", l, j))
                V.tensor_copy(mrow[:, j % 2, :], mod_rows(l, j)).then_inc(dve_done, dve_n("mod_row", l, j))

            def modulated(l, j0, j1):
                dve.wait_ge(pe_done, at("mod_col", l, j1 // 2 - 1))
                for s in range(2):
                    V.tensor_tensor(modT[:, l, j0:j1, s], MOD[:, 96 * l + s + 2 * j0:96 * l + 2 * j1:2],
                                    colv("b_mod", 48 * l + j0, j1 - j0), ALU.add).then_inc(dve_done, dve_n())

            def amplitude(l, w):
                j = 8 * (1 if w == 1 else 4)
                own()
                for s in range(2):
                    V.scalar_tensor_tensor(amp[:, l, w - 1, :, s], modT[:, l, j:j + 8, s], 1.0,
                                           colv(f"g_norm{w}", 8 * l, 8), ALU.add, ALU.mult)\
                        .then_inc(dve_done, dve_n())

            dve.wait_ge(pe_done, at("tables"))
            for n, (_, rows) in enumerate(TABLES):
                i = V.tensor_copy(PT[:, P * n:P * n + rows], STAT[:, P * n:P * n + rows])
                i.then_inc(dve_done, dve_n(*(("PT",) if n == 3 else ())))
            own()
            lam = colv("lru_lam", 0, 16)
            V.tensor_scalar(lt[:, 1, :], lam, -1.0, None, ALU.mult).then_inc(dve_done, dve_n())
            own()
            V.tensor_tensor(lt[:, 0, :], lam, lt[:, 1, :], ALU.max).then_inc(dve_done, dve_n("lam_abs"))
            for name, n in (("conf_w", 124), ("lru_ba", 16), ("lru_bx", 16)):
                V.tensor_scalar(colv(name, 0, n), colv(name, 0, n), 0.5, None, ALU.mult).then_inc(dve_done, dve_n())
            for d in range(KD):
                dve.wait_ge(pe_done, at("xt", d))
                V.tensor_copy(xT[:, d, :], bank[d % 6][:, :]).then_inc(dve_done, dve_n("xT", "in", d))
            dve.wait_ge(act_done, at("lam_exp"))
            V.tensor_scalar(lt[:, 2, :], lt[:, 0, :], 2.0, None, ALU.add).then_inc(dve_done, dve_n())
            own()
            V.reciprocal(lt[:, 2, :], lt[:, 2, :]).then_inc(dve_done, dve_n())
            own()
            V.tensor_tensor(lt[:, 0, :], lt[:, 0, :], lt[:, 2, :], ALU.mult).then_inc(dve_done, dve_n())
            own()
            V.tensor_tensor(lt[:, 2, :], lt[:, 0, :], lt[:, 0, :], ALU.mult).then_inc(dve_done, dve_n())
            own()
            V.tensor_scalar(lt[:, 3, :], lt[:, 2, :], 1.0 / 15, 1.0 / 13, ALU.mult, ALU.add).then_inc(dve_done, dve_n())
            for k in (11, 9, 7, 5, 3, 1):
                own()
                V.tensor_tensor(lt[:, 3, :], lt[:, 3, :], lt[:, 2, :], ALU.mult).then_inc(dve_done, dve_n())
                own()
                V.tensor_scalar(lt[:, 3, :], lt[:, 3, :], 1.0 / k, None, ALU.add).then_inc(dve_done, dve_n())
            own()
            V.scalar_tensor_tensor(lt[:, 3, :], lt[:, 3, :], 2.0, lt[:, 0, :], ALU.mult, ALU.mult)\
                .then_inc(dve_done, dve_n())
            own()
            V.scalar_tensor_tensor(lt[:, 3, :], lt[:, 1, :], 0.0, lt[:, 3, :], ALU.max, ALU.add)\
                .then_inc(dve_done, dve_n())
            own()
            V.tensor_scalar(clp[:, :], lt[:, 3, :], 4.0, None, ALU.mult).then_inc(dve_done, dve_n())
            V.tensor_scalar(cln[:, :], lt[:, 3, :], -4.0, None, ALU.mult).then_inc(dve_done, dve_n("clp"))
            inverse_rms(0, 1)
            for j in range(NORM1):
                if j == NORM1 - 1:
                    low(0)
                mod_row(0, j)
            modulated(0, 0, 16)
            amplitude(0, 1)

            for l in range(2):
                ts = slice(lo[l], T)
                st = streams[l]
                if l == 1:
                    inverse_rms(1, 1)
                    modulated(1, 0, 16)
                    amplitude(1, 1)
                normed(l, 1, (0, 1), True)

                def conf_taps(n):
                    for k in [next(taps, None) for _ in range(n)]:
                        if k is None:
                            return
                        for t in range(2):
                            w = colv("conf_w", 62 * l + 2 * k + t)
                            for s in st:
                                out_v, in_v = grid(y[:, t, tok(s)], s), padded_v(t, s, k)
                                own(2 * len(st) - 1)
                                if k == 0:
                                    i = V.tensor_scalar(out_v, in_v, w, colv("conf_b", 2 * l + t), ALU.mult, ALU.add)
                                else:
                                    i = V.scalar_tensor_tensor(out_v, in_v, w, out_v, ALU.mult, ALU.add)
                                i.then_inc(dve_done, dve_n(*(("conf_u", l) if (k, t, s) == (CONF_K - 1, 1, 1) else ())))

                taps = iter(range(CONF_K))
                for n, c in enumerate(WIN_ORDER):
                    s0 = ORD[("w_in", l, c)]
                    b = bank[2 * (s0 % 3):2 * (s0 % 3) + 2]
                    dve.wait_ge(pe_done, at("mm", s0))
                    low(s0 + SPL)
                    if c in (7, 8):
                        for v in range(2):
                            conf_taps(2)
                            for j in MOD_AT[l].get(-1, [])[2 * (c - 7) + v:][:1]:
                                mod_row(l, j)
                    if c == 1:
                        dve.wait_ge(pool_done, at("padded", l))
                        dve.wait_ge(act_done, at("evac", s0))
                        for t in range(2):
                            for s in st:
                                V.scalar_tensor_tensor(padded_v(t, s, CONF_PAD) if s else vp[:, t, CONF_PAD:CONF_PAD + NC],
                                                       grid(sq[:, t, tok(s)], s), 1.0, grid(tb[:, t, tok(s)], s),
                                                       ALU.add, ALU.mult).then_inc(dve_done, dve_n())
                        own()
                        conf_taps(4 - 2 * l)
                    elif c == 4:
                        conf_taps(5 - 2 * l)
                    elif c == 3:
                        dve.wait_ge(act_done, at("evac", ORD[("w_in", l, 4)]))
                        for t in range(2):
                            for s in st:
                                V.tensor_tensor(padded_s(t, s, 1), b[t][:, tok(s)], sx[:, t, tok(s)], ALU.mult)\
                                    .then_inc(dve_done, dve_n(*(("evac", s0) if (t, s) == (1, 1) else ())))
                        conf_taps(3 - l)
                    elif c == 2:
                        conf_taps(5 - 3 * l)
                    elif c == 5:
                        for k in range(SCONV_K):
                            for t in range(2):
                                w = colv("sconv_w", 6 * l + 2 * k + t)
                                for s in st:
                                    own(2 * len(st) - 1)
                                    if k == 0:
                                        i = V.tensor_scalar(sx[:, t, tok(s)], padded_s(t, s, k), w, None, ALU.mult)
                                    else:
                                        i = V.scalar_tensor_tensor(sx[:, t, tok(s)], padded_s(t, s, k), w,
                                                                   sx[:, t, tok(s)], ALU.mult, ALU.add)
                                    i.then_inc(dve_done, dve_n())
                        own()
                        dve.wait_ge(act_done, at("evac", ORD[("w_in", l, 2)]))
                        V.tensor_tensor(y[:, 2:4, ts], y[:, 2:4, ts], sx[:, :, ts], ALU.mult)\
                            .then_inc(dve_done, dve_n("sx_read", l))
                    elif c == 6:
                        dve.wait_ge(act_done, at("evac", s0))
                        for k in range(LRU_K):
                            for t in range(4):
                                w = colv("lru_conv_w", 16 * l + 4 * k + t)
                                out_v = xc[:, t, :].rearrange("p (s w) -> p s w", s=2)
                                own(3)
                                if k == 0:
                                    i = V.tensor_scalar(out_v, cxp[:, t, :, k:k + 256], w,
                                                        colv("lru_conv_b", 4 * l + t), ALU.mult, ALU.add)
                                else:
                                    i = V.scalar_tensor_tensor(out_v, cxp[:, t, :, k:k + 256], w, out_v,
                                                               ALU.mult, ALU.add)
                                i.then_inc(dve_done, dve_n(*(("xc", l, t) if k == LRU_K - 1 else ())))
                for d in range(2):
                    for t in range(4):
                        q = 4 * d + t
                        dve.wait_ge(act_done, at("a2", l, q))
                        V.scalar_tensor_tensor(lm[:, t, :], lm[:, t, :], 1.0, lr[:, t, :], ALU.add, ALU.mult)\
                            .then_inc(dve_done, dve_n())
                        V.scalar_tensor_tensor(li[:, t, :], li[:, t, :], 1.0, xc[:, t, :], ALU.add, ALU.mult)\
                            .then_inc(dve_done, dve_n())
                        own(1)
                        V.tensor_scalar(lm[:, t, :], lm[:, t, :], 0.0, None, ALU.max)\
                            .then_inc(dve_done, dve_n("m", l, q))
                        if d == 0 and t < 3:
                            conf_taps(2 + 2 * l if t < 2 else CONF_K)
                        for j in MOD_AT[l].get(q, []):
                            mod_row(l, j)
                    if d == 0:
                        dve.wait_ge(pe_done, at("conf_mean", l))
                        for t in range(2):
                            V.tensor_tensor(y[:, t, ts], y[:, t, ts], STAT[:, ts], ALU.subtract)\
                                .then_inc(dve_done, dve_n("conf_c", l, t))
                    for t in range(4):
                        if (d, t) == (1, 2):
                            dve.wait_ge(act_done, at("conf_sd", l))
                            V.reciprocal(rs[:, ts], rs[:, ts]).then_inc(dve_done, dve_n())
                            own()
                            for v in range(2):
                                V.tensor_tensor(y[:, v, ts], y[:, v, ts], rs[:, ts], ALU.mult)\
                                    .then_inc(dve_done, dve_n("conf_n", l, v))
                        dve.wait_ge(act_done, at("mult", l, 4 * d + t))
                        V.tensor_tensor(li[:, t, :], lm[:, t, :], li[:, t, :], ALU.mult).then_inc(dve_done, dve_n())
                        own()
                        if d == 0:
                            V.tensor_tensor_scan(y[:, 4 + t, :], la[:, t, :], li[:, t, :], 0.0, ALU.mult, ALU.add)\
                                .then_inc(dve_done, dve_n("scan", l, 0, t))
                            continue
                        for s in range(2):
                            V.tensor_tensor_scan(lr[:, t, tok(s)][:, ::-1], la[:, t, tok(s)][:, ::-1],
                                                 li[:, t, tok(s)][:, ::-1], lr[:, t, 0:1] if s else 0.0,
                                                 ALU.mult, ALU.add).then_inc(dve_done, dve_n())
                            own()
                        V.tensor_tensor(y[:, 4 + t, ts], y[:, 4 + t, ts], lr[:, t, ts], ALU.add)\
                            .then_inc(dve_done, dve_n())
                        own()
                        g_v = cxp[:, t, lo[l] // NC:2, 2:2 + 256]
                        y_v = y[:, 4 + t, ts].rearrange("p (s w) -> p s w", w=256)
                        if t == 0:
                            dve.wait_ge(act_done, at("evac", ORD[("w_in", l, 8)]))
                        V.tensor_tensor(y_v, y_v, g_v, ALU.mult)\
                            .then_inc(dve_done, dve_n("y", l, t))
                        for j in MOD_AT[l].get(8, [])[t:][:1]:
                            mod_row(l, j)
                modulated(l, 16, 48)
                amplitude(l, 2)
                dve.wait_ge(act_done, at("head_sd", l))
                V.reciprocal(rs[0:HEADS, ts], rs[0:HEADS, ts]).then_inc(dve_done, dve_n("head_r", l))
                for i8 in range(KD):
                    dve.wait_ge(pe_done, at("head_f", l, i8))
                    V.tensor_tensor(y[:, i8, ts], y[:, i8, ts], bank[2 + i8 % 4][:, ts], ALU.mult)\
                        .then_inc(dve_done, dve_n("y_n", l, i8))
                    if i8 >= 1:
                        y_low(i8 - 1, l, ts, dve, V)
                y_low(KD - 1, l, ts, dve, V)
                for c in range(NWOUT):
                    s0 = ORD[("w_out", l, c)]
                    dve.wait_ge(pe_done, at("mm", s0))
                    for t in range(2):
                        d = 2 * c + t
                        for s in st:
                            i = V.scalar_tensor_tensor(xT[:, d, tok(s)], bank[2 * (s0 % 3) + t][:, tok(s)],
                                                       modT[:, l, 16 + d, s:s + 1], xT[:, d, tok(s)],
                                                       ALU.mult, ALU.add)
                            i.then_inc(dve_done, dve_n(*(("xT", "w_out", l, d) if s == 1 else ())))
                    low(s0 + SPL)
                own()
                if l == 1:
                    break
                inverse_rms(0, 2)
                normed(0, 2, (0, 1), True)
                mod = iter(range(IN_FFN))

                def next_mod_row(first):
                    for j in [] if first else [next(mod, None)]:
                        if j is not None:
                            mod_row(1, j)

                for g in range(2):
                    for i11 in range(KG):
                        s0 = ORD[("up", g, i11)]
                        next_mod_row((g, i11) == (0, 0))
                        dve.wait_ge(act_done, at("silu", g, i11))
                        if i11 >= 2:
                            dve.wait_ge(dve_done, at("f_lo", g, i11 - 2))
                        V.tensor_tensor(sq[:, i11 % 2, :], tb[:, i11 % 2, :], bank[2 * (s0 % 3) + 1][:, :], ALU.mult)\
                            .then_inc(dve_done, dve_n("hid", g, i11))
                        dve.wait_ge(act_done, at("f_hi", g, i11))
                        V.tensor_tensor(f_lo[:, i11, :], sq[:, i11 % 2, :], f_hi[:, i11, :].bitcast(F32),
                                        ALU.subtract).then_inc(dve_done, dve_n("f_lo", g, i11))
                        low(s0 + SPL)
                    for d in range(KD):
                        s0 = ORD[("down", g, d)]
                        next_mod_row(False)
                        dve.wait_ge(pe_done, at("mm", s0))
                        for s in range(2):
                            i = V.scalar_tensor_tensor(xT[:, d, tok(s)], bank[2 * (s0 % 3)][:, tok(s)],
                                                       modT[:, 0, 40 + d, s:s + 1], xT[:, d, tok(s)],
                                                       ALU.mult, ALU.add)
                            i.then_inc(dve_done, dve_n(*(("xT", "down", g, d) if s == 1 else ())))
                        low(s0 + SPL)
                own()

            inverse_rms(1, 2)
            normed(1, 2, (1,), False)
            dve.wait_ge(pe_done, at("logits"))
            V.tensor_copy(lg[:, :, :], MOD[:, LOGIT:LOGIT + 2 * NE].rearrange("p (t e) -> p t e", t=2))\
                .then_inc(dve_done, dve_n())
            own()
            for t in range(2):
                V.max(top[:, t, :], lg[:, t, :]).then_inc(dve_done, dve_n())
            own()
            for t in range(2):
                V.max_index(topi[:, t, :], top[:, t, :], lg[:, t, :]).then_inc(dve_done, dve_n())
            V.tensor_tensor(pr[:, :, 0], top[:, :, 1], top[:, :, 0], ALU.subtract).then_inc(dve_done, dve_n("gap"))
            own(1)
            V.tensor_copy(topf[:, :, :], topi[:, :, :]).then_inc(dve_done, dve_n())
            own()
            for j in range(2):
                for t in range(2):
                    V.tensor_scalar(oh[:, j, t, :], iota_e[:, :], topf[:, t, j:j + 1], None, ALU.is_equal)\
                        .then_inc(dve_done, dve_n())
            own()
            V.tensor_tensor(mask[:, :, :], oh[:, 0, :, :], oh[:, 1, :, :], ALU.add).then_inc(dve_done, dve_n("mask"))
            dve.wait_ge(act_done, at("gap_exp"))
            V.tensor_scalar(pr[:, :, 2], pr[:, :, 1], 1.0, None, ALU.add).then_inc(dve_done, dve_n())
            own()
            V.reciprocal(pr[:, :, 2], pr[:, :, 2]).then_inc(dve_done, dve_n())
            own()
            V.tensor_tensor(pr[:, :, 3], pr[:, :, 1], pr[:, :, 2], ALU.mult).then_inc(dve_done, dve_n())
            own()
            for t in range(2):
                V.tensor_scalar(comb[:, t, 0:NE], oh[:, 0, t, :], pr[:, t, 2:3], None, ALU.mult).then_inc(dve_done, dve_n())
            own()
            for t in range(2):
                V.scalar_tensor_tensor(comb[:, t, 0:NE], oh[:, 1, t, :], pr[:, t, 3:4], comb[:, t, 0:NE],
                                       ALU.mult, ALU.add).then_inc(dve_done, dve_n())
            dve.wait_ge(pe_done, at("rank"))
            V.scalar_tensor_tensor(pos[:, :, 0:NE], MOD[:, RANK:RANK + 2 * NE].rearrange("p (t e) -> p t e", t=2), 1.0,
                                   mask[:, :, :], ALU.add, ALU.mult).then_inc(dve_done, dve_n())
            own()
            V.tensor_scalar(pos[:, :, 0:NE], pos[:, :, 0:NE], -1.0, None, ALU.add).then_inc(dve_done, dve_n())
            V.tensor_scalar(rev[:, :], iota_e[:, :], -1.0, float(NE), ALU.mult, ALU.add).then_inc(dve_done, dve_n())
            own()
            V.scalar_tensor_tensor(full[:, :], MOD[:, RANK + 2 * NE:RANK + 3 * NE], float(CAP), rev[:, :],
                                   ALU.is_gt, ALU.mult).then_inc(dve_done, dve_n())
            own()
            V.max(again[:, 0, :], full[:, :]).then_inc(dve_done, dve_n())
            own()
            V.tensor_scalar(again[:, 1, :], again[:, 0, :], -1.0, float(NE), ALU.mult, ALU.add)\
                .then_inc(dve_done, dve_n())
            own()
            V.tensor_scalar(again[:, 1, :], again[:, 1, :], float(NE - 1), None, ALU.min).then_inc(dve_done, dve_n())
            own()
            V.tensor_copy(again_i[:, :, :], again[:, :, :]).then_inc(dve_done, dve_n("again"))
            for t in range(2):
                for half in range(2):
                    cols = slice(512 * half, 512 * half + 512)
                    dve.wait_ge(act_done, at("ht_hi", t, half))
                    V.tensor_tensor(ht_lo[:, t, cols], bank[2 * t + half][:, :], ht_hi[:, t, cols].bitcast(F32),
                                    ALU.subtract).then_inc(dve_done, dve_n())

            Kp, Ka, Kd = (at("per_expert", x) for x in ("pe", "act", "dve"))

            def pick(column, name, shift):
                dve.wait_ge(dve_done, dve_n.n + shift)
                V.tensor_copy(pos1[:, :, :], pos[:, :, column]).then_inc(dve_done, dve_n())
                V.tensor_copy(cw1[:, :, :], comb[:, :, column]).then_inc(dve_done, dve_n())
                dve.wait_ge(dve_done, dve_n.n + shift)
                for t in range(2):
                    V.tensor_scalar(sel[:, t, :], iota_s[:, :], pos1[:, t, :], None, ALU.is_equal)\
                        .then_inc(dve_done, dve_n(*((name,) if t else ())))

            def e_low(j, shift, high, name):
                dve.wait_ge(act_done, at(high, j) + shift)
                V.tensor_tensor(w_lo[:, j % SPL, :], raw[:, E_SLOT[j], :], w_hi[:, j % SPL, :].bitcast(F32),
                                ALU.subtract).then_inc(dve_done, dve_n(name, j))

            def gathered(shift, which, name):
                dve.wait_ge(pe_done, at(which, 1) + shift)
                for half in range(2):
                    V.tensor_copy(hc_lo[:, 4 * half:4 * half + 4, :],
                                  bank[half][:, :].rearrange("p (k c) -> p k c", c=CAP))\
                        .then_inc(dve_done, dve_n(*((name,) if half else ())))

            def expert(turn_no):
                pp, ae, de = turn_no * Kp, turn_no * Ka, turn_no * Kd

                def hd_low(fc):
                    dve.wait_ge(act_done, at("e_hd_hi", fc) + ae)
                    V.tensor_tensor(hd_lo[:, 2 * fc:2 * fc + 2, :],
                                    bank[2 + fc % 2][:, 0:256].rearrange("p (k c) -> p k c", c=CAP),
                                    hd_hi[:, 2 * fc:2 * fc + 2, :].bitcast(F32), ALU.subtract)\
                        .then_inc(dve_done, dve_n("e_hd", fc))

                for j in range(PER_EXPERT):
                    fc, n = j // 2, j + SPL
                    dve.wait_ge(pe_done, at("e_mm", j) + pp)
                    if j == PER_EXPERT - 1:
                        for half in range(2):
                            cols = slice(512 * half, 512 * half + 512)
                            dve.wait_ge(act_done, at("e_y_hi", half) + ae)
                            V.scalar_tensor_tensor(y_lo[:, cols], bank[4 + half][:, :], slot_w[:, :],
                                                   y_hi[:, cols].bitcast(F32), ALU.mult, ALU.subtract)\
                                .then_inc(dve_done, dve_n("e_y", half))
                    if n < PER_EXPERT:
                        e_low(n, ae, "e_hi", "e_lo")
                    else:
                        e_low(n - PER_EXPERT, ae, "next_hi", "next_lo")
                    if j == 1:
                        dve.wait_ge(pe_done, at("e_turned") + pp)
                        dve.wait_ge(dve_done, at("e_end") - Kd + de)
                        V.tensor_copy(slot_w[:, :], bank[3][:, 256:257]).then_inc(dve_done, dve_n("e_slot_w"))
                    if j % 2 and j < UP:
                        dve.wait_ge(act_done, at("e_silu", fc) + ae)
                        V.tensor_tensor(hid[:, 256 * fc:256 * fc + 256], gs[:, fc % 2, :], bank[fc % 2][:, 256:512],
                                        ALU.mult).then_inc(dve_done, dve_n("e_hid", fc))
                        if fc >= 1:
                            hd_low(fc - 1)
                    if j == UP:
                        hd_low(DOWN - 1)
                        pick(bass.ds(turn_no + 1, 1), "next_sel", de)
                    if j == GATHER + 1:
                        gathered(pp, "next_gather", "next_hc_lo")
                for d in range(KD):
                    dve.wait_ge(pe_done, at("e_back", d | 1) + pp)
                    V.scalar_tensor_tensor(xT[:, d, NC:T],
                                           bank[(6, 7, 2, 3)[d // 2]][:, 256 * (d % 2):256 * (d % 2) + 256],
                                           modT[:, 1, 40 + d, 1:2], xT[:, d, NC:T], ALU.mult, ALU.add)\
                        .then_inc(dve_done, dve_n("e_add", d))
                dve.wait_ge(dve_done, dve_n.n + de)
                V.memset(slot_w[:, :], 0.0).then_inc(dve_done, dve_n("e_end"))

            pick(slice(0, 1), "first_sel", 0)
            own()
            for r in range(MORE + 1):
                e = dve.value_load(again_i[0:1, 1, r:r + 1], min_val=0, max_val=NE - 1)
                V.tensor_scalar(pos[:, :, NE + r:NE + r + 1], pos[:, :, bass.ds(e, 1)], -float(CAP), None,
                                ALU.add).then_inc(dve_done, dve_n())
                V.tensor_copy(comb[:, :, NE + r:NE + r + 1], comb[:, :, bass.ds(e, 1)]).then_inc(dve_done, dve_n())
            for j in range(SPL):
                e_low(j, 0, "first_hi", "first_lo")
            gathered(0, "first_gather", "first_hc_lo")
            n0 = dve_n.n
            with dve.Fori(0, NE, 1) as e:
                expert(e)
            K = dve_n.n - n0
            marks[("per_expert", "dve")] = K
            dve.wait_ge(dve_done, n0 + NE * K)
            dve_n.n, dve_n.again = n0, True
            with dve.Fori(0, MORE, 1) as r:
                left = dve.value_load(again_i[0:1, 0, bass.ds(r, 1)], min_val=0, max_val=NE)
                with dve.If(left > 0):
                    expert(r + NE)
                dve.nop()
            for d in range(KD):
                V.tensor_tensor(fq[:, d, :], xT[:, d, NC:T], xT[:, d, NC:T], ALU.mult)\
                    .then_inc(fin_dve, fdve_n("fin_sq", d))
            dve.wait_ge(fin_act, at("fin_sd"))
            V.reciprocal(rs[:, 0:NX], rs[:, 0:NX]).then_inc(fin_dve, fdve_n())
            dve.wait_ge(fin_dve, fdve_n.n)
            for d in range(KD):
                V.scalar_tensor_tensor(fy[:, d, :], xT[:, d, NC:T], colv("g_final", d), rs[:, 0:NX],
                                       ALU.mult, ALU.mult).then_inc(fin_dve, fdve_n("fin_y", d))
            for t in range(2):
                dve.wait_ge(fin_act, at("fin_o", t))
                V.tensor_copy(fo[:, t, 512:D], bank[2 * t + 1][:, :])\
                    .then_inc(fin_dve, fdve_n(*(("fin_out",) if t else ())))


_INS = ["x", "c", "ctx", "c_ctx", "w_mod", "b_mod", "g_norm1", "g_norm2", "w_in", "conf_w", "conf_b", "conf_ln_g",
        "conf_ln_b", "sconv_w", "lru_conv_w", "lru_conv_b", "lru_wa", "lru_ba", "lru_wx", "lru_bx", "lru_lam",
        "g_mix", "w_out", "ffn_w1", "ffn_w3", "ffn_w2", "router_w", "router_b", "moe_w1", "moe_w3", "moe_w2",
        "g_final"]


def build(nc, shapes, known):
    aps = {n: nc.dram_tensor(f"in_{n}", shape, F32, kind="ExternalInput").ap() for n, shape in shapes.items()}
    out = nc.dram_tensor("out_0", (1, NX, D), F32, kind="ExternalOutput").ap()
    marks = {}
    program(nc, aps, out, known, marks)
    return marks


def kernel(**inputs):
    import numpy as np
    import concourse.bacc as bacc
    from concourse.bass_utils import run_bass_kernel_spmd

    arrays = {f"in_{n}": np.ascontiguousarray(inputs[n]) for n in _INS}
    shapes = {n: inputs[n].shape for n in _INS}
    marks = build(bacc.Bacc("TRN2", target_bir_lowering=False, num_devices=1), shapes, None)
    nc = bacc.Bacc("TRN2", target_bir_lowering=False, num_devices=1)
    build(nc, shapes, marks)
    r = run_bass_kernel_spmd(nc, [arrays], core_ids=[0])
    return r.results[0]["out_0"]
```
